# Optimizing a Trainium2 kernel written in Bass

```python
import math
import jax, jax.numpy as jnp
from jax import lax
import numpy as np

D_MODEL = 1024
BATCH = 1
SEQ = 256
DEPTH = 2
DEC_BATCH = 8
DEC_SEQ = 1
PAST_LEN = 2048
PAGE_SIZE = 128

HEAD_DIM = 64
MIX_WIDTH = D_MODEL
X_HEADS = 4
X_WIDTH = X_HEADS * HEAD_DIM
TOK_WIDTH = MIX_WIDTH - X_WIDTH
N_MEM = 256
M_HEADS = 8
M_HEAD_DIM = TOK_WIDTH // M_HEADS
CONV_W = 4
MLSTM_CHUNK = 64
N_Q = TOK_WIDTH // HEAD_DIM
N_KV = 4
GROUP = N_Q // N_KV
KV_WIDTH = N_KV * HEAD_DIM
CMP_STRIDE = 16
CMP_LEN = 2 * CMP_STRIDE
SLC_BLOCK = 64
N_SEL = 16
WINDOW = 512
Q_BLOCK = 128
D_FF = 2816
N_EXPERTS = 8
TOP_K = 2
E_FF = 7 * D_MODEL // 4

N_A = (DEPTH + 1) // 2
N_B = DEPTH // 2
A_IN = 4 * TOK_WIDTH + 2 * M_HEADS + X_WIDTH
B_IN = TOK_WIDTH + 6 * KV_WIDTH + 3 * N_Q + X_WIDTH
RMS_EPS = 1e-6
NEG = -1e30
BIG = 1e9

kernel_name = 'hybrid_mlstm_nsa_memory_decoder_step'

def rmsnorm(x, g):
    xf = x.astype(jnp.float32)
    return xf * lax.rsqrt(jnp.mean(xf * xf, axis=-1, keepdims=True) + RMS_EPS) * g.astype(jnp.float32)

def masked_softmax(s, mask):
    s = jnp.where(mask, s, NEG)
    e = jnp.where(mask, jnp.exp(s - jnp.max(s, axis=-1, keepdims=True)), 0.0)
    return e / jnp.maximum(jnp.sum(e, axis=-1, keepdims=True), 1e-30)

def alibi_slopes():
    return jnp.exp2(-8.0 * jnp.arange(1, N_Q + 1, dtype=jnp.float32) / N_Q)

def swiglu(u, w_gu, w_d):
    g, v = jnp.split(u @ w_gu, 2, axis=-1)
    return (jax.nn.silu(g) * v) @ w_d

def moe_swiglu(u, w_router, w_gu, w_d):
    logits = (u @ w_router).astype(jnp.float32)
    top_v, top_i = lax.top_k(logits, TOP_K)
    gates = jax.nn.softmax(top_v, axis=-1)
    comb = jnp.sum(jax.nn.one_hot(top_i, N_EXPERTS, dtype=jnp.float32) * gates[..., None], axis=-2)
    out = 0.0
    for e in range(N_EXPERTS):
        out = out + comb[..., e:e + 1] * swiglu(u, w_gu[e], w_d[e])
    return out

def mem_kv(mem, g, w):
    b, n, _ = mem.shape
    kv = (rmsnorm(mem, g) @ w).reshape(b, n, 2, X_HEADS, HEAD_DIM)
    return kv[:, :, 0], kv[:, :, 1]

def mem_attention(q, mk, mv):
    b, t = q.shape[:2]
    s = jnp.einsum('bthd,bnhd->bhtn', q, mk.astype(jnp.float32)) * HEAD_DIM ** -0.5
    p = jax.nn.softmax(s, axis=-1)
    return jnp.einsum('bhtn,bnhd->bthd', p, mv.astype(jnp.float32)).reshape(b, t, X_WIDTH)

def causal_conv(hist, w):
    t = hist.shape[1] - (CONV_W - 1)
    return sum(hist[:, j:j + t] * w[j] for j in range(CONV_W))

def mlstm_chunked(q, k, v, ig, lf, C0, n0, m0):
    b, t, h, d = q.shape
    L = MLSTM_CHUNK if t % MLSTM_CHUNK == 0 else t
    nc = t // L

    def chunks(a):
        return jnp.moveaxis(a.reshape((b, nc, L) + a.shape[2:]), 1, 0)

    causal = jnp.tril(jnp.ones((L, L), dtype=bool))[None, :, :, None]

    def step(carry, inp):
        C, n, m = carry
        qc, kc, vc, ic, fc = inp
        F = jnp.cumsum(fc, axis=1)
        a = F + m[:, None, :]
        D = jnp.where(causal, F[:, :, None, :] - F[:, None, :, :] + ic[:, None, :, :], NEG)
        mt = jnp.maximum(a, jnp.max(D, axis=2))
        W = jnp.exp(D - mt[:, :, None, :])
        g = jnp.exp(a - mt)
        qk = jnp.einsum('bthd,bshd->btsh', qc, kc) * W
        num = jnp.einsum('btsh,bshd->bthd', qk, vc) + g[..., None] * jnp.einsum('bhvk,bthk->bthv', C, qc)
        den = jnp.sum(qk, axis=2) + g * jnp.einsum('bhk,bthk->bth', n, qc)
        hc = num / jnp.maximum(jnp.abs(den), jnp.exp(-mt))[..., None]
        wl, gl = W[:, -1], g[:, -1]
        C = gl[..., None, None] * C + jnp.einsum('bsh,bshv,bshk->bhvk', wl, vc, kc)
        n = gl[..., None] * n + jnp.einsum('bsh,bshk->bhk', wl, kc)
        return (C, n, mt[:, -1]), hc

    (C, n, m), hs = lax.scan(step, (C0, n0, m0), (chunks(q), chunks(k), chunks(v), chunks(ig), chunks(lf)))
    return jnp.moveaxis(hs, 0, 1).reshape(b, t, h, d), C, n, m

def mlstm_mixer(z, conv_hist, C0, n0, m0, conv_w, b_gate, head_g):
    b, t, _ = z.shape
    qk_pre, v, o_pre, g_pre, xq = jnp.split(
        z, [2 * TOK_WIDTH, 3 * TOK_WIDTH, 4 * TOK_WIDTH, 4 * TOK_WIDTH + 2 * M_HEADS], axis=-1)
    hist = jnp.concatenate([conv_hist.astype(jnp.float32), qk_pre], axis=1)
    q, k = jnp.split(jax.nn.silu(causal_conv(hist, conv_w.astype(jnp.float32))), 2, axis=-1)
    shp = (b, t, M_HEADS, M_HEAD_DIM)
    ig, fg = jnp.split(g_pre + b_gate, 2, axis=-1)
    h, C, n, m = mlstm_chunked(q.reshape(shp), k.reshape(shp) * M_HEAD_DIM ** -0.5, v.reshape(shp),
                               ig, jax.nn.log_sigmoid(fg), C0.astype(jnp.float32),
                               n0.astype(jnp.float32), m0.astype(jnp.float32))
    h = jax.nn.sigmoid(o_pre).reshape(shp) * h
    h = h * lax.rsqrt(jnp.mean(h * h, axis=-1, keepdims=True) + RMS_EPS) * head_g.reshape(M_HEADS, M_HEAD_DIM)
    new_state = (C, n, m, hist[:, t:])
    return h.reshape(b, t, TOK_WIDTH), xq.reshape(b, t, X_HEADS, HEAD_DIM), new_state

def nsa_split(z, b_gate):
    b, t, _ = z.shape
    q, kv, g, xq = jnp.split(z, [TOK_WIDTH, TOK_WIDTH + 6 * KV_WIDTH, TOK_WIDTH + 6 * KV_WIDTH + 3 * N_Q], axis=-1)
    return (q.reshape(b, t, N_Q, HEAD_DIM), kv.reshape(b, t, 6, N_KV, HEAD_DIM),
            jax.nn.sigmoid(g + b_gate).reshape(b, t, 3, N_Q), xq.reshape(b, t, X_HEADS, HEAD_DIM))

def nsa_merge(gates, o):
    b, t = gates.shape[:2]
    return jnp.einsum('btcn,btcnd->btnd', gates, o).reshape(b, t, TOK_WIDTH)

def compress_rows(a, pe, w1, w2):
    n = a.shape[0] // CMP_STRIDE
    seg = a.reshape(n, CMP_STRIDE, N_KV, HEAD_DIM)
    nxt = jnp.concatenate([seg[1:], jnp.zeros_like(seg[:1])], axis=0)
    blk = jnp.concatenate([seg, nxt], axis=1) + pe[None, :, None, :]
    flat = blk.transpose(0, 2, 1, 3).reshape(n, N_KV, CMP_LEN * HEAD_DIM)
    return jax.nn.gelu(flat @ w1) @ w2

def nsa_sequence(q, q_start, rows, win, w_c1, w_c2, pe, slopes):
    tk, tq = rows.shape[0], q.shape[0]
    k_cmp = compress_rows(rows[:, 0], pe[0], w_c1[0], w_c2[0])
    v_cmp = compress_rows(rows[:, 1], pe[1], w_c1[1], w_c2[1])
    n_cmp, n_slc = tk // CMP_STRIDE, tk // SLC_BLOCK
    n_top = min(N_SEL, n_slc)
    cmp_start = jnp.arange(n_cmp) * CMP_STRIDE
    cmp_end = cmp_start + CMP_LEN - 1
    slc_start = jnp.arange(n_slc) * SLC_BLOCK
    overlap = ((cmp_start[:, None] < slc_start[None, :] + SLC_BLOCK)
               & (cmp_end[:, None] >= slc_start[None, :])).astype(jnp.float32)
    k_blk = rows[:, 2].reshape(n_slc, SLC_BLOCK, N_KV, HEAD_DIM).transpose(2, 0, 1, 3)
    v_blk = rows[:, 3].reshape(n_slc, SLC_BLOCK, N_KV, HEAD_DIM).transpose(2, 0, 1, 3)
    sl = slopes.reshape(N_KV, GROUP)[None, :, :, None]
    scale = HEAD_DIM ** -0.5
    qb = Q_BLOCK if tq % Q_BLOCK == 0 else tq
    n_qb = tq // qb
    qg = q.reshape(n_qb, qb, N_KV, GROUP, HEAD_DIM)
    kv_idx = jnp.arange(N_KV)[None, :, None]
    blk_id = jnp.arange(n_slc)[None, :]

    def block(args):
        j, qj = args
        t = q_start + j * qb + jnp.arange(qb)
        tb = t[:, None, None, None]
        s_c = jnp.einsum('tgrd,ngd->tgrn', qj, k_cmp) * scale - sl * (tb - cmp_end)
        p_c = masked_softmax(s_c, (cmp_end[None, :] <= t[:, None])[:, None, None, :])
        o_c = jnp.einsum('tgrn,ngd->tgrd', p_c, v_cmp)
        imp = jnp.einsum('tgrn,nj->tgj', p_c, overlap)
        cur = (t // SLC_BLOCK)[:, None]
        forced = (blk_id == 0) | (blk_id == cur) | (blk_id == cur - 1)
        future = slc_start[None, :] > t[:, None]
        imp = jnp.where(forced[:, None], BIG, jnp.where(future[:, None], -BIG, imp))
        _, idx = lax.top_k(imp, n_top)
        k_sel = k_blk[kv_idx, idx].reshape(qb, N_KV, n_top * SLC_BLOCK, HEAD_DIM)
        v_sel = v_blk[kv_idx, idx].reshape(qb, N_KV, n_top * SLC_BLOCK, HEAD_DIM)
        pos = (idx[..., None] * SLC_BLOCK + jnp.arange(SLC_BLOCK)).reshape(qb, N_KV, 1, n_top * SLC_BLOCK)
        s_s = jnp.einsum('tgrd,tgmd->tgrm', qj, k_sel) * scale - sl * (tb - pos)
        p_s = masked_softmax(s_s, pos <= tb)
        o_s = jnp.einsum('tgrm,tgmd->tgrd', p_s, v_sel)
        w_rows = lax.dynamic_slice_in_dim(win, j * qb, WINDOW + qb, axis=0)
        wpos = q_start - WINDOW + j * qb + jnp.arange(WINDOW + qb)
        dist = t[:, None] - wpos[None, :]
        s_w = jnp.einsum('tgrd,wgd->tgrw', qj, w_rows[:, 0]) * scale - sl * dist[:, None, None, :]
        mask_w = (dist >= 0) & (dist <= WINDOW) & (wpos >= 0)[None, :]
        p_w = masked_softmax(s_w, mask_w[:, None, None, :])
        o_w = jnp.einsum('tgrw,wgd->tgrd', p_w, w_rows[:, 1])
        return jnp.stack([o_c, o_s, o_w], axis=1)

    out = lax.map(block, (jnp.arange(n_qb), qg))
    return out.reshape(tq, 3, N_Q, HEAD_DIM)

def nsa_prompt(q, kv, w_c1, w_c2, pe, slopes):
    def one(args):
        qs, kvs = args
        win = jnp.concatenate([jnp.zeros((WINDOW, 2, N_KV, HEAD_DIM), kvs.dtype), kvs[:, 4:]], axis=0)
        return nsa_sequence(qs, 0, kvs[:, :4], win, w_c1, w_c2, pe, slopes)
    return lax.map(one, (q, kv))

def nsa_sample(q, kv, pool, layer, page_table, win_buf, past_len, w_c1, w_c2, pe, slopes):
    tq = q.shape[1]
    total = past_len + tq
    tk = -(-total // SLC_BLOCK) * SLC_BLOCK
    wbuf = win_buf.shape[1]

    def one(args):
        qs, kvs, pages, buf = args
        past = pool[layer, pages].reshape(past_len, 4, N_KV, HEAD_DIM).astype(jnp.float32)
        rows = jnp.concatenate([past, kvs[:, :4], jnp.zeros((tk - total, 4, N_KV, HEAD_DIM), jnp.float32)], axis=0)
        win = jnp.concatenate([jnp.zeros((WINDOW - wbuf, 2, N_KV, HEAD_DIM), jnp.float32),
                               buf.astype(jnp.float32), kvs[:, 4:]], axis=0)
        return nsa_sequence(qs, past_len, rows, win, w_c1, w_c2, pe, slopes)
    return lax.map(one, (q, kv, page_table, win_buf))

def setup_inputs(seed: int = 0) -> dict:
    key = jax.random.key(seed)
    keys = iter(jax.random.split(key, 48))

    def nrm(shape, scale):
        return scale * jax.random.normal(next(keys), shape, jnp.float32)

    def gain(shape):
        return 1.0 + nrm(shape, 0.02)

    n_pages = PAST_LEN // PAGE_SIZE
    n_used = DEC_BATCH * n_pages
    n_pool = n_used + n_used // 4
    wbuf = min(WINDOW, PAST_LEN)
    inp = {}
    inp['x_prompt'] = nrm((BATCH, SEQ, D_MODEL), 1.0)
    inp['x_sample'] = nrm((DEC_BATCH, DEC_SEQ, D_MODEL), 1.0)
    inp['cache_mem_k'] = nrm((DEPTH, DEC_BATCH, N_MEM, X_HEADS, HEAD_DIM), 1.0)
    inp['cache_mem_v'] = nrm((DEPTH, DEC_BATCH, N_MEM, X_HEADS, HEAD_DIM), 1.0)
    inp['state_mlstm_C'] = nrm((N_A, DEC_BATCH, M_HEADS, M_HEAD_DIM, M_HEAD_DIM), 0.1)
    inp['state_mlstm_n'] = nrm((N_A, DEC_BATCH, M_HEADS, M_HEAD_DIM), 0.1)
    inp['state_mlstm_m'] = nrm((N_A, DEC_BATCH, M_HEADS), 1.0)
    inp['state_mlstm_conv'] = nrm((N_A, DEC_BATCH, CONV_W - 1, 2 * TOK_WIDTH), 1.0)
    inp['cache_nsa'] = nrm((N_B, n_pool, PAGE_SIZE, 4, N_KV, HEAD_DIM), 1.0)
    inp['cache_nsa_win'] = nrm((N_B, DEC_BATCH, wbuf, 2, N_KV, HEAD_DIM), 1.0)
    inp['page_table'] = jax.random.permutation(next(keys), n_pool)[:n_used].reshape(DEC_BATCH, n_pages).astype(jnp.int32)
    inp['mem_prompt'] = nrm((BATCH, N_MEM, D_MODEL), 1.0)
    inp['norm_mix'] = gain((DEPTH, D_MODEL))
    inp['norm_mem'] = gain((DEPTH, D_MODEL))
    inp['norm_ffn'] = gain((DEPTH, D_MODEL))
    inp['norm_final'] = gain((D_MODEL,))
    inp['w_mem_kv'] = nrm((DEPTH, D_MODEL, 2 * X_WIDTH), D_MODEL ** -0.5)
    inp['w_in_a'] = nrm((N_A, D_MODEL, A_IN), D_MODEL ** -0.5)
    inp['b_gate_a'] = jnp.concatenate([nrm((N_A, M_HEADS), 0.1), 3.0 + nrm((N_A, M_HEADS), 0.5)], axis=-1)
    inp['conv_a'] = nrm((N_A, CONV_W, 2 * TOK_WIDTH), CONV_W ** -0.5)
    inp['head_norm_a'] = gain((N_A, TOK_WIDTH))
    inp['w_in_b'] = nrm((N_B, D_MODEL, B_IN), D_MODEL ** -0.5)
    inp['b_gate_b'] = nrm((N_B, 3 * N_Q), 0.1)
    inp['w_cmp1'] = nrm((N_B, 2, CMP_LEN * HEAD_DIM, HEAD_DIM), (CMP_LEN * HEAD_DIM) ** -0.5)
    inp['w_cmp2'] = nrm((N_B, 2, HEAD_DIM, HEAD_DIM), HEAD_DIM ** -0.5)
    inp['pe_cmp'] = nrm((N_B, 2, CMP_LEN, HEAD_DIM), 0.1)
    inp['w_out'] = nrm((DEPTH, MIX_WIDTH, D_MODEL), MIX_WIDTH ** -0.5)
    inp['w_ffn_gu'] = nrm((N_A, D_MODEL, 2 * D_FF), D_MODEL ** -0.5)
    inp['w_ffn_d'] = nrm((N_A, D_FF, D_MODEL), D_FF ** -0.5)
    inp['w_router'] = nrm((N_B, D_MODEL, N_EXPERTS), D_MODEL ** -0.5)
    inp['w_moe_gu'] = nrm((N_B, N_EXPERTS, D_MODEL, 2 * E_FF), D_MODEL ** -0.5)
    inp['w_moe_d'] = nrm((N_B, N_EXPERTS, E_FF, D_MODEL), E_FF ** -0.5)
    return inp

def reference(x_prompt, x_sample, cache_mem_k, cache_mem_v, state_mlstm_C, state_mlstm_n,
              state_mlstm_m, state_mlstm_conv, cache_nsa, cache_nsa_win, page_table, mem_prompt,
              norm_mix, norm_mem, norm_ffn, norm_final, w_mem_kv, w_in_a, b_gate_a, conv_a,
              head_norm_a, w_in_b, b_gate_b, w_cmp1, w_cmp2, pe_cmp, w_out, w_ffn_gu, w_ffn_d,
              w_router, w_moe_gu, w_moe_d):
    f32 = jnp.float32
    bp, seq = x_prompt.shape[0], x_prompt.shape[1]
    past_len = page_table.shape[1] * cache_nsa.shape[2]
    wbuf = cache_nsa_win.shape[2]
    slopes = alibi_slopes()
    xp = x_prompt.astype(f32)
    xs = x_sample.astype(f32)
    mem_k_p, mem_v_p = [], []
    C_p, n_p, m_p, conv_p, rows_p, win_p = [], [], [], [], [], []
    C_s, n_s, m_s, conv_s, rows_s, win_s = [], [], [], [], [], []
    for i in range(DEPTH):
        li = i // 2
        up = rmsnorm(xp, norm_mix[i])
        us = rmsnorm(xs, norm_mix[i])
        mk, mv = mem_kv(mem_prompt, norm_mem[i], w_mem_kv[i])
        mem_k_p.append(mk)
        mem_v_p.append(mv)
        if i % 2 == 0:
            par = (conv_a[li], b_gate_a[li], head_norm_a[li])
            hp, qxp, st_p = mlstm_mixer(
                up @ w_in_a[li], jnp.zeros((bp, CONV_W - 1, 2 * TOK_WIDTH), f32),
                jnp.zeros((bp, M_HEADS, M_HEAD_DIM, M_HEAD_DIM), f32),
                jnp.zeros((bp, M_HEADS, M_HEAD_DIM), f32), jnp.zeros((bp, M_HEADS), f32), *par)
            hs, qxs, st_s = mlstm_mixer(
                us @ w_in_a[li], state_mlstm_conv[li], state_mlstm_C[li], state_mlstm_n[li],
                state_mlstm_m[li], *par)
            C_p.append(st_p[0]); n_p.append(st_p[1]); m_p.append(st_p[2]); conv_p.append(st_p[3])
            C_s.append(st_s[0]); n_s.append(st_s[1]); m_s.append(st_s[2]); conv_s.append(st_s[3])
        else:
            par = (w_cmp1[li], w_cmp2[li], pe_cmp[li], slopes)
            qp, kvp, gp, qxp = nsa_split(up @ w_in_b[li], b_gate_b[li])
            qs, kvs, gs, qxs = nsa_split(us @ w_in_b[li], b_gate_b[li])
            hp = nsa_merge(gp, nsa_prompt(qp, kvp, *par))
            hs = nsa_merge(gs, nsa_sample(qs, kvs, cache_nsa, li, page_table, cache_nsa_win[li], past_len, *par))
            rows_p.append(kvp[:, :, :4])
            win_p.append(kvp[:, seq - min(WINDOW, seq):, 4:])
            rows_s.append(kvs[:, :, :4])
            win_s.append(jnp.concatenate([cache_nsa_win[li].astype(f32), kvs[:, :, 4:]], axis=1)[:, -wbuf:])
        xp = xp + jnp.concatenate([hp, mem_attention(qxp, mk, mv)], axis=-1) @ w_out[i]
        xs = xs + jnp.concatenate([hs, mem_attention(qxs, cache_mem_k[i], cache_mem_v[i])], axis=-1) @ w_out[i]
        if i % 2 == 0:
            xp = xp + swiglu(rmsnorm(xp, norm_ffn[i]), w_ffn_gu[li], w_ffn_d[li])
            xs = xs + swiglu(rmsnorm(xs, norm_ffn[i]), w_ffn_gu[li], w_ffn_d[li])
        else:
            xp = xp + moe_swiglu(rmsnorm(xp, norm_ffn[i]), w_router[li], w_moe_gu[li], w_moe_d[li])
            xs = xs + moe_swiglu(rmsnorm(xs, norm_ffn[i]), w_router[li], w_moe_gu[li], w_moe_d[li])
    y_prompt = rmsnorm(xp, norm_final)
    y_sample = rmsnorm(xs, norm_final)
    return (y_prompt, y_sample,
            jnp.stack(mem_k_p), jnp.stack(mem_v_p),
            jnp.stack(C_p), jnp.stack(n_p), jnp.stack(m_p), jnp.stack(conv_p),
            jnp.stack(rows_p), jnp.stack(win_p),
            jnp.stack(C_s), jnp.stack(n_s), jnp.stack(m_s), jnp.stack(conv_s),
            jnp.stack(rows_s), jnp.stack(win_s))


_drawn_inputs = setup_inputs


def setup_inputs(seed=0):
    import zlib

    import numpy as np

    out = dict(_drawn_inputs(seed))
    spreads = {}
    factors = {'norm_mem': 2.775, 'norm_final': 2.85}
    for name, (base, spread) in spreads.items():
        noise = np.random.default_rng([zlib.crc32(name.encode()), seed]).standard_normal(out[name].shape)
        drawn = base * np.exp(spread * noise) if base else spread * noise
        out[name] = __import__('jax').numpy.asarray(drawn.astype(out[name].dtype))
    for name, factor in factors.items():
        out[name] = (out[name] * factor).astype(out[name].dtype)
    return out
```

```python
from contextlib import ExitStack

import numpy as np
import concourse.bass as bass
from concourse import mybir

F32 = mybir.dt.float32
I32 = mybir.dt.int32
ALU = mybir.AluOpType
ACT = mybir.ActivationFunctionType
AX = mybir.AxisListType

P = 128
D = 1024
KT = D // P
TP, TS = 256, 8
NT = TP + TS
HD = 64
MH, MD = 8, 96
TOK = MH * MD
NQ, NKV, GRP = 12, 4, 3
NMEM = 256
XH = 4
CW = 4
DFF, EFF, NE = 2816, 1792, 8
PAGE, NPAGES, NPOOL = 128, 16, 160
PAST = PAGE * NPAGES
WBUF = 512
CST = 16
NSEG = PAST // CST
NCMP = NSEG - 1
NBLK = PAST // 64
NSEL = 16
EPS = 1e-6
FAR = 1e30
SLOPES = [float(np.float32(2.0) ** np.float32(-8.0 * (h + 1) / NQ)) for h in range(NQ)]
RING = 3
SLOT = 4096

SHARED = {
    "proj_mm": (("qk_mm", 16), ("v_mm", 6), ("o_mm", 8), ("g_mm", 3), ("woa_mm", 8),
                ("bq_mm", 6), ("bkv_mm", 9), ("bg_mm", 3), ("wob_mm", 8)),
    "turn_mm": (("set_mm", 17), ("cvh_mm", 1), ("cvo_mm", 4), ("bT_mm", 1), ("qks_mm", 1), ("ms_pt0", 1),
                ("kd_mm", 8), ("kn_mm", 3), ("ms_pt1", 1), ("om_mm", 6), ("pct", 1), ("cbt", 1), ("y_mm", 18)),
    "once_mm": (("mkT_mm0", 1), ("gb_mm", 1), ("hn_mm", 8), ("ms_o0", 1), ("mkT_mm1", 1), ("ms_o1", 1), ("im", 1), ("oc_mm", 1),
                ("rt", 1), ("cbb", 8)),
    "proj_ev": (("woa_ev", 8), ("bq_ev", 6), ("bkv_ev", 9), ("wob_ev", 8)),
    "turn_ev": (("set_ev", 17), ("cvo_ev", 4), ("kd_ev", 8), ("kn_ev", 3), ("om_ev", 6), ("cbb_ev", 8), ("y_ev", 18)),
    "once_dve": tuple((n, 1) for n in (
        "pre0", "qk_done", "mt_s", "n_s", "bd", "hsq", "ms_q0", "ms_d0", "ms_p0", "ms_pte0", "mixm0",
        "q12", "idx", "ms_q1", "ms_d1", "ms_p1", "ms_pte1", "mixm1", "pc_d", "pc_p", "pc_s", "imp", "pct_ev",
        "sel", "oc_ev", "pz0", "mixT", "rt_d", "cb", "cbt_ev")),
    "copied": (("qk_ev", 16), ("v_ev", 6), ("o_ev", 8)),
    "once_act": (("ms_e0", 1), ("gates", 2), ("ms_e1", 1), ("pc_e", 1), ("rt_e", 1)),
}
STAGE = {}
for _sem, _stages in SHARED.items():
    _at = 0
    for _name, _n in _stages:
        STAGE[_name] = (_sem, _at)
        _at += _n


MIX0, MIX1, MEM0, MEM1, FFN0, FFN1, FINAL = range(7)

CONSTS = {}


def _const_arrays():
    p = np.arange(P)
    cols = []

    def add(name, a):
        a = np.asarray(a, np.float32).reshape(P, -1)
        CONSTS[name] = (sum(c.shape[1] for c in cols), a.shape[1])
        cols.append(a)

    add("ident", np.eye(P))
    add("ones", np.ones((P, P)))
    sel = np.zeros((P, 8, P))
    for e in range(8):
        sel[e, e] = 1
    add("sel8", sel)
    t = np.arange(P)
    dist = np.stack([(i * P + t)[:, None] - np.arange(TP)[None] for i in range(2)], 1).astype(np.float64)
    add("dist", np.where(dist >= 0, dist, FAR))
    add("tri", (t[:, None] <= t[None, :]))
    cend = np.arange(TP // CST) * CST + 2 * CST - 1
    dc = np.stack([(i * P + t)[:, None] - cend[None] for i in range(2)], 1).astype(np.float64)
    add("distc", np.where(dc >= 0, dc, FAR))
    add("maskc", dc >= 0)
    g = np.zeros((P, 4))
    for h in range(NQ):
        g[h, h // GRP] = 1
    add("grp", g)
    nsl = np.zeros((P, 1))
    nsl[:NQ, 0] = -np.array(SLOPES)
    add("nsl", nsl)
    add("seg", (p % 8) * 2 * CST)
    first = np.zeros((P, 1, 33, 33))
    first[:] = (np.arange(33)[None, :] < np.arange(33)[:, None])
    add("lower", first)
    return np.ascontiguousarray(np.concatenate(cols, 1))


def _dist12_arrays():
    l, n = np.arange(CST), np.arange(NSEG)
    slc = PAST - (n[None, :] * CST + l[:, None])
    cmp_ = PAST - (n * CST + 2 * CST - 1)
    r, q = np.arange(WBUF // P), np.arange(P)
    win = WBUF - (q[None, :] * (WBUF // P) + r[:, None])
    row = np.concatenate([slc.ravel(), cmp_.ravel(), win.ravel()]).astype(np.float32)
    return np.ascontiguousarray(np.broadcast_to(row, (NQ, row.size)))


def bc(ap, axis, n):
    v = ap.unsqueeze(axis)
    shape = list(v.shape)
    shape[axis] = n
    return v.broadcast_to(tuple(shape))


def chunk_list(I):
    ch = []

    def kview(w, c0, c1):
        return w.rearrange("(k p) c -> p k c", p=P)[:, :, c0:c1]

    def add(name, read, *dmas):
        ch.append((name, read, dmas))

    def std(name, read, w, c0, c1, kt=KT):
        add(name, read, (0, P, (kt, c1 - c0), kview(w, c0, c1)))

    wa, wb, wo, wm = I["w_in_a"][0], I["w_in_b"][0], I["w_out"], I["w_mem_kv"]
    std("mkv0", ("mkv_mm", 2), wm[0], 0, 512)
    for c in range(8):
        read = (("qk_mm", 4 * c + 4), ("v_mm", 3 * (c - 4) + 3), ("o_mm", 4 * (c - 6) + 4))[(c >= 4) + (c >= 6)]
        std(("q", "k", "v", "o")[c // 2] + str(c % 2), read, wa, 384 * c, 384 * c + 384)
    std("gxa", ("g_mm", 3), wa, 3072, 3344)
    for m in range(4):
        sl = slice(256 * m, 256 * m + 256)
        add(f"woa{m}", ("woa_mm", 2 * m + 2),
            (0, MD, (MH, 256), wo[0, 0:TOK, :].rearrange("(k p) c -> p k c", p=MD)[:, :, sl]),
            (MH * 256, P, (2, 256), wo[0, TOK:D, :].rearrange("(k p) c -> p k c", p=P)[:, :, sl]))
    for j in range(DFF // 256):
        gu = I["w_ffn_gu"][0]
        add(f"gu{j}", ("ff_gu", 2 * j + 2), (0, P, (KT, 256), kview(gu, 256 * j, 256 * j + 256)),
            (KT * 256, P, (KT, 256), kview(gu, DFF + 256 * j, DFF + 256 * j + 256)))
    for m in range(KT):
        std(f"dn{m}", ("ff_d", m + 1), I["w_ffn_d"][0], P * m, P * m + P, kt=DFF // P)
    std("mkv1", ("mkv_mm", 4), wm[1], 0, 512)
    for c in range(2):
        std(f"bq{c}", ("bq_mm", 3 * c + 3), wb, 384 * c, 384 * c + 384)
    for c in range(3):
        std(f"bkv{c}", ("bkv_mm", 3 * c + 3), wb, 768 + 512 * c, 1280 + 512 * c)
    std("gxb", ("bg_mm", 3), wb, 2304, 2596)
    for m in range(4):
        std(f"wob{m}", ("wob_mm", 2 * m + 2), wo[1], 256 * m, 256 * m + 256)
    return ch


GU, DN = EFF // 256, D // 256


class Ring:

    def __init__(self, ch):
        self.at, loads = {}, [0] * RING
        for n, (name, _, dmas) in enumerate(ch):
            s = n % RING
            loads[s] += 16 * len(dmas)
            self.at[name] = (s, loads[s])
        self.expert, self.per = [], [0] * RING
        for i in range(GU + DN):
            s = (len(ch) + i) % RING
            self.per[s] += 32 if i < GU else 16
            self.expert.append((s, loads[s] + self.per[s]))


def build(nc, I, O):
    ctx = ExitStack()
    with ctx:
        def sb(name, shape, dt=F32):
            return ctx.enter_context(nc.sbuf_tensor(name, shape, dt))

        sems = {}

        def S(name):
            name = STAGE.get(name, (name,))[0]
            if name not in sems:
                sems[name] = ctx.enter_context(nc.semaphore(name))
            return sems[name]

        def done(name, n=1):
            sem, before = STAGE.get(name, (name, 0))
            return S(sem), before + n

        bank = [ctx.enter_context(nc.psum_tensor(f"bank{i}", [P, 512], F32)) for i in range(8)]

        chunks = chunk_list(I)
        ring_at = Ring(chunks)
        by_name = {name: dmas for name, _, dmas in chunks}
        scr_imp = nc.dram_tensor("scr_imp", (NKV, TS * 33), F32).ap()
        scr_sel = nc.dram_tensor("scr_sel", (NKV, TS * 33), F32).ap()

        ncst = I["consts"].shape[1]
        consts = sb("consts_sb", [P, ncst])

        def C(name):
            a, n = CONSTS[name]
            return consts[:, a:a + n]

        ident, ones = C("ident"), C("ones")
        sel8 = C("sel8").rearrange("p (e m) -> p e m", e=8)
        dist = C("dist").rearrange("p (i k) -> p i k", i=2)
        distc = C("distc").rearrange("p (i n) -> p i n", i=2)
        maskc = C("maskc").rearrange("p (i n) -> p i n", i=2)
        tri, grp, nsl = C("tri"), C("grp"), C("nsl")
        lower = C("lower")
        xT = sb("xT", [P, KT, NT])
        uT = sb("uT", [P, KT, NT])
        rstd = sb("rstd", [P, NT])
        rtmp = sb("rtmp", [P, NT])
        gain = sb("gain", [P, 56])
        memT = sb("memT", [P, KT, NMEM])
        ring = sb("ring", [P, RING, SLOT])
        mkv = sb("mkv", [P, 2, 512])
        mkT = sb("mkT", [P, 2, NMEM])
        xq = sb("xq", [P, 2, NT])
        mixm = sb("mixm", [P, 2, NT])
        small = sb("small", [P, 512])
        nfree = nc.sbuf_bytes_remaining // 4 - 64
        arena = sb("arena", [P, nfree])

        top = [0]

        def area(*shape, at=None):
            n = int(np.prod(shape[1:]))
            a = top[0] if at is None else at
            top[0] = max(top[0], a + n)
            assert top[0] <= nfree, (top[0], nfree)
            v = arena[0:shape[0], a:a + n]
            if len(shape) > 2:
                names = "abcd"[:len(shape) - 1]
                v = v.rearrange(f"p ({' '.join(names)}) -> p {' '.join(names)}",
                                **{x: s for x, s in zip(names[:-1], shape[1:-1])})
            return v

        def place():
            return top[0]

        xin = area(P, 2, D)
        xsin = area(TS, D)
        min_ = area(P, 2, D)
        grow = area(56, P)
        cwrow = area(64, MD)
        hgrow = area(MH, MD)
        top[0] = 0
        sq = area(P, KT, NT)
        kept = place()
        cw = area(MD, 64)
        hg = area(MD, MH)
        og = area(MD, MH, NT)
        vs = area(TS, TOK)
        hT = area(MD, MH, NT)
        gs = area(TS, 16, MH)
        bT = area(P, 2, 16)
        gbias_p = area(MH, 2)
        gbias_s = area(TS, 16)
        late = place()
        qk = area(MD, 16, NT)
        vp = area(P, 2, TOK)
        ab = area(MH, 12, TP)
        a_work = place()
        preP = area(MD, 16, TP + 3)
        preS = area(MD, 16, TS, CW)
        cvh = area(24, 2 * TOK)
        cv3 = area(3, 2 * TOK)
        cv8 = area(TS, 2 * TOK)
        ctmp = area(MD, 16, TS)
        top[0] = a_work
        wdec = area(P, 2, 384)
        sw = area(P, 2, 384)
        kw = area(P, 2, 2, MD)
        hden = area(MD, TP)
        cout = area(MD, MH, MD)
        nout = area(1, MH, MD)
        assert place() <= a_work + 16 * (TP + 3)
        top[0] = late
        cs = area(MD, TS, MH, MD)
        assert place() <= a_work
        top[0] = a_work
        qks = area(TS, 16, MD)
        kws = area(TS, MH, MD)
        ns = area(TS, MH, MD)
        n0 = area(TS, MH, MD)
        m0 = area(TS, MH)
        bdg = area(TS, 2, TS, MH)
        kdiag = area(TS, 2, TS, MD)
        qdiag = area(TS, 2, TS, MD)
        ctm = area(MD, 2, 4, MD)
        gb = area(MD, 2, TS, MH)
        num = area(MD, MH, TS)
        top[0] = late
        mvs_a = area(P, TS, 2, 256)
        assert place() <= a_work
        top[0] = a_work
        mem_u_a = area(P, KT, NMEM)
        top[0] = a_work
        pm_a = area(P, 2, NMEM)
        pmT_a = area(P, 2, 2, P)
        mks_a = area(P, TS, 2, 256)
        mksT_a = area(P, 2, 512)
        xqz_a = area(P, TS, 2, XH)
        pms_a = area(XH, TS, NMEM)
        pmsT_a = area(P, TS, 2, XH)
        top[0] = kept
        hff = area(P, DFF // P, NT)
        silu = area(P, 2, NT)
        ytmp = area(P, 2, NT)
        comb = area(P, NE, NT)
        combT = area(NE, NT)
        lg = area(P, 3, 4, 8)
        rk = area(P, 3, 8, 8)
        rk2 = area(P, 3, 8, 8)
        l8 = area(P, 3, 8)
        wr = area(P, KT, NE)
        top[0] = kept
        ysb = area(P, 3, D)

        top[0] = kept
        mixT = area(P, 6, NT)
        kvS = area(TS, 6, 256)
        g12 = area(NQ, 3, TS)
        pages = area(P, TS).bitcast(I32)
        idxb = area(P, TS).bitcast(I32)
        q12 = area(HD, TS, NKV, NQ)
        qblk = area(P, TS, 2, NQ)
        knT = area(HD, 2, NKV, TS)
        sel12 = area(NQ, TS, 33)
        oc = area(P, TS, 2, 6)
        slc0 = place()
        perow = area(32, P)
        w2 = area(HD, 2, HD)
        vcp = area(TP // CST, NKV, HD)
        kcp2 = area(P, NKV, 16)
        hconst = area(HD, 2)
        pec = area(P, 2, CST)
        gb12 = area(NQ, 3)
        gbp = area(P, 36)
        gp = area(P, 2, 36)
        qT = area(P, 6, NT)
        w1 = area(P, 2, 8, 2, HD)
        b_work = place()
        mem_u_b = area(P, KT, NMEM)
        top[0] = b_work
        pm_b = area(P, 2, NMEM)
        pmT_b = area(P, 2, 2, P)
        mks_b = area(P, TS, 2, 256)
        mvs_b = area(P, TS, 2, 256)
        mksT_b = area(P, 2, 512)
        xqz_b = area(P, TS, 2, XH)
        pms_b = sq.rearrange("p k n -> p (k n)")[0:XH, 0:TS * NMEM].rearrange("p (b n) -> p b n", b=TS)
        pmsT_b = area(P, TS, 2, XH)
        mem_end = place()
        top[0] = b_work
        gat = area(P, 2, 8, 512)
        xt = area(P, 2, 512)
        hb = area(HD, 2, 512)
        hs = area(HD, 2, 512)
        cmp_end = place()
        kc = area(HD, 2, 512)
        vcmp = area(P, TS, 256)
        imp = area(NKV, TS, 33)
        imp32 = area(32, 33)
        sel32 = area(32, 33)
        pc = area(NQ, TS, NSEG)
        pcT = area(P, TS, NQ)
        top[0] = b_work
        rank = area(32, 33, 33)
        rank2 = area(32, 33, 33)
        psum4 = area(NKV, TS, NSEG)
        top[0] = b_work
        sc = area(P, 2, 2, TP)
        scc = area(P, 2, 16)
        pT = area(P, 2, 4, P)
        pcpT = area(16, 2, P)
        assert place() <= cmp_end
        top[0] = max(cmp_end, mem_end)
        kvP = area(P, 2, 6, 256)
        kdup = area(P, 2, NKV, TP)
        oP = sq.rearrange("p k n -> p (k n)")[:, 0:2 * TOK].rearrange("p (i c) -> p i c", i=2)
        d12s = memT.rearrange("p k n -> p (k n)")[0:NQ, :]
        d12b = mkv.rearrange("p k n -> p (k n)")[0:NQ, 0:NSEG + WBUF]
        top[0] = slc0
        gsl = area(P, 2, CST, 512)
        winb = area(P, 4, 512)
        s12 = area(NQ, PAST + 1 + WBUF + 1)
        sqf = sq.rearrange("p k n -> p (k n)")
        kTb = sqf[:, 0:1024].rearrange("p (j n) -> p j n", j=2)
        pTs = sqf[:, 1024:1024 + 2 * 264].rearrange("p (a n) -> p a n", a=2)
        pz = sqf[0:NQ, 1600:1600 + 128].rearrange("p (r b c) -> p r b c", r=2, b=TS)
        oTsb = sqf[:, 1728:1728 + 96].rearrange("p (b j c) -> p b j c", b=TS, j=2)

        block = ctx.enter_context(nc.Block())
        counts = {}

        def chain(eng, own):
            def link(ins, name=None):
                s = name or own
                counts[s] = counts.get(s, 0) + 1
                ins.then_inc(S(s), 1)
                eng.wait_ge(*done(s, counts[s]))
            return link

        def slot_view(name):
            s, _ = ring_at.at[name]
            dmas = by_name[name]
            out = []
            for off, parts, dims, _ in dmas:
                n = int(np.prod(dims))
                out.append(ring[0:parts, s, off:off + n].rearrange("p (k c) -> p k c", k=dims[0]))
            return out[0] if len(out) == 1 else out

        MEMPLACES = [(pm_a, pmT_a, mks_a, mvs_a, mksT_a, xqz_a, pms_a, pmsT_a),
                     (pm_b, pmT_b, mks_b, mvs_b, mksT_b, xqz_b, pms_b, pmsT_b)]

        def mem_project(pe, mm, tr, got, L):
            mem_u = (mem_u_a, mem_u_b)[L]
            w = got(f"mkv{L}")
            for i in range(2):
                for k in range(KT):
                    m = mm(bank[5 + i][:, :], mem_u[:, k, P * i:P * i + P], w[:, k, :], k == 0, k == KT - 1)
                m.then_inc(S("mkv_mm"), 1)
            pe.wait_ge(S("mkv_ev"), 3 * L + 2)
            for j in range(2):
                for i in range(2):
                    m = tr(bank[5][:, NMEM * j + P * i:NMEM * j + P * i + P], mkv[:, i, P * j:P * j + P], P)
            m.then_inc(S(f"mkT_mm{L}"), 1)

        def mem_project_dve(dve, link, V, L):
            if L:
                dve.wait_ge(S("st_mem"), 64)
            for i in range(2):
                dve.wait_ge(S("mkv_mm"), 2 * L + i + 1)
                link(V.tensor_copy(mkv[:, i, :], bank[5 + i][:, :]), "mkv_ev")
            dve.wait_ge(*done(f"mkT_mm{L}"))
            link(V.tensor_copy(mkT.rearrange("p j n -> p (j n)"), bank[5][:, :]), "mkv_ev")

        def mem_store(pool, store, L):
            pool.wait_ge(S("mkv_ev"), 3 * L + 2)
            for c, name in enumerate(("mem_k_p", "mem_v_p")):
                for i in range(2):
                    store(O[name][L, 0, P * i:P * i + P].rearrange("n h d -> n (h d)"),
                          mkv[:, i, 256 * c:256 * c + 256], "st_mem")

        def mem_load(pool, load, L):
            if L == 0:
                pool.wait_ge(S("st_c"), 16)
            mks, mvs = MEMPLACES[L][2:4]
            load("ld_mks", mks, I["cache_mem_k"][L].rearrange("b (p r) h d -> p b r (h d)", r=2))
            load("ld_mvs", mvs, I["cache_mem_v"][L].rearrange("b (p r) h d -> p b r (h d)", r=2))

        def mem_attend(pe, mm, tr, L):
            pm, pmT, mks, mvs, mksT, xqz, pms, pmsT = MEMPLACES[L]
            o = 8 * L

            def scores(n):
                h, i = n // 2, n % 2
                r = slice(64 * (h % 2), 64 * (h % 2) + 64)
                if n >= 2:
                    pe.wait_ge(S("ma_p"), o + n - 1)
                mm(bank[n % 2][:, 0:NMEM], xq[r, h // 2, P * i:P * i + P], mkT[r, h // 2, :]).then_inc(S("ma_s"), 1)

            def values(n):
                h = n // 2
                pe.wait_ge(S("ma_p"), o + n + 1)
                if n >= 2:
                    pe.wait_ge(S("ma_pt"), o + n - 1)
                for t in range(2):
                    m = tr(bank[2 + n % 2][:, P * t:P * t + P], pm[:, n % 2, P * t:P * t + P], P)
                m.then_inc(S("ma_t"), 1)
                pe.wait_ge(S("ma_pt"), o + n + 1)
                if n >= 2:
                    pe.wait_ge(S("ma_oe"), o + n - 1)
                for t in range(2):
                    m = mm(bank[4 + n % 2][:, 0:P], mkv[:, t, 256 + P * (h // 2):256 + P * (h // 2) + P],
                           pmT[:, n % 2, t, :], t == 0, t == 1)
                m.then_inc(S("ma_o"), 1)

            scores(0)
            for n in range(8):
                if n + 1 < 8:
                    scores(n + 1)
                values(n)
            pe.wait_ge(S("ld_mks"), 16 * L + 16)
            pe.wait_ge(*done(f"ms_q{L}"))
            pe.wait_ge(S("ma_oe"), o + 8)
            for b in range(TS):
                if b >= 2:
                    pe.wait_ge(S("ms_k"), o + b - 1)
                for j in range(2):
                    for r in range(2):
                        m = tr(bank[b % 2][:, 256 * j + P * r:256 * j + P * r + P], mks[:, b, r, P * j:P * j + P], P)
                m.then_inc(S("ms_t"), 1)
                pe.wait_ge(S("ms_k"), o + b + 1)
                for j in range(2):
                    m = mm(bank[4 + b // 2][0:XH, 256 * (b % 2):256 * (b % 2) + 256], xqz[:, b, j, :],
                           mksT[:, b % 2, 256 * j:256 * j + 256], j == 0, j == 1)
                m.then_inc(S("ms_s"), 1)
            pe.wait_ge(*done(f"ms_p{L}"))
            pe.wait_ge(S("ms_k"), o + 8)
            for b in range(TS):
                for r in range(2):
                    m = tr(bank[0][:, 8 * b + 4 * r:8 * b + 4 * r + 4], pms[:, b, P * r:P * r + P], XH)
            m.then_inc(S(f"ms_pt{L}"), 1)
            pe.wait_ge(S("ld_mvs"), 16 * L + 16)
            pe.wait_ge(*done(f"ms_pte{L}"))
            for b in range(TS):
                for j in range(2):
                    for r in range(2):
                        m = mm(bank[1][:, 4 * b + 2 * j:4 * b + 2 * j + 2], mvs[:, b, r, P * j:P * j + P],
                               pmsT[:, b, r, 2 * j:2 * j + 2], r == 0, r == 1)
            m.then_inc(S(f"ms_o{L}"), 1)

        def mem_attend_dve(dve, link, V, L):
            pm, pmT, mks, mvs, mksT, xqz, pms, pmsT = MEMPLACES[L]
            o = 8 * L
            st = small[:, 0:64]
            link(V.memset(xqz, 0.0))
            for h in range(XH):
                r = slice(64 * (h % 2), 64 * (h % 2) + 64)
                link(V.tensor_copy(xqz[r, :, h // 2, h], xq[r, h // 2, TP:NT]), f"ms_q{L}" if h == XH - 1 else None)
            for n in range(8):
                h, i = n // 2, n % 2
                r = slice(64 * (h % 2), 64 * (h % 2) + 64)
                dve.wait_ge(S("ma_s"), o + n + 1)
                link(V.tensor_reduce(st[:, 4 * (n % 2):4 * (n % 2) + 1], bank[n % 2][:, 0:NMEM], AX.X, ALU.max, negate=True), "ma_mx")
                dve.wait_ge(S("ma_e"), o + n + 1)
                link(V.reciprocal(st[:, 4 * (n % 2) + 2:4 * (n % 2) + 3], st[:, 4 * (n % 2) + 1:4 * (n % 2) + 2]))
                link(V.tensor_scalar(pm[:, n % 2, :], pm[:, n % 2, :], st[:, 4 * (n % 2) + 2:4 * (n % 2) + 3], None, ALU.mult), "ma_p")
                dve.wait_ge(S("ma_t"), o + n + 1)
                link(V.tensor_copy(pmT[:, n % 2, :, :].rearrange("p t n -> p (t n)"), bank[2 + n % 2][:, 0:256]), "ma_pt")
                dve.wait_ge(S("ma_o"), o + n + 1)
                link(V.tensor_copy(mixm[r, h // 2, P * i:P * i + P], bank[4 + n % 2][r, 0:P]), "ma_oe")
            for i in range(4):
                dve.wait_ge(S("ms_s"), o + 2 * i + 2)
                link(V.tensor_copy(pms[:, 2 * i:2 * i + 2, :].rearrange("p b n -> p (b n)"), bank[4 + i][0:XH, :]))
            mx, sm = small[0:XH, 64:72], small[0:XH, 72:80]
            link(V.tensor_reduce(mx, pms, AX.X, ALU.max))
            link(V.tensor_tensor(pms, pms, bc(mx, 2, NMEM), ALU.subtract), f"ms_d{L}")
            dve.wait_ge(*done(f"ms_e{L}"))
            link(V.tensor_reduce(sm, pms, AX.X, ALU.add))
            link(V.reciprocal(mx, sm))
            link(V.tensor_tensor(pms, pms, bc(mx, 2, NMEM), ALU.mult), f"ms_p{L}")
            dve.wait_ge(*done(f"ms_pt{L}"))
            link(V.tensor_copy(pmsT.rearrange("p b r h -> p (b r h)"), bank[0][:, 0:64]), f"ms_pte{L}")
            dve.wait_ge(*done(f"ms_o{L}"))
            ov = bank[1][:, 0:32].rearrange("p (b c) -> p b c", b=TS)
            for h in range(XH):
                r = slice(64 * (h % 2), 64 * (h % 2) + 64)
                link(V.tensor_copy(mixm[r, h // 2, TP:NT], ov[r, :, 2 * (h // 2) + h % 2]), f"mixm{L}" if h == XH - 1 else None)

        def mem_attend_act(act, link, f, L):
            pm, pmT, mks, mvs, mksT, xqz, pms, pmsT = MEMPLACES[L]
            o = 8 * L
            st = small[:, 0:64]
            for n in range(8):
                act.wait_ge(S("ma_mx"), o + n + 1)
                if n >= 2:
                    act.wait_ge(S("ma_t"), o + n - 1)
                link(f(pm[:, n % 2, :], bank[n % 2][:, 0:NMEM], ACT.Exp, bias=st[:, 4 * (n % 2):4 * (n % 2) + 1],
                       accum_out=st[:, 4 * (n % 2) + 1:4 * (n % 2) + 2]), "ma_e")
            for b in range(TS):
                act.wait_ge(S("ms_t"), o + b + 1)
                if b >= 2:
                    act.wait_ge(S("ms_s"), o + b - 1)
                link(f(mksT[:, b % 2, :], bank[b % 2][:, :], ACT.Copy), "ms_k")
            act.wait_ge(*done(f"ms_d{L}"))
            link(f(pms, pms, ACT.Exp), f"ms_e{L}")

        def layer_b_pe(pe, mm, tr, got, norm):
            norm(3, NT)
            pe.wait_ge(S("mem_u"), 2)
            mem_project(pe, mm, tr, got, 1)
            pe.wait_ge(S("nrm_out"), 4)
            for t in range(6):
                if t % 3 == 0:
                    w = got(f"bq{t // 3}")
                if t >= 2:
                    pe.wait_ge(*done("bq_ev", t - 1))
                c0 = (t % 3) * P
                for k in range(KT):
                    m = mm(bank[t % 2][:, 0:NT], w[:, k, c0:c0 + P], uT[:, k, :], k == 0, k == KT - 1)
                m.then_inc(S("bq_mm"), 1)
            for n in range(9):
                c, i = n // 3, n % 3
                if i == 0:
                    w = got(f"bkv{c}")
                if n >= 3:
                    pe.wait_ge(*done("bkv_ev", n - 2))
                a, z = P * i, min(P * i + P, NT)
                for k in range(KT):
                    m = mm(bank[2 + i][0:z - a, :], uT[:, k, a:z], w[:, k, :], k == 0, k == KT - 1)
                m.then_inc(S("bkv_mm"), 1)
            w = got("gxb")
            pe.wait_ge(*done("bkv_ev", 9))
            for i in range(2):
                for k in range(KT):
                    mm(bank[2 + i][:, 0:36], uT[:, k, P * i:P * i + P], w[:, k, 0:36], k == 0, k == KT - 1)
            for c in range(3):
                for k in range(KT):
                    m = mm(bank[4][0:NQ, TS * c:TS * c + TS], w[:, k, NQ * c:NQ * c + NQ], uT[:, k, TP:NT], k == 0, k == KT - 1)
            m.then_inc(S("bg_mm"), 1)
            pe.wait_ge(S("mkv_ev"), 6)
            for j in range(2):
                for k in range(KT):
                    m = mm(bank[5 + j][:, 0:NT], w[:, k, 36 + P * j:36 + P * j + P], uT[:, k, :], k == 0, k == KT - 1)
                m.then_inc(S("bg_mm"), 1)
            pe.wait_ge(*done("bq_ev", 6))
            for n in range(8):
                br, g = n // 4, n % 4
                if n >= 2:
                    pe.wait_ge(*done("kd_ev", n - 1))
                for t in range(2):
                    m = tr(bank[n % 2][0:HD, P * t:P * t + P], kvP[:, t, 2 + 2 * br, HD * g:HD * g + HD], P)
                m.then_inc(S("kd_mm"), 1)
            pe.wait_ge(S("bg_ev"), 1)
            for n in range(8):
                br, g = n // 4, n % 4
                m = tr(bank[2][0:HD, TS * n:TS * n + TS], kvS[:, 2 + 2 * br, HD * g:HD * g + HD], TS)
            m.then_inc(S("kn_mm"), 1)
            pe.wait_ge(S("ld_w1"), 96)
            tr(bank[3][:, 0:32], perow, 32).then_inc(S("kn_mm"), 1)
            pe.wait_ge(*done("kn_ev", 2))
            for c in range(2):
                for i in range(CST):
                    m = mm(bank[4][0:HD, c:c + 1], w1[:, c, i % 8, i // 8, :], pec[:, c, i:i + 1], i == 0, i == CST - 1)
            m.then_inc(S("kn_mm"), 1)
            pe.wait_ge(*done("kn_ev", 3))
            mem_attend(pe, mm, tr, 1)
            pe.wait_ge(*done("mixm1"))
            compress_pe(pe, mm, tr, 0)

            def scores(n):
                h, i = n // 2, n % 2
                g, nk, r = h // GRP, P * (i + 1), slice(64 * (h % 2), 64 * (h % 2) + 64)
                q = qT[r, h // 2, P * i:P * i + P]
                if n >= 2:
                    pe.wait_ge(S("ps"), n - 1)
                mm(bank[n % 2][:, 0:nk], q, kdup[r, 0, g, 0:nk])
                mm(bank[n % 2][:, TP:TP + nk], q, kdup[r, 1, g, 0:nk])
                mm(bank[(2, 5)[n % 2]][:, 0:15], q, kcp2[r, g, 0:15]).then_inc(S("p_s"), 1)

            def values(n):
                h, i = n // 2, n % 2
                g = h // GRP
                pe.wait_ge(S("p_p"), n + 1)
                if n >= 2:
                    pe.wait_ge(S("p_te"), n - 1)
                    pe.wait_ge(S("p_oe"), n - 1)
                for br in range(2):
                    for t in range(i + 1):
                        tr(bank[3 + n % 2][:, TP * br + P * t:TP * br + P * t + P], sc[:, n % 2, br, P * t:P * t + P], P)
                tr(bank[6 + n % 2][0:15, P:2 * P], scc[:, n % 2, 0:15], P).then_inc(S("p_t"), 1)
                pe.wait_ge(S("p_te"), n + 1)
                o = bank[6 + n % 2][:, 0:HD]
                for br in range(2):
                    for t in range(i + 1):
                        mm(o, pT[:, n % 2, 2 * br + t, :], kvP[:, t, 3 + 2 * br, HD * g:HD * g + HD], br == 0 and t == 0, False)
                mm(o, pcpT[0:15, n % 2, :], vcp[0:15, g, :], False, True).then_inc(S("p_o"), 1)

            pe.wait_ge(*done("kd_ev", 8))
            pe.wait_ge(S("kve"), 1)
            scores(0)
            for n in range(2 * NQ):
                if n + 1 < 2 * NQ:
                    scores(n + 1)
                values(n)
            pe.wait_ge(S("p_oe"), 2 * NQ)
            for j in range(6):
                if j >= 2:
                    pe.wait_ge(*done("om_ev", j - 1))
                for i in range(2):
                    m = tr(bank[j % 2][:, P * i:P * i + P], oP[:, i, P * j:P * j + P], P)
                m.then_inc(S("om_mm"), 1)
            pe.wait_ge(*done("om_ev", 6))

            pe.wait_ge(*done("q12"))
            for c in range(1, TS + 1):
                compress_pe(pe, mm, tr, c)
            pe.wait_ge(*done("pc_p"))
            for i in range(2):
                m = mm(bank[i][0:NKV, 0:4 * NCMP], grp[0:NQ, :], pc[:, 4 * i:4 * i + 4, 0:NCMP])
            m.then_inc(S("im"), 1)
            pe.wait_ge(*done("pc_s"))
            for b in range(TS):
                m = tr(bank[2][0:NCMP, NQ * b:NQ * b + NQ], pc[:, b, 0:NCMP], NQ)
            m.then_inc(S("pct"), 1)
            pe.wait_ge(*done("pct_ev"))
            for b in range(TS):
                for j in range(2):
                    m = mm(bank[3][:, NQ * b + 6 * j:NQ * b + 6 * j + 6], vcmp[0:NCMP, b, P * j:P * j + P],
                           pcT[0:NCMP, b, 6 * j:6 * j + 6])
            m.then_inc(S("oc_mm"), 1)

            def keys(b):
                for c in range(5):
                    n = 5 * b + c
                    if c == 0:
                        pe.wait_ge(S(f"ld_g{b % 2}"), 256 * (b // 2 + 1))
                    if c == 4:
                        pe.wait_ge(S("ld_win"), 16 * (b + 1))
                    for j in range(2):
                        if n:
                            pe.wait_ge(S("kt_e"), 2 * n - 1 + j)
                        for r in range(4):
                            src = gsl[:, b % 2, 4 * c + r, P * j:P * j + P] if c < 4 else winb[:, r, P * j:P * j + P]
                            m = tr(bank[j][:, P * r:P * r + P], src, P)
                        m.then_inc(S("kt_t"), 1)
                    pe.wait_ge(S("kt_e"), 2 * n + 2)
                    if b:
                        pe.wait_ge(S("s_ev"), 5 * b - 4 + c)
                    mm(bank[2 + c][0:NQ, :], qblk[:, b, 0, :], kTb[:, 0, :], True, False)
                    mm(bank[2 + c][0:NQ, :], qblk[:, b, 1, :], kTb[:, 1, :], False, True).then_inc(S("k_s"), 1)
                if b:
                    pe.wait_ge(S("s_n"), b)
                for br in range(2):
                    for g in range(NKV):
                        m = mm(bank[7][0:NQ, br:br + 1], q12[:, b, g, :], knT[:, br, g, b:b + 1], g == 0, g == NKV - 1)
                m.then_inc(S("k_n"), 1)

            def vals(b):
                pe.wait_ge(S("p12"), b + 1)
                for l in range(CST):
                    tr(bank[7][:, 8 + NQ * l:8 + NQ * l + NQ], s12[:, P * l:P * l + P], NQ)
                for r in range(4):
                    a = PAST + 1 + P * r
                    tr(bank[7][:, 200 + NQ * r:200 + NQ * r + NQ], s12[:, a:a + P], NQ)
                for br in range(2):
                    m = tr(bank[7][0:TS, 248 + NQ * br:248 + NQ * br + NQ], pz[:, br, b, :], NQ)
                m.then_inc(S("pt_mm"), 1)
                pe.wait_ge(S("pt_ev"), b + 1)
                p_ = pTs[:, b % 2, :]
                for j in range(2):
                    o = bank[7][:, 272 + NQ * b + 6 * j:272 + NQ * b + 6 * j + 6]
                    for l in range(CST):
                        mm(o, gsl[:, b % 2, l, 256 + P * j:256 + P * j + P], p_[:, NQ * l + 6 * j:NQ * l + 6 * j + 6], l == 0, False)
                    for r in range(4):
                        mm(o, winb[:, r, 256 + P * j:256 + P * j + P], p_[:, 192 + NQ * r + 6 * j:192 + NQ * r + 6 * j + 6], False, False)
                    for br in range(2):
                        m = mm(o, kvS[:, 3 + 2 * br, P * j:P * j + P], p_[0:TS, 240 + NQ * br + 6 * j:240 + NQ * br + 6 * j + 6],
                               False, br == 1)
                m.then_inc(S("pv_mm"), 1)

            pe.wait_ge(*done("oc_ev"))
            pe.wait_ge(*done("pz0"))
            keys(0)
            for b in range(TS):
                vals(b)
                if b + 1 < TS:
                    keys(b + 1)

            pe.wait_ge(*done("mixT"))
            for m_ in range(KT):
                if m_ % 2 == 0:
                    w = got(f"wob{m_ // 2}")
                if m_ >= 2:
                    pe.wait_ge(*done("wob_ev", m_ - 1))
                c0 = (m_ % 2) * P
                for j in range(KT):
                    rhs = mixT[:, j, :] if j < 6 else mixm[:, j - 6, :]
                    m = mm(bank[m_ % 2][:, 0:NT], w[:, j, c0:c0 + P], rhs, j == 0, j == KT - 1)
                m.then_inc(S("wob_mm"), 1)
            norm(4, NT)

            pe.wait_ge(S("ld_wr"), 16)
            pe.wait_ge(S("nrm_out"), 5)
            for i in range(3):
                a, z = P * i, min(P * i + P, NT)
                for k in range(KT):
                    m = mm(bank[2][0:z - a, NE * i:NE * i + NE], uT[:, k, a:z], wr[:, k, :], k == 0, k == KT - 1)
            m.then_inc(S("rt"), 1)
            pe.wait_ge(*done("cb"))
            for i in range(3):
                a, z = P * i, min(P * i + P, NT)
                m = tr(bank[3][0:NE, a:z], lg[0:z - a, i, 2, :], z - a)
            m.then_inc(S("cbt"), 1)
            pe.wait_ge(*done("cbt_ev"))
            for e in range(NE):
                if e >= 2:
                    pe.wait_ge(*done("cbb_ev", e - 1))
                mm(bank[e % 2][:, 0:NT], sel8[0:NE, e, :], combT).then_inc(S("cbb"), 1)
            pe.wait_ge(*done("cbb_ev", NE))

            with pe.Fori(0, NE) as e:
                def in_slot(i):
                    s, first = ring_at.expert[i]
                    pe.wait_ge(S(f"w_in{s}"), e * ring_at.per[s] + first)
                    return ring[:, s, :]

                for j in range(EFF // P):
                    if j % 2 == 0:
                        w = in_slot(j // 2).rearrange("p (u k c) -> p u k c", u=2, k=KT)
                    if j >= 2:
                        pe.wait_ge(S("m_h"), e * (EFF // P) + j)
                    c0 = (j % 2) * P
                    for u in range(2):
                        for k in range(KT):
                            m = mm(bank[2 * (j % 2) + u][:, 0:NT], w[:, u, k, c0:c0 + P], uT[:, k, :], k == 0, k == KT - 1)
                    m.then_inc(S("m_gu"), 1)
                pe.wait_ge(S("m_h"), e * (EFF // P) + EFF // P + 1)
                for m_ in range(KT):
                    if m_ % 2 == 0:
                        w = in_slot(GU + m_ // 2)[:, 0:EFF // P * 256].rearrange("p (k c) -> p k c", c=256)
                    if m_ < 4:
                        pe.wait_ge(S("m_y"), e * KT + 1)
                    else:
                        pe.wait_ge(S("m_y"), e * KT + (m_ - 2))
                    c0 = (m_ % 2) * P
                    for k in range(EFF // P):
                        m = mm(bank[4 + m_ % 4][:, 0:NT], w[:, k, c0:c0 + P], hff[:, k, :], k == 0, k == EFF // P - 1)
                    m.then_inc(S("m_d"), 1)

            norm(5, NT)
            pe.wait_ge(S("nrm_out"), 6)
            for n in range(2 * KT + 2):
                i, k = (n // 8, n % 8) if n < 16 else (2, n - 16)
                if n >= 4:
                    pe.wait_ge(*done("y_ev", n - 3))
                if i < 2:
                    m = tr(bank[n % 4][:, 0:P], uT[:, k, P * i:P * i + P], P)
                else:
                    for q in range(4):
                        m = tr(bank[n % 4][0:TS, P * q:P * q + P], uT[:, 4 * k + q, TP:NT], P)
                m.then_inc(S("y_mm"), 1)

        def spread(kd, r, ns):
            row, odd = r // 2, r % 2
            return (xt[HD * row:HD * row + HD, kd, 0:NKV * ns].rearrange("p (j o n) -> p j o n", j=2, o=2)[:, :, odd, :],
                    bank[kd][HD * odd:HD * odd + HD, 2 * ns * row:2 * ns * row + 2 * ns].rearrange("p (j n) -> p j n", j=2))

        def compress_pe(pe, mm, tr, c):
            ns = TP // CST if c == 0 else NSEG
            nv, W = ns - 1, NKV * ns

            def turn(i, kd):
                half = i // 4
                if kd == 0 and i % 4 == 0:
                    pe.wait_ge(S(f"ld_c{half}"), 16 if c == 0 else 16 + 128 * c)
                if c or i:
                    pe.wait_ge(S(f"xe{kd}"), 8 * c + i)
                for r in range(2):
                    for j in range(2):
                        a = 256 * kd + P * j
                        m = tr(bank[kd][:, ns * (2 * r + j):ns * (2 * r + j) + ns],
                               gat[0:ns, half, 2 * (i % 4) + r, a:a + P], ns)
                m.then_inc(S("ct"), 1)

            def mul(i, kd):
                if i == 0 and c:
                    pe.wait_ge(S("hs"), 2 * c)
                pe.wait_ge(S(f"xe{kd}"), 8 * c + i + 1)
                pair = w1[:, kd, i, :, :].rearrange("p a e -> p (a e)")
                mm(bank[2 + kd][:, 0:W], pair, xt[:, kd, 0:W], i == 0, i == 7).then_inc(S("cm"), 1)

            steps = [(i, kd) for i in range(8) for kd in range(2)]
            turn(*steps[0])
            for n, s in enumerate(steps):
                if n + 1 < len(steps):
                    turn(*steps[n + 1])
                mul(*s)
            pe.wait_ge(S("ge"), c + 1)
            if c:
                pe.wait_ge(S("kve"), c)
            mm(bank[4][0:HD, 0:NKV * nv], w2[:, 0, :], hs[:, 0, 0:NKV * nv])
            for g in range(NKV):
                m = mm(bank[5][0:nv, HD * g:HD * g + HD], hs[:, 1, nv * g:nv * g + nv], w2[:, 1, :])
            m.then_inc(S("kv2"), 1)
            if c:
                b = c - 1
                pe.wait_ge(S("kve"), c + 1)
                for g in range(NKV):
                    m = mm(bank[6 + b // 4][0:NQ, NCMP * (b % 4):NCMP * (b % 4) + NCMP], q12[:, b, g, :],
                           kc[:, c % 2, NCMP * g:NCMP * g + NCMP], g == 0, g == NKV - 1)
                m.then_inc(S("cs_mm"), 1)

        def compress_dve(dve, link, V, c):
            ns = TP // CST if c == 0 else NSEG
            nv, W = ns - 1, NKV * ns
            for i in range(8):
                dve.wait_ge(S("ct"), 2 * (8 * c + i) + 2)
                if c or i:
                    dve.wait_ge(S("cm"), 2 * (8 * c + i))
                for r in range(4):
                    link(V.tensor_copy(*spread(1, r, ns)), "xe1" if r == 3 else None)
            for kd in range(2):
                dve.wait_ge(S("hb"), 2 * c + kd + 1)
                if c:
                    dve.wait_ge(S("kv2"), c)
                o = hs[:, kd, 0:NKV * nv].rearrange("p (g n) -> p g n", g=NKV)
                link(V.tensor_tensor(o, bank[2 + kd][0:HD, 0:W].rearrange("p (g n) -> p g n", g=NKV)[:, :, 0:nv],
                                     hb[:, kd, 0:W].rearrange("p (g n) -> p g n", g=NKV)[:, :, 1:ns], ALU.add), "hs")
            dve.wait_ge(S("kv2"), c + 1)
            if c == 0:
                k4 = bank[4][0:HD, 0:NKV * nv].rearrange("p (g n) -> p g n", g=NKV)
                link(V.tensor_copy(kcp2[0:HD, :, 0:nv], k4))
                link(V.tensor_copy(kcp2[HD:P, :, 0:nv], k4))
                link(V.tensor_copy(vcp[0:nv, :, :].rearrange("p g d -> p (g d)"), bank[5][0:nv, 0:256]), "kve")
            else:
                if c >= 3:
                    dve.wait_ge(S("cs_mm"), c - 2)
                link(V.tensor_copy(kc[:, c % 2, 0:NKV * nv], bank[4][0:HD, 0:NKV * nv]))
                link(V.tensor_copy(vcmp[0:nv, c - 1, :], bank[5][0:nv, 0:256]), "kve")

        def compress_act(act, link, f, c):
            ns = TP // CST if c == 0 else NSEG
            nv, W = ns - 1, NKV * ns
            for i in range(8):
                act.wait_ge(S("ct"), 2 * (8 * c + i) + 1)
                if c or i:
                    act.wait_ge(S("cm"), 2 * (8 * c + i) - 1)
                for r in range(4):
                    link(f(*spread(0, r, ns), ACT.Copy), "xe0" if r == 3 else None)
            for kd in range(2):
                act.wait_ge(S("cm"), 16 * c + 15 + kd)
                if c:
                    act.wait_ge(S("hs"), 2 * c)
                link(f(hb[:, kd, 0:W], bank[2 + kd][HD:P, 0:W], ACT.Copy), "hb")
            for kd in range(2):
                act.wait_ge(S("hs"), 2 * c + kd + 1)
                o = hs[:, kd, 0:NKV * nv]
                link(f(o, o, ACT.Gelu_apprx_tanh, bias=hconst[:, kd:kd + 1]), "ge" if kd else None)

        def layer_b_dve(dve, link, V, norm):
            norm(3, xT[:, :, :], NT, uT[:, :, :], MIX1)
            dve.wait_ge(S("ma_o"), 8)
            link(V.tensor_tensor(mem_u_b, memT[:, :, :], bc(gain[:, MEM1 * KT:MEM1 * KT + KT], 2, NMEM), ALU.mult), "mem_u")
            mem_project_dve(dve, link, V, 1)
            for t in range(6):
                dve.wait_ge(*done("bq_mm", t + 1))
                link(V.tensor_scalar(qT[:, t, :], bank[t % 2][:, 0:NT], HD ** -0.5, None, ALU.mult), "bq_ev")
            for n in range(9):
                c, i = n // 3, n % 3
                dve.wait_ge(*done("bkv_mm", n + 1))
                dst = kvP[:, i, 2 * c:2 * c + 2, :] if i < 2 else kvS[:, 2 * c:2 * c + 2, :]
                src = bank[2 + i][0:(P if i < 2 else TS), :].rearrange("p (a d) -> p a d", a=2)
                link(V.tensor_copy(dst, src), "bkv_ev")
            dve.wait_ge(*done("bg_mm", 1))
            dve.wait_ge(S("ld_gbb"), 32)
            for i in range(2):
                link(V.tensor_tensor(gp[:, i, :], bank[2 + i][:, 0:36], gbp, ALU.add))
            link(V.tensor_tensor(g12, bank[4][0:NQ, 0:3 * TS].rearrange("p (c b) -> p c b", c=3), bc(gb12, 2, TS), ALU.add), "bg_ev")
            dve.wait_ge(*done("bg_mm", 3))
            link(V.tensor_scalar(xq[:, 0, :], bank[5][:, 0:NT], HD ** -0.5, None, ALU.mult))
            link(V.tensor_scalar(xq[:, 1, :], bank[6][:, 0:NT], HD ** -0.5, None, ALU.mult))
            for n in range(8):
                dve.wait_ge(*done("kd_mm", n + 1))
                link(V.tensor_copy(kdup[0:HD, n // 4, n % 4, :], bank[n % 2][0:HD, 0:TP]))
                link(V.tensor_copy(kdup[HD:P, n // 4, n % 4, :], bank[n % 2][0:HD, 0:TP]), "kd_ev")
            dve.wait_ge(*done("kn_mm", 1))
            link(V.tensor_copy(knT.rearrange("p a g b -> p (a g b)"), bank[2][0:HD, 0:64]), "kn_ev")
            dve.wait_ge(*done("kn_mm", 2))
            link(V.tensor_copy(pec.rearrange("p a b -> p (a b)"), bank[3][:, 0:32]), "kn_ev")
            dve.wait_ge(*done("kn_mm", 3))
            link(V.tensor_copy(hconst, bank[4][0:HD, 0:2]), "kn_ev")
            link(V.memset(q12, 0.0))
            link(V.memset(qblk, 0.0))
            for h in range(NQ):
                g = h // GRP
                src = qT[64 * (h % 2):64 * (h % 2) + 64, h // 2, TP:NT]
                link(V.tensor_copy(q12[:, :, g, h], src))
                link(V.tensor_copy(qblk[64 * (g % 2):64 * (g % 2) + 64, :, g // 2, h], src), "q12" if h == NQ - 1 else None)
            dve.wait_ge(S("ld_pt"), 128)
            link(V.tensor_scalar(idxb, pages, 256.0, C("seg"), ALU.mult, ALU.add), "idx")
            mem_attend_dve(dve, link, V, 1)
            compress_dve(dve, link, V, 0)

            def score(n):
                h, i = n // 2, n % 2
                nk, b0 = P * (i + 1), 128 + 16 * (n % 2)
                dve.wait_ge(S("p_s"), n + 1)
                if n >= 2:
                    dve.wait_ge(S("p_t"), n - 1)
                link(V.scalar_tensor_tensor(sc[:, n % 2, :, 0:nk], bc(dist[:, i, 0:nk], 1, 2), -SLOPES[h],
                                            bank[n % 2][:, :].rearrange("p (a k) -> p a k", a=2)[:, :, 0:nk], ALU.mult, ALU.add))
                link(V.scalar_tensor_tensor(scc[:, n % 2, 0:15], distc[:, i, 0:15], -SLOPES[h],
                                            bank[(2, 5)[n % 2]][:, 0:15], ALU.mult, ALU.add), "ps")
                link(V.tensor_reduce(small[:, b0 + 1:b0 + 3], sc[:, n % 2, :, 0:nk], AX.X, ALU.max, negate=True))
                link(V.tensor_reduce(small[:, b0:b0 + 1], scc[:, n % 2, 0:15], AX.X, ALU.max, negate=True), "p_mx")

            def weigh(n):
                h, i = n // 2, n % 2
                nk, b0 = P * (i + 1), 128 + 16 * (n % 2)
                dve.wait_ge(S("p_e"), n + 1)
                s3 = small[:, b0 + 3:b0 + 6]
                link(V.tensor_tensor(scc[:, n % 2, 0:15], scc[:, n % 2, 0:15], maskc[:, i, 0:15], ALU.mult))
                link(V.tensor_reduce(small[:, b0 + 3:b0 + 4], scc[:, n % 2, 0:15], AX.X, ALU.add))
                link(V.tensor_scalar(s3, s3, 1e-30, None, ALU.max))
                link(V.reciprocal(s3, s3))
                link(V.tensor_tensor(s3, s3, gp[:, i, h:36:NQ], ALU.mult))
                link(V.tensor_scalar(scc[:, n % 2, 0:15], scc[:, n % 2, 0:15], s3[:, 0:1], None, ALU.mult))
                for br in range(2):
                    s_ = sc[:, n % 2, br, 0:nk]
                    link(V.tensor_scalar(s_, s_, s3[:, 1 + br:2 + br], None, ALU.mult), "p_p" if br else None)

            def out(n):
                h, i = n // 2, n % 2
                dve.wait_ge(S("p_o"), n + 1)
                link(V.tensor_copy(oP[:, i, HD * h:HD * h + HD], bank[6 + n % 2][:, 0:HD]), "p_oe")

            dve.wait_ge(*done("gates", 2))
            score(0)
            for n in range(2 * NQ):
                if n + 1 < 2 * NQ:
                    score(n + 1)
                weigh(n)
                if n:
                    out(n - 1)
            out(2 * NQ - 1)
            for j in range(6):
                dve.wait_ge(*done("om_mm", j + 1))
                link(V.tensor_copy(mixT[:, j, 0:TP], bank[j % 2][:, 0:TP]), "om_ev")

            for c in range(1, TS + 1):
                compress_dve(dve, link, V, c)
            dve.wait_ge(S("cs_mm"), TS)
            dve.wait_ge(S("ld_d12"), 32)
            for i in range(2):
                link(V.scalar_tensor_tensor(pc[:, 4 * i:4 * i + 4, 0:NCMP], bc(d12b[:, 0:NCMP], 1, 4), nsl[0:NQ, :],
                                            bank[6 + i][0:NQ, 0:4 * NCMP].rearrange("p (b n) -> p b n", b=4), ALU.mult, ALU.add))
            mx, p_ = small[0:NQ, 160:168], pc[:, :, 0:NCMP]
            link(V.tensor_reduce(mx, p_, AX.X, ALU.max))
            link(V.tensor_tensor(p_, p_, bc(mx, 2, NCMP), ALU.subtract), "pc_d")
            dve.wait_ge(*done("pc_e"))
            link(V.tensor_reduce(mx, p_, AX.X, ALU.add))
            link(V.reciprocal(mx, mx))
            link(V.tensor_tensor(p_, p_, bc(mx, 2, NCMP), ALU.mult), "pc_p")
            dve.wait_ge(*done("im"))
            link(V.tensor_tensor(p_, p_, bc(g12[:, 0, :], 2, NCMP), ALU.mult), "pc_s")
            for i in range(2):
                link(V.tensor_copy(psum4[:, 4 * i:4 * i + 4, 0:NCMP],
                                   bank[i][0:NKV, 0:4 * NCMP].rearrange("p (b n) -> p b n", b=4)))
            link(V.memset(imp, 1e9))
            mid = imp[:, :, 1:31]
            link(V.tensor_reduce(mid, psum4[:, :, 3:123].rearrange("p b (j w) -> p b j w", w=4), AX.X, ALU.add))
            link(V.tensor_tensor(mid, mid, psum4[:, :, 7:127].rearrange("p b (j w) -> p b j w", w=4)[:, :, :, 0], ALU.add), "imp")
            dve.wait_ge(*done("pct"))
            link(V.tensor_copy(pcT[0:NCMP, :, :].rearrange("p b h -> p (b h)"), bank[2][0:NCMP, 0:TS * NQ]), "pct_ev")
            dve.wait_ge(S("ld_imp"), 16)
            other, own = bc(imp32, 1, 33), bc(imp32, 2, 33)
            link(V.tensor_tensor(rank, other, own, ALU.is_gt))
            link(V.tensor_tensor(rank2, other, own, ALU.is_equal))
            link(V.tensor_tensor(rank2, rank2, lower[0:32, :].rearrange("p (a b) -> p a b", a=33), ALU.mult))
            link(V.tensor_tensor(rank, rank, rank2, ALU.add))
            link(V.tensor_reduce(sel32, rank, AX.X, ALU.add))
            link(V.tensor_scalar(sel32, sel32, float(NSEL), -FAR, ALU.is_ge, ALU.mult), "sel")
            dve.wait_ge(*done("oc_mm"))
            link(V.tensor_copy(oc.rearrange("p b j c -> p (b j c)"), bank[3][:, 0:TS * NQ]), "oc_ev")
            link(V.memset(pz, 0.0), "pz0")

            dve.wait_ge(S("ld_sel"), 64)
            for b in range(TS):
                if b:
                    dve.wait_ge(S("pt_mm"), b)
                for c in range(5):
                    dve.wait_ge(S("k_s"), 5 * b + c + 1)
                    a = 512 * c + (c == 4)
                    d_ = d12s[:, 512 * c:512 * c + 512] if c < 4 else d12b[:, NCMP + 1:NCMP + 513]
                    link(V.scalar_tensor_tensor(s12[:, a:a + 512], d_, nsl[0:NQ, :], bank[2 + c][0:NQ, :], ALU.mult, ALU.add), "s_ev")
                dve.wait_ge(S("k_n"), b + 1)
                link(V.tensor_copy(s12[:, PAST:PAST + 1], bank[7][0:NQ, 0:1]))
                link(V.tensor_copy(s12[:, PAST + 513:PAST + 514], bank[7][0:NQ, 1:2]), "s_n")
                v = s12[:, 0:PAST].rearrange("p (l j w) -> p l j w", l=CST, w=4)
                link(V.tensor_tensor(v, v, bc(bc(sel12[:, b, 0:NBLK], 1, CST), 3, 4), ALU.add))
                st = small[0:NQ, 176:184]
                br_ = (s12[:, 0:PAST + 1], s12[:, PAST + 1:PAST + 514])
                for r in range(2):
                    link(V.tensor_reduce(st[:, r:r + 1], br_[r], AX.X, ALU.max, negate=True), "s_mx" if r else None)
                dve.wait_ge(S("s_e"), b + 1)
                link(V.reciprocal(st[:, 2:4], st[:, 2:4]))
                link(V.tensor_tensor(st[:, 2:4], st[:, 2:4], g12[:, 1:3, b], ALU.mult))
                for r in range(2):
                    link(V.tensor_scalar(br_[r], br_[r], st[:, 2 + r:3 + r], None, ALU.mult))
                link(V.tensor_copy(pz[:, 0, b, b:b + 1], s12[:, PAST:PAST + 1]))
                link(V.tensor_copy(pz[:, 1, b, b:b + 1], s12[:, PAST + 513:PAST + 514]), "p12")
                dve.wait_ge(S("pt_mm"), b + 1)
                if b >= 2:
                    dve.wait_ge(S("pv_mm"), b - 1)
                link(V.tensor_copy(pTs[:, b % 2, 0:240], bank[7][:, 8:248]))
                link(V.tensor_copy(pTs[0:TS, b % 2, 240:264], bank[7][0:TS, 248:272]), "pt_ev")
            dve.wait_ge(S("pv_mm"), TS)
            link(V.tensor_tensor(oTsb.rearrange("p b j c -> p (b j c)"), bank[7][:, 272:368], oc.rearrange("p b j c -> p (b j c)"), ALU.add))
            for h in range(NQ):
                g = h // GRP
                link(V.tensor_copy(mixT[64 * (h % 2):64 * (h % 2) + 64, h // 2, TP:NT],
                                   oTsb[64 * (g % 2):64 * (g % 2) + 64, :, g // 2, h - 6 * (g // 2)]), "mixT" if h == NQ - 1 else None)
            for m_ in range(KT):
                dve.wait_ge(*done("wob_mm", m_ + 1))
                link(V.tensor_tensor(xT[:, m_, :], xT[:, m_, :], bank[m_ % 2][:, 0:NT], ALU.add), "wob_ev")
            norm(4, xT[:, :, :], NT, uT[:, :, :], FFN1)

            L_, E_, Cb = lg[:, :, 0, :], lg[:, :, 1, :], lg[:, :, 2, :]
            link(V.memset(lg, 0.0))
            dve.wait_ge(*done("rt"))
            link(V.tensor_copy(L_[:, 0:2, :], bank[2][:, 0:2 * NE].rearrange("p (i e) -> p i e", i=2)))
            link(V.tensor_copy(L_[0:TS, 2, :], bank[2][0:TS, 2 * NE:3 * NE]))
            st = small[:, 192:195]
            link(V.tensor_reduce(st, L_, AX.X, ALU.max))
            link(V.tensor_tensor(E_, L_, bc(st, 2, NE), ALU.subtract), "rt_d")
            other, own = bc(L_, 2, NE), bc(L_, 3, NE)
            low8 = lower[:, :].rearrange("p (a b) -> p a b", a=33)[:, 0:NE, 0:NE]
            link(V.tensor_tensor(rk, other, own, ALU.is_gt))
            link(V.tensor_tensor(rk2, other, own, ALU.is_equal))
            link(V.tensor_tensor(rk2, rk2, bc(low8, 1, 3), ALU.mult))
            link(V.tensor_tensor(rk, rk, rk2, ALU.add))
            link(V.tensor_reduce(l8, rk, AX.X, ALU.add))
            link(V.tensor_scalar(l8, l8, 2.0, None, ALU.is_lt))
            dve.wait_ge(*done("rt_e"))
            link(V.tensor_tensor(E_, E_, l8, ALU.mult))
            link(V.tensor_reduce(st, E_, AX.X, ALU.add))
            link(V.reciprocal(st, st))
            link(V.tensor_tensor(Cb, E_, bc(st, 2, NE), ALU.mult), "cb")
            dve.wait_ge(*done("cbt"))
            link(V.tensor_copy(combT, bank[3][0:NE, 0:NT]), "cbt_ev")
            for e in range(NE):
                dve.wait_ge(*done("cbb", e + 1))
                link(V.tensor_copy(comb[:, e, :], bank[e % 2][:, 0:NT]), "cbb_ev")

            link(V.memset(ytmp[:, 0, 0:1], 0.0), "m_y")
            link(V.memset(ytmp[:, 1, 0:1], 0.0), "m_h")
            with dve.Fori(0, NE) as e:
                for j in range(EFF // P):
                    dve.wait_ge(S("m_si"), e * (EFF // P) + (j + 1))
                    V.tensor_tensor(hff[:, j, :], silu[:, j % 2, :], bank[2 * (j % 2) + 1][:, 0:NT], ALU.mult).then_inc(S("m_h"), 1)
                for m_ in range(KT):
                    dve.wait_ge(S("m_d"), e * KT + (m_ + 1))
                    dve.wait_ge(S("m_y"), e * KT + (m_ + 1))
                    V.tensor_tensor(ytmp[:, 0, :], bank[4 + m_ % 4][:, 0:NT], comb[:, e, :], ALU.mult).then_inc(S("m_yt"), 1)
                    dve.wait_ge(S("m_yt"), e * KT + (m_ + 1))
                    V.tensor_tensor(xT[:, m_, :], xT[:, m_, :], ytmp[:, 0, :], ALU.add).then_inc(S("m_y"), 1)
            dve.wait_ge(S("m_y"), NE * KT + 1)
            norm(5, xT[:, :, :], NT, uT[:, :, :], FINAL)
            for n in range(2 * KT + 2):
                i, k = (n // 8, n % 8) if n < 16 else (2, n - 16)
                dve.wait_ge(*done("y_mm", n + 1))
                if i < 2:
                    link(V.tensor_copy(ysb[:, i, P * k:P * k + P], bank[n % 4][:, 0:P]), "y_ev")
                else:
                    link(V.tensor_copy(ysb[0:TS, 2, 512 * k:512 * k + 512], bank[n % 4][0:TS, :]), "y_ev")

        def layer_b_act(act, link, f, root):
            root(3, NT)
            act.wait_ge(S("bg_ev"), 1)
            link(f(gp, gp, ACT.Sigmoid), "gates")
            link(f(g12, g12, ACT.Sigmoid), "gates")
            mem_attend_act(act, link, f, 1)
            compress_act(act, link, f, 0)

            def expo(n):
                i = n % 2
                nk, b0 = P * (i + 1), 128 + 16 * (n % 2)
                act.wait_ge(S("p_mx"), n + 1)
                link(f(scc[:, n % 2, 0:15], scc[:, n % 2, 0:15], ACT.Exp, bias=small[:, b0:b0 + 1],
                       accum_out=small[:, b0 + 3:b0 + 4]))
                for br in range(2):
                    s_ = sc[:, n % 2, br, 0:nk]
                    link(f(s_, s_, ACT.Exp, bias=small[:, b0 + 1 + br:b0 + 2 + br], accum_out=small[:, b0 + 4 + br:b0 + 5 + br]),
                         "p_e" if br else None)

            def turned(n):
                nk = P * (n % 2 + 1)
                act.wait_ge(S("p_t"), n + 1)
                if n >= 2:
                    act.wait_ge(S("p_o"), n - 1)
                link(f(pT[:, n % 2, :, :].rearrange("p (a t) n -> p a (t n)", a=2)[:, :, 0:nk],
                       bank[3 + n % 2][:, :].rearrange("p (a k) -> p a k", a=2)[:, :, 0:nk], ACT.Copy))
                link(f(pcpT[0:15, n % 2, :], bank[6 + n % 2][0:15, P:2 * P], ACT.Copy), "p_te")

            expo(0)
            for n in range(2 * NQ):
                if n + 1 < 2 * NQ:
                    expo(n + 1)
                turned(n)
            for c in range(1, TS + 1):
                compress_act(act, link, f, c)
            act.wait_ge(*done("pc_d"))
            link(f(pc[:, :, 0:NCMP], pc[:, :, 0:NCMP], ACT.Exp), "pc_e")

            def keys(b):
                for n in range(5 * b, 5 * b + 5):
                    for j in range(2):
                        act.wait_ge(S("kt_t"), 2 * n + j + 1)
                        if n:
                            act.wait_ge(S("k_s"), n)
                        link(f(kTb[:, j, :], bank[j][:, :], ACT.Copy), "kt_e")

            keys(0)
            for b in range(TS):
                act.wait_ge(S("s_mx"), b + 1)
                st = small[0:NQ, 176:184]
                for r, (a, z) in enumerate(((0, PAST + 1), (PAST + 1, PAST + 514))):
                    link(f(s12[:, a:z], s12[:, a:z], ACT.Exp, bias=st[:, r:r + 1], accum_out=st[:, 2 + r:3 + r]),
                         "s_e" if r else None)
                if b + 1 < TS:
                    keys(b + 1)
            root(4, NT)
            act.wait_ge(*done("rt_d"))
            link(f(lg[:, :, 1, :], lg[:, :, 1, :], ACT.Exp), "rt_e")
            with act.Fori(0, NE) as e:
                for j in range(EFF // P):
                    act.wait_ge(S("m_gu"), e * (EFF // P) + (j + 1))
                    act.wait_ge(S("m_h"), e * (EFF // P) + max(j, 1))
                    f(silu[:, j % 2, :], bank[2 * (j % 2)][:, 0:NT], ACT.Silu).then_inc(S("m_si"), 1)
            root(5, NT)

        def layer_b_pool(pool, load, store):
            pool.wait_ge(S("ff_y"), KT)
            load("ld_gbb", gbp, I["b_gate_b"].broadcast_to((P, 36)))
            load("ld_gbb", gb12, I["b_gate_b"][0].rearrange("(c h) -> h c", c=3), allow_slow_non_contiguous=True)
            for c in range(2):
                for a in range(2):
                    load("ld_w1", w1[:, c, :, a, :], I["w_cmp1"][0, c].rearrange("(a i p) e -> a p i e", a=2, p=P)[a])
            load("ld_w1", perow, I["pe_cmp"][0].rearrange("c (i a) d -> (c i) (a d)", a=2))
            load("ld_w1", w2, I["w_cmp2"][0].rearrange("c e d -> e c d"))
            for s in range(8):
                load("ld_pt", pages[s:P:8, :], I["page_table"].rearrange("b n -> n b"), allow_slow_non_contiguous=True)
            pool.wait_ge(S("mem_u"), 2)
            load("ld_d12", d12s, I["dist12"][:, 0:PAST])
            mem_store(pool, store, 1)
            pool.wait_ge(S("mkv_mm"), 4)
            mem_load(pool, load, 1)
            pool.wait_ge(*done("bkv_ev", 9))
            for i in range(2):
                store(O["rows_p"][0, 0, P * i:P * i + P].rearrange("t k g d -> t (k g d)"),
                      kvP[:, i, 0:4, :].rearrange("p k d -> p (k d)"), "st_rows")
            for i in range(2):
                store(O["win_p"][0, 0, P * i:P * i + P].rearrange("t k g d -> t (k g d)"),
                      kvP[:, i, 4:6, :].rearrange("p k d -> p (k d)"), "st_win")
            store(O["rows_s"][0, :, 0].rearrange("b k g d -> b (k g d)"), kvS[:, 0:4, :].rearrange("p k d -> p (k d)"), "st_win")
            store(O["win_s"][0, :, WBUF - 1].rearrange("b k g d -> b (k g d)"), kvS[:, 4:6, :].rearrange("p k d -> p (k d)"), "st_win")
            pool.wait_ge(S("st_rows"), 32)
            pool.wait_ge(*done("mixm1"))
            segs = O["rows_p"][0, 0].rearrange("(s l) k g d -> s l (k g d)", l=CST)
            for half in range(2):
                load(f"ld_c{half}", gat[0:TP // CST, half, :, :], segs[:, 8 * half:8 * half + 8, 0:512])
            pool.wait_ge(S("st_mem"), 128)
            load("ld_d12", d12b, I["dist12"][:, PAST:PAST + NSEG + WBUF])

            rows = I["cache_nsa"][0].rearrange("a r (u k) g d -> (a r u) (k g d)", u=2)

            def gather(dst, b, l, kinds, name):
                pool.indirect_dma_start(dst, None, rows, bass.IndirectOffsetOnAxis(ap=idxb[:, b:b + 1], axis=0),
                                        element_offset=(2 * l + kinds) * 512).then_inc(S(name), 16)

            pool.wait_ge(*done("idx"))
            pool.wait_ge(S("p_oe"), 2 * NQ)
            for c in range(1, TS + 1):
                for half in range(2):
                    pool.wait_ge(S("ct"), 16 * (c - 1) + 8 * half + 8)
                    for l in range(8):
                        gather(gat[:, half, l, :], c - 1, 8 * half + l, 0, f"ld_c{half}")
            pool.wait_ge(*done("imp"))
            store(scr_imp, imp.rearrange("p b j -> p (b j)"), "st_imp")
            pool.wait_ge(S("st_imp"), 16)
            load("ld_imp", imp32, scr_imp.rearrange("g (b j) -> (g b) j", b=TS))
            pool.wait_ge(*done("sel"))
            store(scr_sel.rearrange("g (b j) -> (g b) j", b=TS), sel32, "st_sel")
            pool.wait_ge(S("st_sel"), 16)
            for g in range(NKV):
                load("ld_sel", sel12[GRP * g:GRP * g + GRP, :, :].rearrange("p b j -> p (b j)"),
                     scr_sel[g:g + 1, :].broadcast_to((GRP, TS * 33)))
            pool.wait_ge(*done("oc_ev"))
            pool.wait_ge(S("st_win"), 64)

            def window(b):
                pool.wait_ge(S("pv_mm"), b) if b else None
                load("ld_win", winb, I["cache_nsa_win"][0, b].rearrange("(p r) k g d -> p r (k g d)", r=4))

            for b in range(TS):
                if b >= 2:
                    window(b - 1)
                for l in range(CST):
                    gather(gsl[:, b % 2, l, :], b, l, 1, f"ld_g{b % 2}")
                if b == 0:
                    window(0)
            window(TS - 1)
            pool.wait_ge(*done("wob_ev", KT))
            load("ld_wr", wr, I["w_router"][0].rearrange("(k p) e -> p k e", p=P))
            for i in range(2):
                pool.wait_ge(*done("y_ev", KT * (i + 1)))
                store(O["y_prompt"][0, P * i:P * i + P], ysb[:, i, :], "st_y")
            pool.wait_ge(*done("y_ev", 2 * KT + 2))
            store(O["y_sample"][:, 0], ysb[0:TS, 2, :], "st_y")

        def moe_load(sp):
            def read(i, e):
                if i < GU:
                    sp.wait_ge(S("m_gu"), e * (EFF // P) + 2 * (i + 1))
                else:
                    sp.wait_ge(S("m_d"), e * KT + 2 * (i - GU + 1))

            def load(i, e):
                s, _ = ring_at.expert[i]
                if i < GU:
                    w = I["w_moe_gu"][0, e].rearrange("(k p) c -> p k c", p=P)
                    for u in range(2):
                        a = EFF * u + 256 * i
                        sp.dma_start(ring[:, s, 2048 * u:2048 * u + 2048].rearrange("p (k c) -> p k c", c=256),
                                     w[:, :, a:a + 256]).then_inc(S(f"w_in{s}"), 16)
                else:
                    w = I["w_moe_d"][0, e].rearrange("(k p) c -> p k c", p=P)
                    a = 256 * (i - GU)
                    sp.dma_start(ring[:, s, 0:EFF // P * 256].rearrange("p (k c) -> p k c", c=256),
                                 w[:, :, a:a + 256]).then_inc(S(f"w_in{s}"), 16)

            n = GU + DN
            last = {i: max(j for j in range(n) if j % RING == i) for i in range(RING)}
            assert all((ring_at.expert[i][0] == ring_at.expert[last[i]][0]) for i in range(RING))
            for i in range(RING):
                sem, value = chunks[len(chunks) - RING + i][1]
                sp.wait_ge(*done(sem, value))
                load(i, 0)
            with sp.Fori(0, NE - 1) as e:
                for i in range(RING, n):
                    read(i - RING, e)
                    load(i, e)
                for i in range(RING):
                    read(last[i], e)
                    load(i, e + 1)
            for i in range(RING, n):
                read(i - RING, NE - 1)
                load(i, NE - 1)

        @block.sync
        def _(sp):
            sp.dma_start(consts[:, :], I["consts"]).then_inc(S("ld_const"), 16)
            sp.dma_start(xin, I["x_prompt"][0].rearrange("(i p) d -> p i d", p=P)).then_inc(S("ld_x"), 16)
            sp.dma_start(xsin, I["x_sample"].rearrange("b t d -> (b t) d")).then_inc(S("ld_x"), 16)
            sp.dma_start(min_, I["mem_prompt"][0].rearrange("(i p) d -> p i d", p=P)).then_inc(S("ld_mem"), 16)
            for row, name in ((0, "norm_mix"), (16, "norm_mem"), (32, "norm_ffn")):
                sp.dma_start(grow[row:row + 16, :], I[name].rearrange("a (k p) -> (a k) p", p=P)).then_inc(S("ld_rows"), 16)
            sp.dma_start(grow[48:56, :], I["norm_final"].rearrange("(k p) -> k p", p=P)).then_inc(S("ld_rows"), 16)
            sp.dma_start(cwrow, I["conv_a"][0].rearrange("j (t d) -> (j t) d", d=MD)).then_inc(S("ld_rows"), 16)
            sp.dma_start(hgrow, I["head_norm_a"][0].rearrange("(t d) -> t d", d=MD)).then_inc(S("ld_rows"), 16)

            def load(n):
                name, _, dmas = chunks[n]
                s, _ = ring_at.at[name]
                if n >= RING:
                    sem, value = chunks[n - RING][1]
                    sp.wait_ge(*done(sem, value))
                for off, parts, dims, src in dmas:
                    k = int(np.prod(dims))
                    sp.dma_start(ring[0:parts, s, off:off + k].rearrange("p (k c) -> p k c", k=dims[0]), src)\
                      .then_inc(S(f"w_in{s}"), 16)

            for n in range(len(chunks)):
                load(n)
            moe_load(sp)
            

        @block.tensor
        def _(pe):
            def got(name):
                s, loaded = ring_at.at[name]
                pe.wait_ge(S(f"w_in{s}"), loaded)
                return slot_view(name)

            def mm(out, lhsT, rhs, first=True, last=True, **kw_):
                return nc.tensor.matmul(out, lhsT, rhs, start=first, stop=last, **kw_)

            def tr(out, in_, n):
                return nc.tensor.transpose(out, in_, ident[0:n, 0:n])

            def norm(n, width):
                pe.wait_ge(S("nrm_sq"), n + 1)
                for k in range(KT):
                    m = mm(bank[7][:, 0:width], ones, sq[:, k, 0:width], k == 0, k == KT - 1)
                m.then_inc(S("nrm_mm"), 1)

            pe.wait_ge(S("ld_const"), 16)
            pe.wait_ge(S("ld_x"), 32)
            for k in range(KT):
                if k >= 4:
                    pe.wait_ge(*done("set_ev", k - 3))
                cols = slice(k * P, k * P + P)
                b = bank[k % 4]
                tr(b[:, 0:P], xin[:, 0, cols], P)
                tr(b[:, P:2 * P], xin[:, 1, cols], P)
                tr(b[:, TP:NT], xsin[:, cols], TS).then_inc(S("set_mm"), 1)
            pe.wait_ge(S("ld_mem"), 16)
            for k in range(KT):
                pe.wait_ge(*done("set_ev", k + 5))
                b = bank[k % 4]
                cols = slice(k * P, k * P + P)
                tr(b[:, 0:P], min_[:, 0, cols], P)
                tr(b[:, P:2 * P], min_[:, 1, cols], P).then_inc(S("set_mm"), 1)
            pe.wait_ge(S("ld_rows"), 96)
            tr(bank[4][:, 0:56], grow, 56)
            tr(bank[4][0:MD, 64:128], cwrow, 64)
            tr(bank[4][0:MD, 128:136], hgrow, MH).then_inc(S("set_mm"), 1)

            norm(0, NMEM)
            norm(1, NT)
            pe.wait_ge(S("mem_u"), 1)
            mem_project(pe, mm, tr, got, 0)

            pe.wait_ge(S("nrm_out"), 2)
            for t in range(16):
                if t % 4 == 0:
                    w = got(("q0", "q1", "k0", "k1")[t // 4])
                if t >= 2:
                    pe.wait_ge(*done("qk_ev", t - 1))
                c0 = (t % 4) * MD
                for k in range(KT):
                    m = mm(bank[t % 2][0:MD, 0:NT], w[:, k, c0:c0 + MD], uT[:, k, :], k == 0, k == KT - 1)
                m.then_inc(S("qk_mm"), 1)
            for c in range(2):
                w = got(f"v{c}")
                for i in range(3):
                    n = 3 * c + i
                    if n >= 3:
                        pe.wait_ge(*done("v_ev", n - 2))
                    toks = slice(P * i, min(P * i + P, NT))
                    for k in range(KT):
                        m = mm(bank[2 + i][0:toks.stop - toks.start, 0:384], uT[:, k, toks], w[:, k, :], k == 0, k == KT - 1)
                    m.then_inc(S("v_mm"), 1)
            for t in range(MH):
                if t % 4 == 0:
                    w = got(f"o{t // 4}")
                if t < 2:
                    pe.wait_ge(*done("qk_ev", 15 + t))
                else:
                    pe.wait_ge(*done("o_ev", t - 1))
                c0 = (t % 4) * MD
                for k in range(KT):
                    m = mm(bank[t % 2][0:MD, 0:NT], w[:, k, c0:c0 + MD], uT[:, k, :], k == 0, k == KT - 1)
                m.then_inc(S("o_mm"), 1)
            w = got("gxa")
            pe.wait_ge(*done("v_ev", 6))
            pe.wait_ge(S("mkv_ev"), 2)
            for k in range(KT):
                mm(bank[2][0:MH, 0:TP], w[:, k, 0:MH], uT[:, k, 0:TP], k == 0, k == KT - 1)
            for k in range(KT):
                mm(bank[3][0:MH, 0:TP], w[:, k, MH:2 * MH], uT[:, k, 0:TP], k == 0, k == KT - 1)
            for k in range(KT):
                m = mm(bank[4][0:TS, 0:2 * MH], uT[:, k, TP:NT], w[:, k, 0:2 * MH], k == 0, k == KT - 1)
            m.then_inc(S("g_mm"), 1)
            for j in range(2):
                for k in range(KT):
                    m = mm(bank[5 + j][:, 0:NT], w[:, k, 16 + P * j:16 + P * j + P], uT[:, k, :], k == 0, k == KT - 1)
                m.then_inc(S("g_mm"), 1)

            pe.wait_ge(S("ld_conv"), 16)
            pe.wait_ge(*done("o_ev", 8))
            for t in range(16):
                m = tr(bank[0][0:MD, 24 * t:24 * t + 24], cvh[:, MD * t:MD * t + MD], 24)
            m.then_inc(S("cvh_mm"), 1)
            pe.wait_ge(S("g_ev"), 1)
            pe.wait_ge(*done("qk_ev", 16))
            for c in range(4):
                if c:
                    pe.wait_ge(*done("cvo_ev", c))
                for t in range(4 * c, 4 * c + 4):
                    tr(bank[2][0:3, MD * (t % 4):MD * (t % 4) + MD], preP[:, t, TP:TP + 3], MD)
                    m = tr(bank[3][0:TS, MD * (t % 4):MD * (t % 4) + MD], preS[:, t, :, CW - 1], MD)
                m.then_inc(S("cvo_mm"), 1)

            pe.wait_ge(S("gate_x"), 2)
            pe.wait_ge(*done("cvo_ev", 4))
            for i in range(2):
                tr(bank[4][:, 16 * i:16 * i + MH], ab[:, 4, P * i:P * i + P], MH)
                m = tr(bank[4][:, 16 * i + MH:16 * i + 16], ab[:, 7, P * i:P * i + P], MH)
            m.then_inc(S("bT_mm"), 1)
            pe.wait_ge(*done("qk_done"))
            pe.wait_ge(S("g_ev"), 2)
            for h in range(MH):
                q, k_ = qk[:, h, :], qk[:, MH + h, :]
                if h:
                    pe.wait_ge(S("dec"), h)
                mm(bank[0][:, 0:TP], k_[:, 0:P], q[:, 0:TP])
                mm(bank[0][:, TP:384], k_[:, P:TP], q[:, P:TP])
                mm(bank[1][:, 0:TP], sel8[0:MH, h, :], ab[:, 5, :]).then_inc(S("sc_mm"), 1)
                if h:
                    pe.wait_ge(S("kw_ev"), h)
                tr(bank[5][:, 0:MD], k_[:, 0:P], MD)
                tr(bank[5][:, MD:2 * MD], k_[:, P:TP], MD).then_inc(S("kt_mm"), 1)
                if h:
                    pe.wait_ge(S("hp"), h)
                mm(bank[2][0:MD, 0:TP], sel8[0:MH, h, 0:MD], ab[:, 6, :])
                pe.wait_ge(S("sw"), h + 1)
                s_, v0, v1 = sw[:, h % 2, :], vp[:, 0, h * MD:h * MD + MD], vp[:, 1, h * MD:h * MD + MD]
                mm(bank[3][0:MD, 0:TP], v0, s_[:, 0:TP], True, False)
                mm(bank[3][0:MD, P:TP], v1, s_[:, TP:384], False, True)
                mm(bank[4][0:MD, 0:TP], ones[:, 0:MD], s_[:, 0:TP], True, False)
                mm(bank[4][0:MD, P:TP], ones[:, 0:MD], s_[:, TP:384], False, True).then_inc(S("nd_mm"), 1)
                pe.wait_ge(S("kw_ev"), h + 1)
                if h:
                    pe.wait_ge(S("c_ev"), h)
                mm(bank[6][0:MD, 0:MD], v0, kw[:, h % 2, 0, :], True, False)
                mm(bank[6][0:MD, 0:MD], v1, kw[:, h % 2, 1, :], False, True)
                mm(bank[6][0:1, P:P + MD], ones[:, 0:1], kw[:, h % 2, 0, :], True, False)
                mm(bank[6][0:1, P:P + MD], ones[:, 0:1], kw[:, h % 2, 1, :], False, True).then_inc(S("c_mm"), 1)

            pe.wait_ge(S("c_ev"), 8)
            pe.wait_ge(S("hp"), 8)
            for t in range(16):
                m = tr(bank[t // 4][0:TS, (t % 4) * MD:(t % 4) * MD + MD], qk[:, t, TP:NT], MD)
            m.then_inc(S("qks_mm"), 1)
            pe.wait_ge(*done("bd"))
            mm(bank[4][0:MD, 0:P], ones[0:TS, 0:MD], bdg.rearrange("p a b c -> p (a b c)")).then_inc(S("gb_mm"), 1)
            for n in range(2 * MH):
                h, half = n // 2, n % 2
                pe.wait_ge(S("kd"), h + 1)
                if n >= 2:
                    pe.wait_ge(S("cup"), n - 1)
                    pe.wait_ge(S("cq"), n - 1)
                mm(bank[n % 2][0:MD, 0:384], vs[:, h * MD:h * MD + MD],
                   kdiag[:, h % 2, 4 * half:4 * half + 4, :]).then_inc(S("op_mm"), 1)
                mm(bank[2 + n % 2][0:MD, 0:384], ones[0:TS, 0:MD],
                   qdiag[:, h % 2, 4 * half:4 * half + 4, :]).then_inc(S("qb_mm"), 1)

            for h in range(MH):
                pe.wait_ge(*done("hsq"))
                if h >= 2:
                    pe.wait_ge(S("hn"), h - 1)
                mm(bank[h % 2][0:MD, 0:NT], ones[0:MD, 0:MD], sq[0:MD, h, :]).then_inc(S("hn_mm"), 1)

            pe.wait_ge(S("hn"), 8)
            mem_attend(pe, mm, tr, 0)

            pe.wait_ge(S("hn"), 8)
            pe.wait_ge(*done("mixm0"))
            for m_ in range(KT):
                if m_ % 2 == 0:
                    wh, wx = got(f"woa{m_ // 2}")
                if m_ >= 2:
                    pe.wait_ge(*done("woa_ev", m_ - 1))
                c0 = (m_ % 2) * P
                for h in range(MH):
                    mm(bank[m_ % 2][:, 0:NT], wh[:, h, c0:c0 + P], hT[:, h, :], h == 0, False)
                for j in range(2):
                    m = mm(bank[m_ % 2][:, 0:NT], wx[:, j, c0:c0 + P], mixm[:, j, :], False, j == 1)
                m.then_inc(S("woa_mm"), 1)

            norm(2, NT)
            pe.wait_ge(S("nrm_out"), 3)
            for j in range(DFF // P):
                if j % 2 == 0:
                    wg, wu = got(f"gu{j // 2}")
                if j >= 2:
                    pe.wait_ge(S("ff_h"), j - 1)
                c0 = (j % 2) * P
                for w, b in ((wg, 2 * (j % 2)), (wu, 2 * (j % 2) + 1)):
                    for k in range(KT):
                        m = mm(bank[b][:, 0:NT], w[:, k, c0:c0 + P], uT[:, k, :], k == 0, k == KT - 1)
                m.then_inc(S("ff_gu"), 1)
            pe.wait_ge(S("ff_h"), DFF // P)
            for m_ in range(KT):
                w = got(f"dn{m_}")
                if m_ >= 2:
                    pe.wait_ge(S("ff_y"), m_ - 1)
                for k in range(DFF // P):
                    m = mm(bank[4 + m_ % 2][:, 0:NT], w[:, k, :], hff[:, k, :], k == 0, k == DFF // P - 1)
                m.then_inc(S("ff_d"), 1)

            layer_b_pe(pe, mm, tr, got, norm)

        @block.vector
        def _(dve):
            link = chain(dve, "dve")
            V = nc.vector

            def norm(n, src, width, dst, g):
                link(V.tensor_tensor(sq[:, :, 0:width], src, src, ALU.mult), "nrm_sq")
                dve.wait_ge(S("nrm_mm"), n + 1)
                link(V.tensor_scalar(rtmp[:, 0:width], bank[7][:, 0:width], 1.0 / D, EPS, ALU.mult, ALU.add))
                link(V.reciprocal(rtmp[:, 0:width], rtmp[:, 0:width]), "nrm_rc")
                dve.wait_ge(S("nrm_rs"), n + 1)
                r = rstd[:, 0:width]
                if g is None:
                    link(V.tensor_tensor(dst, src, bc(r, 1, KT), ALU.mult), "nrm_out")
                    return
                for k in range(KT):
                    ins = V.scalar_tensor_tensor(dst[:, k, :], src[:, k, :], gain[:, g * KT + k:g * KT + k + 1], r,
                                                 ALU.mult, ALU.mult)
                    link(ins, "nrm_out" if k == KT - 1 else None)

            for k in range(KT):
                dve.wait_ge(*done("set_mm", k + 1))
                link(V.tensor_copy(xT[:, k, :], bank[k % 4][:, 0:NT]), "set_ev")
            for k in range(KT):
                dve.wait_ge(*done("set_mm", KT + k + 1))
                link(V.tensor_copy(memT[:, k, :], bank[k % 4][:, 0:NMEM]), "set_ev")
            dve.wait_ge(*done("set_mm", 17))
            link(V.tensor_copy(gain[:, :], bank[4][:, 0:56]))
            link(V.tensor_copy(cw, bank[4][0:MD, 64:128]))
            link(V.tensor_copy(hg, bank[4][0:MD, 128:136]), "set_ev")
            norm(0, memT[:, :, :], NMEM, memT[:, :, :], None)
            link(V.tensor_tensor(mem_u_a, memT[:, :, :], bc(gain[:, MEM0 * KT:MEM0 * KT + KT], 2, NMEM), ALU.mult), "mem_u")
            norm(1, xT[:, :, :], NT, uT[:, :, :], MIX0)
            mem_project_dve(dve, link, V, 0)

            link(V.memset(preP[:, :, 0:3], 0.0), "pre0")
            for t in range(16):
                dve.wait_ge(*done("qk_ev", t + 1))
                o = qk[:, t, 0:TP]
                link(V.tensor_scalar(o, preP[:, t, 0:TP], cw[:, t:t + 1], None, ALU.mult))
                for j in range(1, CW):
                    link(V.scalar_tensor_tensor(o, preP[:, t, j:j + TP], cw[:, 16 * j + t:16 * j + t + 1], o,
                                                ALU.mult, ALU.add), "cv" if j == CW - 1 else None)
            dve.wait_ge(*done("g_mm", 1))
            dve.wait_ge(S("ld_gb"), 48)
            link(V.tensor_scalar(ab[:, 0, :], bank[2][0:MH, 0:TP], gbias_p[:, 0:1], None, ALU.add))
            link(V.tensor_scalar(ab[:, 1, :], bank[3][0:MH, 0:TP], gbias_p[:, 1:2], None, ALU.add))
            gsf = gs.rearrange("p a b -> p (a b)")
            link(V.tensor_tensor(gsf[:, 0:16], bank[4][0:TS, 0:16], gbias_s, ALU.add), "g_ev")
            dve.wait_ge(*done("g_mm", 3))
            link(V.tensor_scalar(xq[:, 0, :], bank[5][:, 0:NT], HD ** -0.5, None, ALU.mult))
            link(V.tensor_scalar(xq[:, 1, :], bank[6][:, 0:NT], HD ** -0.5, None, ALU.mult), "g_ev")
            dve.wait_ge(*done("cvh_mm"))
            link(V.tensor_copy(preS[:, :, :, 0:CW - 1],
                               bank[0][0:MD, 0:384].rearrange("p (t b j) -> p t b j", t=16, b=TS)))
            cwv = cw.rearrange("p (j t) -> p j t", j=CW)
            qs = qk[:, :, TP:NT]
            link(V.tensor_tensor(qs, preS[:, :, :, 0], bc(cwv[:, 0, :], 2, TS), ALU.mult))
            for j in range(1, CW):
                link(V.tensor_tensor(ctmp, preS[:, :, :, j], bc(cwv[:, j, :], 2, TS), ALU.mult))
                link(V.tensor_tensor(qs, qs, ctmp, ALU.add), "cv" if j == CW - 1 else None)
            for c in range(4):
                dve.wait_ge(*done("cvo_mm", c + 1))
                link(V.tensor_copy(cv3[:, 384 * c:384 * c + 384], bank[2][0:3, 0:384]))
                link(V.tensor_copy(cv8[:, 384 * c:384 * c + 384], bank[3][0:TS, 0:384]), "cvo_ev")
            dve.wait_ge(S("qk_si"), 17)
            link(V.tensor_scalar(qk[:, MH:16, :], qk[:, MH:16, :], MD ** -0.5, None, ALU.mult), "qk_done")

            ig, fg, tm, lf = (ab[:, i, :] for i in range(4))
            link(V.scalar_tensor_tensor(tm, fg, -1.0, fg, ALU.mult, ALU.max), "lf_abs")
            dve.wait_ge(S("lf_ln"), 1)
            link(V.scalar_tensor_tensor(lf, fg, 0.0, tm, ALU.min, ALU.subtract))
            F, M, b_, emt, wl, one = (ab[:, i, :] for i in (8, 5, 4, 6, 7, 9))
            link(V.memset(one, 1.0))
            link(V.tensor_tensor_scan(F, one, lf, 0.0, ALU.mult, ALU.add))
            link(V.tensor_tensor(b_, ig, F, ALU.subtract))
            link(V.tensor_tensor_scan(M, one, b_, 0.0, ALU.mult, ALU.max))
            link(V.tensor_tensor(ab[:, 10, :], F, M, ALU.add), "mt_p")
            link(V.tensor_scalar(ab[:, 11, :], b_, M[:, TP - 1:TP], None, ALU.subtract), "mt_p")
            dve.wait_ge(*done("bT_mm"))
            link(V.tensor_copy(bT.rearrange("p a b -> p (a b)"), bank[4][:, 0:32]))

            for h in range(MH):
                if h == 0:
                    dve.wait_ge(*done("cvo_mm", 4))
                dve.wait_ge(S("sc_mm"), h + 1)
                if h >= 2:
                    dve.wait_ge(S("nd_mm"), h - 1)
                w = wdec[:, h % 2, :]
                link(V.tensor_scalar(w[:, 0:TP], bank[1][:, 0:TP], bT[:, 0, h:h + 1], 0.0, ALU.subtract, ALU.max))
                link(V.tensor_scalar(w[:, TP:384], bank[1][:, P:TP], bT[:, 1, h:h + 1], 0.0, ALU.subtract, ALU.max), "wd")
                dve.wait_ge(S("wd_x"), h + 1)
                s_ = sw[:, h % 2, :]
                link(V.tensor_tensor(s_, w, bank[0][:, 0:384], ALU.mult), "dec")
                link(V.tensor_tensor(s_[:, 0:P], s_[:, 0:P], tri, ALU.mult))
                link(V.tensor_tensor(s_[:, TP:384], s_[:, TP:384], tri, ALU.mult), "sw")
                dve.wait_ge(S("kt_mm"), h + 1)
                if h >= 2:
                    dve.wait_ge(S("c_mm"), h - 1)
                link(V.tensor_scalar(kw[:, h % 2, 0, :], bank[5][:, 0:MD], bT[:, 0, MH + h:MH + h + 1], None, ALU.mult))
                link(V.tensor_scalar(kw[:, h % 2, 1, :], bank[5][:, MD:2 * MD], bT[:, 1, MH + h:MH + h + 1], None, ALU.mult), "kw_ev")
                dve.wait_ge(S("den_x"), h + 1)
                link(V.tensor_tensor(hden, hden, bank[2][0:MD, 0:TP], ALU.max))
                link(V.reciprocal(hden, hden))
                link(V.tensor_tensor(hT[:, h, 0:TP], bank[3][0:MD, 0:TP], hden, ALU.mult), "hp")
                dve.wait_ge(S("c_mm"), h + 1)
                link(V.tensor_copy(cout[:, h, :], bank[6][0:MD, 0:MD]))
                link(V.tensor_copy(nout[:, h, :], bank[6][0:1, P:P + MD]), "c_ev")

            tms, lfs, a_, mts, ws, gg, emts = (gs[:, i, :] for i in range(2, 9))
            igs, fgs = gs[:, 0, :], gs[:, 1, :]
            dve.wait_ge(S("ld_st"), 32)
            link(V.scalar_tensor_tensor(tms, fgs, -1.0, fgs, ALU.mult, ALU.max), "lf_abs")
            dve.wait_ge(S("lf_ln"), 2)
            link(V.scalar_tensor_tensor(lfs, fgs, 0.0, tms, ALU.min, ALU.subtract))
            link(V.tensor_tensor(a_, lfs, m0, ALU.add))
            link(V.tensor_tensor(mts, a_, igs, ALU.max))
            link(V.tensor_tensor(gs[:, 9, :], igs, mts, ALU.subtract))
            link(V.tensor_tensor(gs[:, 10, :], a_, mts, ALU.subtract), "mt_s")
            dve.wait_ge(S("gate_x"), 5)
            dve.wait_ge(*done("qks_mm"))
            for i in range(4):
                link(V.tensor_copy(qks[:, 4 * i:4 * i + 4, :], bank[i][0:TS, 0:384].rearrange("p (t d) -> p t d", t=4)),
                     "qks_ev" if i == 3 else None)
            link(V.tensor_tensor(kws, qks[:, MH:16, :], bc(ws, 2, MD), ALU.mult))
            link(V.tensor_tensor(ns, n0, bc(gg, 2, MD), ALU.mult))
            link(V.tensor_tensor(ns, ns, kws, ALU.add), "n_s")
            link(V.tensor_tensor(n0, ns, qks[:, 0:MH, :], ALU.mult))
            den, rr = gs[:, 11, :], gs[:, 12, :]
            link(V.tensor_reduce(den, n0, AX.X, ALU.add))
            link(V.scalar_tensor_tensor(den, den, -1.0, den, ALU.mult, ALU.max))
            link(V.tensor_tensor(den, den, emts, ALU.max))
            link(V.reciprocal(rr, den))
            d8 = ident[0:TS, 0:TS]
            link(V.tensor_tensor(bdg[:, 0, :, :], bc(gg, 1, TS), bc(d8, 2, MH), ALU.mult))
            link(V.tensor_tensor(bdg[:, 1, :, :], bc(rr, 1, TS), bc(d8, 2, MH), ALU.mult), "bd")
            dve.wait_ge(*done("gb_mm"))
            link(V.tensor_copy(gb.rearrange("p a b c -> p (a b c)"), bank[4][0:MD, 0:P]))
            dve.wait_ge(S("ld_c"), 16)
            link(V.tensor_tensor(cs.rearrange("p b h k -> p (b h) k"), cs.rearrange("p b h k -> p (b h) k"),
                                 bc(gb[:, 0, :, :].rearrange("p b h -> p (b h)"), 2, MD), ALU.mult))

            def diag(h):
                if h >= 2:
                    dve.wait_ge(S("op_mm"), 2 * h - 2)
                    dve.wait_ge(S("qb_mm"), 2 * h - 2)
                link(V.tensor_tensor(kdiag[:, h % 2, :, :], bc(kws[:, h, :], 1, TS), bc(d8, 2, MD), ALU.mult))
                link(V.tensor_tensor(qdiag[:, h % 2, :, :], bc(qks[:, h, :], 1, TS), bc(d8, 2, MD), ALU.mult), "kd")

            diag(0)
            for h in range(MH):
                if h + 1 < MH:
                    diag(h + 1)
                for half in range(2):
                    n = 2 * h + half
                    c_ = cs[:, 4 * half:4 * half + 4, h, :]
                    dve.wait_ge(S("op_mm"), n + 1)
                    link(V.tensor_tensor(c_, c_, bank[n % 2][0:MD, 0:384].rearrange("p (b k) -> p b k", b=4), ALU.add), "cup")
                    dve.wait_ge(S("qb_mm"), n + 1)
                    link(V.tensor_tensor(ctm[:, 0, :, :], c_, bank[2 + n % 2][0:MD, 0:384].rearrange("p (b k) -> p b k", b=4),
                                         ALU.mult), "cq")
                    link(V.tensor_reduce(num[:, h, 4 * half:4 * half + 4], ctm[:, 0, :, :], AX.X, ALU.add))
            link(V.tensor_tensor(hT[:, :, TP:NT], num, gb[:, 1, :, :].rearrange("p b h -> p h b"), ALU.mult))

            dve.wait_ge(*done("o_ev", 8))
            link(V.tensor_tensor(hT, hT, og, ALU.mult))
            link(V.tensor_tensor(sq[0:MD, :, :], hT, hT, ALU.mult), "hsq")
            for h in range(MH):
                dve.wait_ge(*done("hn_mm", h + 1))
                r = rtmp[0:MD, 0:NT]
                link(V.tensor_scalar(r, bank[h % 2][0:MD, 0:NT], 1.0 / MD, EPS, ALU.mult, ALU.add))
                link(V.reciprocal(r, r), "hn_rc")
                dve.wait_ge(S("hn_rs"), h + 1)
                link(V.scalar_tensor_tensor(hT[:, h, :], hT[:, h, :], hg[:, h:h + 1], rstd[0:MD, 0:NT], ALU.mult, ALU.mult), "hn")

            mem_attend_dve(dve, link, V, 0)

            for m_ in range(KT):
                dve.wait_ge(*done("woa_mm", m_ + 1))
                link(V.tensor_tensor(xT[:, m_, :], xT[:, m_, :], bank[m_ % 2][:, 0:NT], ALU.add), "woa_ev")
            norm(2, xT[:, :, :], NT, uT[:, :, :], FFN0)
            for j in range(DFF // P):
                dve.wait_ge(S("ff_si"), j + 1)
                link(V.tensor_tensor(hff[:, j, :], silu[:, j % 2, :], bank[2 * (j % 2) + 1][:, 0:NT], ALU.mult), "ff_h")
            for m_ in range(KT):
                dve.wait_ge(S("ff_d"), m_ + 1)
                link(V.tensor_tensor(xT[:, m_, :], xT[:, m_, :], bank[4 + m_ % 2][:, 0:NT], ALU.add), "ff_y")

            layer_b_dve(dve, link, V, norm)

        @block.scalar
        def _(act):
            link = chain(act, "act")

            def f(out, in_, fn, **kw_):
                return nc.scalar.activation(out, in_, fn, **kw_)

            def root(n, width):
                act.wait_ge(S("nrm_rc"), n + 1)
                link(f(rstd[:, 0:width], rtmp[:, 0:width], ACT.Sqrt), "nrm_rs")

            root(0, NMEM)
            root(1, NT)
            act.wait_ge(*done("pre0"))
            for t in range(16):
                act.wait_ge(*done("qk_mm", t + 1))
                link(f(preP[:, t, 3:TP + 3], bank[t % 2][0:MD, 0:TP], ACT.Copy))
                link(f(preS[:, t, :, CW - 1], bank[t % 2][0:MD, TP:NT], ACT.Copy), "qk_ev")
            for n in range(6):
                act.wait_ge(*done("v_mm", n + 1))
                c, i = n // 3, n % 3
                dst = vp[:, i, 384 * c:384 * c + 384] if i < 2 else vs[:, 384 * c:384 * c + 384]
                link(f(dst, bank[2 + i][0:(P if i < 2 else TS), 0:384], ACT.Copy), "v_ev")
            for h in range(MH):
                act.wait_ge(*done("o_mm", h + 1))
                link(f(og[:, h, :], bank[h % 2][0:MD, 0:NT], ACT.Sigmoid), "o_ev")
            for t in range(16):
                act.wait_ge(S("cv"), t + 1)
                link(f(qk[:, t, 0:TP], qk[:, t, 0:TP], ACT.Silu), "qk_si")
            act.wait_ge(S("cv"), 17)
            link(f(qk[:, :, TP:NT], qk[:, :, TP:NT], ACT.Silu), "qk_si")
            act.wait_ge(S("lf_abs"), 1)
            tm = ab[:, 2, :]
            link(f(tm, tm, ACT.Exp, scale=-1.0))
            link(f(tm, tm, ACT.Ln, bias=1.0), "lf_ln")
            act.wait_ge(S("mt_p"), 2)
            link(f(ab[:, 6, :], ab[:, 10, :], ACT.Exp, scale=-1.0), "gate_x")
            link(f(ab[:, 7, :], ab[:, 11, :], ACT.Exp), "gate_x")
            for h in range(MH):
                act.wait_ge(S("wd"), h + 1)
                w = wdec[:, h % 2, :]
                link(f(w, w, ACT.Exp, scale=-1.0), "wd_x")
                act.wait_ge(S("nd_mm"), h + 1)
                if h:
                    act.wait_ge(S("hp"), h)
                link(f(hden, bank[4][0:MD, 0:TP], ACT.Abs), "den_x")
            act.wait_ge(S("lf_abs"), 2)
            tms = gs[:, 2, :]
            link(f(tms, tms, ACT.Exp, scale=-1.0))
            link(f(tms, tms, ACT.Ln, bias=1.0), "lf_ln")
            act.wait_ge(*done("mt_s"))
            link(f(gs[:, 6, :], gs[:, 9, :], ACT.Exp), "gate_x")
            link(f(gs[:, 7, :], gs[:, 10, :], ACT.Exp), "gate_x")
            link(f(gs[:, 8, :], gs[:, 5, :], ACT.Exp, scale=-1.0), "gate_x")
            for h in range(MH):
                act.wait_ge(S("hn_rc"), h + 1)
                link(f(rstd[0:MD, 0:NT], rtmp[0:MD, 0:NT], ACT.Sqrt), "hn_rs")
            mem_attend_act(act, link, f, 0)
            root(2, NT)
            for j in range(DFF // P):
                act.wait_ge(S("ff_gu"), j + 1)
                if j >= 2:
                    act.wait_ge(S("ff_h"), j - 1)
                link(f(silu[:, j % 2, :], bank[2 * (j % 2)][:, 0:NT], ACT.Silu), "ff_si")
            layer_b_act(act, link, f, root)

        @block.gpsimd
        def _(pool):
            def load(name, dst, src, **kw_):
                pool.dma_start(dst, src, **kw_).then_inc(S(name), 16)

            stores, named = [0], {}

            def store(dst, src, name="stored"):
                pool.dma_start(dst, src).then_inc(S(name), 16)
                stores[0] += name == "stored"
                named[name] = named.get(name, 0) + 1

            pool.wait_ge(*done("set_mm", 17))
            load("ld_conv", cvh, I["state_mlstm_conv"][0].rearrange("b j c -> (b j) c"))
            load("ld_gb", gbias_p[:, 0:1], I["b_gate_a"][0].rearrange("(g h o) -> g h o", g=2, o=1)[0])
            load("ld_gb", gbias_p[:, 1:2], I["b_gate_a"][0].rearrange("(g h o) -> g h o", g=2, o=1)[1])
            load("ld_gb", gbias_s, I["b_gate_a"].broadcast_to((TS, 16)))
            store(O["conv_s"][0, :, 0:CW - 2, :], I["state_mlstm_conv"][0, :, 1:CW - 1, :])
            store(O["win_s"][0, :, 0:WBUF - 1], I["cache_nsa_win"][0, :, 1:WBUF])
            mem_store(pool, store, 0)
            pool.wait_ge(S("mt_p"), 1)
            store(O["m_p"][0, 0].rearrange("(h o) -> h o", o=1), ab[:, 10, TP - 1:TP], "st_a")
            pool.wait_ge(*done("cvo_ev", 4))
            store(O["conv_p"][0, 0], cv3, "st_cv")
            store(O["conv_s"][0, :, CW - 2, :], cv8, "st_cv")
            pool.wait_ge(S("c_ev"), 8)
            store(O["C_p"][0, 0].rearrange("h v k -> v h k"), cout, "st_cv")
            store(O["n_p"][0], nout, "st_cv")
            pool.wait_ge(S("c_mm"), 8)
            pool.wait_ge(S("nd_mm"), 8)
            pool.wait_ge(*done("qks_mm"))
            pool.wait_ge(S("st_a"), 16)
            load("ld_c", cs.rearrange("p b h k -> p (b h) k"), I["state_mlstm_C"][0].rearrange("b h v k -> v (b h) k"))
            pool.wait_ge(S("st_cv"), 64)
            load("ld_st", n0, I["state_mlstm_n"][0])
            load("ld_st", m0, I["state_mlstm_m"][0])
            pool.wait_ge(*done("mt_s"))
            store(O["m_s"][0], gs[:, 5, :])
            pool.wait_ge(*done("n_s"))
            store(O["n_s"][0], ns, "st_n")
            pool.wait_ge(S("cup"), 16)
            store(O["C_s"][0].rearrange("b h v k -> v (b h) k"), cs.rearrange("p b h k -> p (b h) k"), "st_c")
            pool.wait_ge(S("st_n"), 16)
            pool.wait_ge(*done("hsq"))
            pool.wait_ge(S("gate_x"), 5)
            mem_load(pool, load, 0)
            layer_b_pool(pool, load, store)
            pool.wait_ge(S("stored"), 16 * stores[0])
            for name in ("st_mem", "st_a", "st_cv", "st_n", "st_c", "st_rows", "st_win", "st_y"):
                pool.wait_ge(S(name), 16 * named[name])


_OUTS = [("y_prompt", (1, TP, D)), ("y_sample", (TS, 1, D)),
         ("mem_k_p", (2, 1, NMEM, XH, HD)), ("mem_v_p", (2, 1, NMEM, XH, HD)),
         ("C_p", (1, 1, MH, MD, MD)), ("n_p", (1, 1, MH, MD)), ("m_p", (1, 1, MH)), ("conv_p", (1, 1, CW - 1, 2 * TOK)),
         ("rows_p", (1, 1, TP, 4, NKV, HD)), ("win_p", (1, 1, TP, 2, NKV, HD)),
         ("C_s", (1, TS, MH, MD, MD)), ("n_s", (1, TS, MH, MD)), ("m_s", (1, TS, MH)), ("conv_s", (1, TS, CW - 1, 2 * TOK)),
         ("rows_s", (1, TS, 1, 4, NKV, HD)), ("win_s", (1, TS, WBUF, 2, NKV, HD))]


def kernel(**inputs):
    import concourse.bacc as _bacc
    from concourse.bass_utils import run_bass_kernel_spmd as _run

    nc = _bacc.Bacc("TRN2", target_bir_lowering=False, num_devices=1)
    arrays, I, O = {}, {}, {}
    laid = dict(inputs)
    laid["consts"], laid["dist12"] = _const_arrays(), _dist12_arrays()
    for name, a in laid.items():
        a = np.ascontiguousarray(a)
        arrays[f"in_{name}"] = a
        I[name] = nc.dram_tensor(f"in_{name}", a.shape, mybir.dt.from_np(a.dtype), kind="ExternalInput").ap()
    for name, shape in _OUTS:
        O[name] = nc.dram_tensor(f"out_{name}", shape, F32, kind="ExternalOutput").ap()
    build(nc, I, O)
    r = _run(nc, [arrays], core_ids=[0])
    return tuple(r.results[0][f"out_{name}"] for name, _ in _OUTS)
```

```python
from contextlib import ExitStack

import numpy as np
import concourse.bass as bass
from concourse import mybir

F32 = mybir.dt.float32
F32R = mybir.dt.float32r
I32 = mybir.dt.int32
ALU = mybir.AluOpType
ACT = mybir.ActivationFunctionType
AX = mybir.AxisListType

P = 128
D = 1024
KT = D // P
TP, TS = 256, 8
NT = TP + TS
HD = 64
MH, MD = 8, 96
TOK = MH * MD
NQ, NKV, GRP = 12, 4, 3
NMEM = 256
XH = 4
CW = 4
DFF, EFF, NE = 2816, 1792, 8
PAGE, NPAGES, NPOOL = 128, 16, 160
PAST = PAGE * NPAGES
WBUF = 512
CST = 16
NSEG = PAST // CST
NCMP = NSEG - 1
NBLK = PAST // 64
NSEL = 16
EPS = 1e-6
FAR = 1e30
SLOPES = [float(np.float32(2.0) ** np.float32(-8.0 * (h + 1) / NQ)) for h in range(NQ)]
RING = 3
SLOT = 4096

SHARED = {
    "proj_mm": (("g_mm", 3), ("qk_mm", 16), ("v_mm", 6), ("o_mm", 8), ("woa_mm", 8),
                ("bq_mm", 6), ("bkv_mm", 9), ("bg_mm", 3), ("wob_mm", 8)),
    "turn_mm": (("set_mm", 17), ("cvh_mm", 1), ("cvo_mm", 4), ("bT_mm", 1), ("qks_mm", 1), ("ms_pt0", 1),
                ("kd_mm", 8), ("kn_mm", 3), ("ms_pt1", 1), ("om_mm", 6), ("pct", 1), ("cbt", 1), ("y_mm", 18)),
    "once_mm": (("mkT_mm0", 1), ("gb_mm", 1), ("hn_mm", 1), ("hn_bc", 8), ("ms_o0", 1), ("mkT_mm1", 1), ("ms_o1", 1), ("im", 1), ("oc_mm", 1),
                ("rt", 1), ("cbb", 8)),
    "proj_ev": (("woa_ev", 8), ("bq_ev", 6), ("bkv_ev", 9), ("wob_ev", 8)),
    "turn_ev": (("set_ev", 17), ("cvo_ev", 4), ("kd_ev", 8), ("kn_ev", 3), ("om_ev", 6), ("cbb_ev", 8), ("y_ev", 18)),
    "once_dve": tuple((n, 1) for n in (
        "pre0", "mt_s", "bd0", "qk_done", "n_s", "bd", "hsq", "ms_q0", "ms_d0", "ms_p0", "ms_pte0", "mixm0", "u_split0",
        "q12", "idx", "ms_q1", "ms_d1", "ms_p1", "ms_pte1", "mixm1", "pc_d", "pc_p", "pc_s", "imp", "pct_ev",
        "sel", "oc_ev", "pz0", "mixT", "rt_d", "cb", "u_split1", "cbt_ev")),
    "copied": (("qk_ev", 16), ("v_ev", 6), ("o_ev", 8)),
    "once_act": (("ms_e0", 1), ("gates", 2), ("ms_e1", 1), ("pc_e", 1), ("rt_e", 1)),
}
STAGE = {}
for _sem, _stages in SHARED.items():
    _at = 0
    for _name, _n in _stages:
        STAGE[_name] = (_sem, _at)
        _at += _n


MIX0, MIX1, MEM0, MEM1, FFN0, FFN1, FINAL = range(7)

CONSTS = {}


def _const_arrays():
    p = np.arange(P)
    cols = []

    def add(name, a):
        a = np.asarray(a, np.float32).reshape(P, -1)
        CONSTS[name] = (sum(c.shape[1] for c in cols), a.shape[1])
        cols.append(a)

    add("ident", np.eye(P))
    add("ones", np.ones((P, P)))
    sel = np.zeros((P, 8, P))
    for e in range(8):
        sel[e, e] = 1
    add("sel8", sel)
    t = np.arange(P)
    dist = np.stack([(i * P + t)[:, None] - np.arange(TP)[None] for i in range(2)], 1).astype(np.float64)
    add("dist", np.where(dist >= 0, dist, FAR))
    add("tri", (t[:, None] <= t[None, :]))
    cend = np.arange(TP // CST) * CST + 2 * CST - 1
    dc = np.stack([(i * P + t)[:, None] - cend[None] for i in range(2)], 1).astype(np.float64)
    add("distc", np.where(dc >= 0, dc, FAR))
    add("maskc", dc >= 0)
    g = np.zeros((P, 4))
    for h in range(NQ):
        g[h, h // GRP] = 1
    add("grp", g)
    nsl = np.zeros((P, 1))
    nsl[:NQ, 0] = -np.array(SLOPES)
    add("nsl", nsl)
    add("seg", (p % 8) * 2 * CST)
    first = np.zeros((P, 1, 33, 33))
    first[:] = (np.arange(33)[None, :] < np.arange(33)[:, None])
    add("lower", first)
    return np.ascontiguousarray(np.concatenate(cols, 1))


def _dist12_arrays():
    l, n = np.arange(CST), np.arange(NSEG)
    slc = PAST - (n[None, :] * CST + l[:, None])
    cmp_ = PAST - (n * CST + 2 * CST - 1)
    r, q = np.arange(WBUF // P), np.arange(P)
    win = WBUF - (q[None, :] * (WBUF // P) + r[:, None])
    row = np.concatenate([slc.ravel(), cmp_.ravel(), win.ravel()]).astype(np.float32)
    return np.ascontiguousarray(np.broadcast_to(row, (NQ, row.size)))


def bc(ap, axis, n):
    v = ap.unsqueeze(axis)
    shape = list(v.shape)
    shape[axis] = n
    return v.broadcast_to(tuple(shape))


def chunk_list(I):
    ch = []

    def kview(w, c0, c1):
        return w.rearrange("(k p) c -> p k c", p=P)[:, :, c0:c1]

    def add(name, read, *dmas):
        ch.append((name, read, dmas))

    def std(name, read, w, c0, c1, kt=KT):
        add(name, read, (0, P, (kt, c1 - c0), kview(w, c0, c1)))

    wa, wb, wo, wm = I["w_in_a"][0], I["w_in_b"][0], I["w_out"], I["w_mem_kv"]
    std("mkv0", ("mkv_mm", 2), wm[0], 0, 512)
    std("gxa", ("g_mm", 3), wa, 3072, 3344)
    for c in range(8):
        read = (("qk_mm", 4 * c + 4), ("v_mm", 3 * (c - 4) + 3), ("o_mm", 4 * (c - 6) + 4))[(c >= 4) + (c >= 6)]
        std(("q", "k", "v", "o")[c // 2] + str(c % 2), read, wa, 384 * c, 384 * c + 384)
    for m in range(4):
        sl = slice(256 * m, 256 * m + 256)
        add(f"woa{m}", ("woa_mm", 2 * m + 2),
            (0, MD, (MH, 256), wo[0, 0:TOK, :].rearrange("(k p) c -> p k c", p=MD)[:, :, sl]),
            (MH * 256, P, (2, 256), wo[0, TOK:D, :].rearrange("(k p) c -> p k c", p=P)[:, :, sl]))
    for j in range(DFF // 256):
        gu = I["w_ffn_gu"][0]
        add(f"gu{j}", ("ff_mm", 2 * j + 2), (0, P, (KT, 256), kview(gu, 256 * j, 256 * j + 256)),
            (KT * 256, P, (KT, 256), kview(gu, DFF + 256 * j, DFF + 256 * j + 256)))
    for m in range(KT):
        std(f"dn{m}", ("ff_mm", DFF // P + m + 1), I["w_ffn_d"][0], P * m, P * m + P, kt=DFF // P)
    std("mkv1", ("mkv_mm", 4), wm[1], 0, 512)
    for c in range(2):
        std(f"bq{c}", ("bq_mm", 3 * c + 3), wb, 384 * c, 384 * c + 384)
    for c in range(3):
        std(f"bkv{c}", ("bkv_mm", 3 * c + 3), wb, 768 + 512 * c, 1280 + 512 * c)
    std("gxb", ("bg_mm", 3), wb, 2304, 2596)
    for m in range(4):
        std(f"wob{m}", ("wob_mm", 2 * m + 2), wo[1], 256 * m, 256 * m + 256)
    return ch


ITEMS = EFF // P + D // P
GU, DN = EFF // 256, D // 256


class Ring:

    def __init__(self, ch):
        self.at, loads = {}, [0] * RING
        for n, (name, _, dmas) in enumerate(ch):
            s = n % RING
            loads[s] += 16 * len(dmas)
            self.at[name] = (s, loads[s])
        self.expert, self.per = [], [0] * RING
        for i in range(GU + DN):
            s = (len(ch) + i) % RING
            self.per[s] += 32 if i < GU else 16
            self.expert.append((s, loads[s] + self.per[s]))


def build(nc, I, O):
    ctx = ExitStack()
    with ctx:
        def sb(name, shape, dt=F32):
            return ctx.enter_context(nc.sbuf_tensor(name, shape, dt))

        def sb_split(name, shape):
            at = nc.sbuf_base
            at += -at % 32
            t = sb(name, shape)
            return t, nc.alloc_sbuf_tensor_at(name + "_r", shape, F32R, offset=at)

        sems = {}

        def S(name):
            name = STAGE.get(name, (name,))[0]
            if name not in sems:
                sems[name] = ctx.enter_context(nc.semaphore(name))
            return sems[name]

        def done(name, n=1):
            sem, before = STAGE.get(name, (name, 0))
            return S(sem), before + n

        bank = [ctx.enter_context(nc.psum_tensor(f"bank{i}", [P, 512], F32)) for i in range(8)]

        chunks = chunk_list(I)
        ring_at = Ring(chunks)
        by_name = {name: dmas for name, _, dmas in chunks}
        scr_imp = nc.dram_tensor("scr_imp", (NKV, TS * 33), F32).ap()
        scr_sel = nc.dram_tensor("scr_sel", (NKV, TS * 33), F32).ap()

        ncst = I["consts"].shape[1]
        consts = sb("consts_sb", [P, ncst])

        def C(name):
            a, n = CONSTS[name]
            return consts[:, a:a + n]

        ident, ones = C("ident"), C("ones")
        sel8 = C("sel8").rearrange("p (e m) -> p e m", e=8)
        dist = C("dist").rearrange("p (i k) -> p i k", i=2)
        distc = C("distc").rearrange("p (i n) -> p i n", i=2)
        maskc = C("maskc").rearrange("p (i n) -> p i n", i=2)
        tri, grp, nsl = C("tri"), C("grp"), C("nsl")
        lower = C("lower")
        xT = sb("xT", [P, KT, NT])
        uT, uT_r = sb_split("uT", [P, KT, NT])
        rstd = sb("rstd", [P, NT])
        rtmp = sb("rtmp", [P, NT])
        gain = sb("gain", [P, 56])
        memT = sb("memT", [P, KT, NMEM])
        ring, ring_r = sb_split("ring", [P, RING, SLOT])
        mkv = sb("mkv", [P, 2, 512])
        mkT = sb("mkT", [P, 2, NMEM])
        xq = sb("xq", [P, 2, NT])
        mixm = sb("mixm", [P, 2, NT])
        small = sb("small", [P, 512])
        nfree = nc.sbuf_bytes_remaining // 4 - 64
        arena, arena_r = sb_split("arena", [P, nfree])

        top = [0]

        def area(*shape, base=arena):
            n = int(np.prod(shape[1:]))
            a = top[0]
            top[0] += n
            assert top[0] <= nfree, (top[0], nfree)
            v = base[0:shape[0], a:a + n]
            if len(shape) > 2:
                names = "abcd"[:len(shape) - 1]
                v = v.rearrange(f"p ({' '.join(names)}) -> p {' '.join(names)}",
                                **{x: s for x, s in zip(names[:-1], shape[1:-1])})
            return v

        def place():
            return top[0]

        xin = area(P, 2, D)
        xsin = area(TS, D)
        min_ = area(P, 2, D)
        grow = area(56, P)
        cwrow = area(64, MD)
        hgrow = area(MH, MD)
        top[0] = 0
        sq = area(P, KT, NT)
        kept = place()
        top[0] = 0
        uh = area(P, KT, NT, base=arena_r)
        cw = area(MD, 64)
        hg = area(MD, MH)
        og = area(MD, MH, NT)
        vs = area(TS, TOK)
        hT = area(MD, MH, NT)
        gs = area(TS, 16, MH)
        bT = area(P, 2, 16)
        gbias_p = area(MH, 2)
        gbias_s = area(TS, 16)
        csel = area(P, MH, MH)
        rs8 = area(MH, NT)
        late = place()
        qk = area(MD, 16, NT)
        vp = area(P, 2, TOK)
        ab = area(MH, 12, TP)
        a_work = place()
        preP = area(MD, 16, TP + 3)
        preS = area(MD, 16, TS, CW)
        cvh = area(24, 2 * TOK)
        cv3 = area(3, 2 * TOK)
        cv8 = area(TS, 2 * TOK)
        ctmp = area(MD, 16, TS)
        conv_end = place()
        top[0] = a_work
        wdec = area(P, 2, 384)
        sw = area(P, 2, 384)
        kw = area(P, 2, 2, MD)
        hden = area(MD, TP)
        cout = area(MD, MH, MD)
        nout = area(1, MH, MD)
        assert place() <= a_work + 16 * (TP + 3)
        c_place = place()
        cs = area(MD, TS, MH, MD)
        n0 = area(TS, MH, MD)
        m0 = area(TS, MH)
        bdg = area(TS, 2, TS, MH)
        gb = area(MD, 2, TS, MH)
        assert c_place + TS * MH * MD >= conv_end
        top[0] = late
        qks = area(TS, 16, MD)
        kws = area(TS, MH, MD)
        ns = area(TS, MH, MD)
        kdiag = area(TS, 2, TS, MD)
        qdiag = area(TS, 2, TS, MD)
        ctm = area(MD, 4, MD)
        num = area(MD, MH, TS)
        assert place() <= a_work
        top[0] = late
        mvs_a = area(P, TS, 2, 256)
        assert place() <= a_work
        top[0] = a_work
        mem_u_a = area(P, KT, NMEM)
        top[0] = a_work
        pm_a = area(P, 2, NMEM)
        pmT_a = area(P, 2, 2, P)
        mksT_a = area(P, 2, 512)
        xqz_a = area(P, TS, 2, XH)
        assert place() <= a_work + 4 * 384 + 4 * MD + TP
        top[0] = c_place
        mks_a = area(P, TS, 2, 256)
        pms_a = area(XH, TS, NMEM)
        pmsT_a = area(P, TS, 2, XH)
        top[0] = kept
        whi = area(P, 2, DFF // P, P, base=arena_r)
        silu = area(P, 2, NT)
        ytmp = area(P, 2, NT)
        hsum = area(P, 2, NT)
        hff = area(P, 2, DFF // P, NT, base=arena_r)
        top[0] -= 2 * (DFF // P - EFF // P) * NT
        hfe = hff.rearrange("p u j n -> p (u j) n")[:, 0:2 * (EFF // P), :].rearrange("p (u j) n -> p u j n", u=2)
        comb = area(P, NE, NT)
        combT = area(NE, NT)
        lg = area(P, 3, 4, 8)
        rk = area(P, 3, 8, 8)
        rk2 = area(P, 3, 8, 8)
        l8 = area(P, 3, 8)
        wr = area(P, KT, NE)
        top[0] = kept
        ysb = area(P, 3, D)

        top[0] = kept
        mixT = area(P, 6, NT)
        kvS = area(TS, 6, 256)
        g12 = area(NQ, 3, TS)
        pages = area(P, TS).bitcast(I32)
        idxb = area(P, TS).bitcast(I32)
        q12 = area(HD, TS, NKV, NQ)
        qblk = area(P, TS, 2, NQ)
        knT = area(HD, 2, NKV, TS)
        sel12 = area(NQ, TS, 33)
        oc = area(P, TS, 2, 6)
        slc0 = place()
        perow = area(32, P)
        w2 = area(HD, 2, HD)
        vcp = area(TP // CST, NKV, HD)
        kcp2 = area(P, NKV, 16)
        hconst = area(HD, 2)
        pec = area(P, 2, CST)
        gb12 = area(NQ, 3)
        gbp = area(P, 36)
        gp = area(P, 2, 36)
        qT = area(P, 6, NT)
        w1 = area(P, 2, 8, 2, HD)
        b_work = place()
        mem_u_b = area(P, KT, NMEM)
        top[0] = b_work
        pm_b = area(P, 2, NMEM)
        pmT_b = area(P, 2, 2, P)
        mks_b = area(P, TS, 2, 256)
        mvs_b = area(P, TS, 2, 256)
        mksT_b = area(P, 2, 512)
        xqz_b = area(P, TS, 2, XH)
        pms_b = sq.rearrange("p k n -> p (k n)")[0:XH, 0:TS * NMEM].rearrange("p (b n) -> p b n", b=TS)
        pmsT_b = area(P, TS, 2, XH)
        mem_end = place()
        top[0] = b_work
        gat = area(P, 2, 8, 512)
        x_place = place()
        xt = area(P, 2, 512)
        hb = area(HD, 2, 512)
        hs = area(HD, 2, 512)
        cmp_end = place()
        kc = area(HD, 2, 512)
        vcmp = area(P, TS, 256)
        imp = area(NKV, TS, 33)
        imp32 = area(32, 33)
        sel32 = area(32, 33)
        pc = area(NQ, TS, NSEG)
        pcT = area(P, TS, NQ)
        psum4 = uT.rearrange("p k n -> p (k n)")[0:NKV, 0:TS * NSEG].rearrange("p (b n) -> p b n", b=TS)
        top[0] = x_place
        rank = area(32, 33, 33)
        rank2 = area(32, 33, 33)
        assert top[0] <= cmp_end and x_place >= slc0 + CST * 512
        top[0] = b_work
        sc = area(P, 3, 2, TP)
        scc = area(P, 3, 16)
        pT = area(P, 2, 4, P)
        pcpT = area(16, 2, P)
        assert place() <= cmp_end
        top[0] = max(cmp_end, mem_end)
        kvP = area(P, 2, 6, 256)
        kdup = area(P, 2, NKV, TP)
        oP = sq.rearrange("p k n -> p (k n)")[:, 0:2 * TOK].rearrange("p (i c) -> p i c", i=2)
        d12s = memT.rearrange("p k n -> p (k n)")[0:NQ, :]
        d12b = mkv.rearrange("p k n -> p (k n)")[0:NQ, 0:NSEG + WBUF]
        top[0] = slc0
        gsl = area(P, 2, CST, 512)

        def past_row(b, l):
            if b % 3 == 0:
                return ring[:, 2 * (l // 8), 512 * (l % 8):512 * (l % 8) + 512]
            return gsl[:, b % 3 - 1, l, :]

        winb = (area(P, 4, 512), uT.rearrange("p k n -> p (k n)")[:, 0:2048].rearrange("p (r d) -> p r d", r=4))
        s12 = area(NQ, PAST + 1 + WBUF + 1)
        sqf = sq.rearrange("p k n -> p (k n)")
        kTb = sqf[:, 0:1024].rearrange("p (j n) -> p j n", j=2)
        pTs = sqf[:, 1024:1024 + 2 * 264].rearrange("p (a n) -> p a n", a=2)
        pz = sqf[0:NQ, 1600:1600 + 128].rearrange("p (r b c) -> p r b c", r=2, b=TS)
        oTsb = sqf[:, 1728:1728 + 96].rearrange("p (b j c) -> p b j c", b=TS, j=2)
        o12 = sqf[0:NQ, 1824:1824 + 256]

        block = ctx.enter_context(nc.Block())
        counts = {}

        def chain(eng, own):
            def link(ins, name=None, signal=True):
                if not signal:
                    return
                s = name or own
                counts[s] = counts.get(s, 0) + 1
                ins.then_inc(S(s), 1)
                eng.wait_ge(*done(s, counts[s]))
            return link

        def slot_view(name):
            s, _ = ring_at.at[name]
            dmas = by_name[name]
            out = []
            for off, parts, dims, _ in dmas:
                n = int(np.prod(dims))
                out.append(ring[0:parts, s, off:off + n].rearrange("p (k c) -> p k c", k=dims[0]))
            return out[0] if len(out) == 1 else out

        MEMPLACES = [(pm_a, pmT_a, mks_a, mvs_a, mksT_a, xqz_a, pms_a, pmsT_a),
                     (pm_b, pmT_b, mks_b, mvs_b, mksT_b, xqz_b, pms_b, pmsT_b)]


        def split_mm(mm, out, kt, weights, values):
            for k in range(kt):
                (w_h, w_l), (v_h, v_l) = weights(k), values(k)
                mm(out, w_h, v_h, k == 0, False)
                mm(out, w_h, v_l, False, False)
                m = mm(out, w_l, v_h, False, k == kt - 1)
            return m

        def gate_up(mm, signal, j, low):
            c0 = (j % 2) * P
            for u in range(2):
                m = split_mm(mm, bank[2 * (j % 2) + u][:, 0:NT], KT,
                             lambda k: (whi[:, j % 2, u * KT + k, :], low[:, u * KT + k, c0:c0 + P]),
                             lambda k: (uh[:, k, :], uT_r[:, k, :]))
            m.then_inc(S(signal[0]), signal[1])

        def by_gu(name, base=ring):
            s_, _ = ring_at.at[name]
            return base[:, s_, :].rearrange("p (k c) -> p k c", c=256)

        def by_dn(name, base=ring):
            s_, _ = ring_at.at[name]
            return base[:, s_, 0:DFF // P * P].rearrange("p (k c) -> p k c", c=P)

        def split(V, link, signal, value, high, low):
            link(V.tensor_copy(high, value))
            link(V.tensor_tensor(low, value, high, ALU.subtract), signal)

        def mem_project(mm, w, L, i):
            mem_u = (mem_u_a, mem_u_b)[L]
            for k in range(KT):
                m = mm(bank[5 + i][:, :], mem_u[:, k, P * i:P * i + P], w[:, k, :], k == 0, k == KT - 1)
            m.then_inc(S("mkv_mm"), 1)

        def mem_turn(pe, tr, L):
            pe.wait_ge(S("mkv_ev"), 3 * L + 2)
            for j in range(2):
                for i in range(2):
                    m = tr(bank[5][:, NMEM * j + P * i:NMEM * j + P * i + P], mkv[:, i, P * j:P * j + P], P)
            m.then_inc(S(f"mkT_mm{L}"), 1)

        def mem_rows_dve(dve, link, V, L):
            if L:
                dve.wait_ge(S("st_mem"), 64)
            for i in range(2):
                dve.wait_ge(S("mkv_mm"), 2 * L + i + 1)
                link(V.tensor_copy(mkv[:, i, :], bank[5 + i][:, :]), "mkv_ev")

        def mem_turn_dve(dve, link, V, L):
            dve.wait_ge(*done(f"mkT_mm{L}"))
            link(V.tensor_copy(mkT.rearrange("p j n -> p (j n)"), bank[5][:, :]), "mkv_ev")

        def mem_store(pool, store, L):
            pool.wait_ge(S("mkv_ev"), 3 * L + 2)
            for c, name in enumerate(("mem_k_p", "mem_v_p")):
                for i in range(2):
                    store(O[name][L, 0, P * i:P * i + P].rearrange("n h d -> n (h d)"),
                          mkv[:, i, 256 * c:256 * c + 256], "st_mem")

        def mem_load(pool, load, L):
            if L == 0:
                pool.wait_ge(S("st_c"), 16)
                pool.wait_ge(S("st_cv"), 64)
            mks, mvs = MEMPLACES[L][2:4]
            load("ld_mks", mks, I["cache_mem_k"][L].rearrange("b (p r) h d -> p b r (h d)", r=2))
            load("ld_mvs", mvs, I["cache_mem_v"][L].rearrange("b (p r) h d -> p b r (h d)", r=2))

        def mem_attend(pe, mm, tr, L, between=None):
            pm, pmT, mks, mvs, mksT, xqz, pms, pmsT = MEMPLACES[L]
            o = 8 * L

            def scores(n):
                h, i = n // 2, n % 2
                r = slice(64 * (h % 2), 64 * (h % 2) + 64)
                if n >= 2:
                    pe.wait_ge(S("ma_e"), o + n - 1)
                mm(bank[n % 2][:, 0:NMEM], xq[r, h // 2, P * i:P * i + P], mkT[r, h // 2, :]).then_inc(S("ma_s"), 1)

            def turn(n):
                pe.wait_ge(S("ma_p"), o + n + 1)
                if n >= 2:
                    pe.wait_ge(S("ma_pt"), o + n - 1)
                for t in range(2):
                    m = tr(bank[2 + n % 2][:, P * t:P * t + P], pm[:, n % 2, P * t:P * t + P], P)
                m.then_inc(S("ma_t"), 1)

            def values(n):
                h = n // 2
                pe.wait_ge(S("ma_pt"), o + n + 1)
                if n >= 2:
                    pe.wait_ge(S("ma_oe"), o + n - 1)
                for t in range(2):
                    m = mm(bank[4 + n % 2][:, 0:P], mkv[:, t, 256 + P * (h // 2):256 + P * (h // 2) + P],
                           pmT[:, n % 2, t, :], t == 0, t == 1)
                m.then_inc(S("ma_o"), 1)

            scores(0)
            scores(1)
            for n in range(8):
                turn(n)
                if n + 2 < 8:
                    scores(n + 2)
                if n:
                    values(n - 1)
            values(7)
            pe.wait_ge(S("ld_mks"), 16 * L + 16)
            pe.wait_ge(*done(f"ms_q{L}"))
            pe.wait_ge(S("ma_oe"), o + 8)

            def turn_keys(b):
                if b >= 2:
                    pe.wait_ge(S("ms_k"), o + b - 1)
                for j in range(2):
                    for r in range(2):
                        m = tr(bank[b % 2][:, 256 * j + P * r:256 * j + P * r + P], mks[:, b, r, P * j:P * j + P], P)
                m.then_inc(S("ms_t"), 1)

            turn_keys(0)
            for b in range(TS):
                if b + 1 < TS:
                    turn_keys(b + 1)
                pe.wait_ge(S("ms_k"), o + b + 1)
                for j in range(2):
                    m = mm(bank[4 + b // 2][0:XH, 256 * (b % 2):256 * (b % 2) + 256], xqz[:, b, j, :],
                           mksT[:, b % 2, 256 * j:256 * j + 256], j == 0, j == 1)
                m.then_inc(S("ms_s"), 1)
            if between:
                between()
            pe.wait_ge(*done(f"ms_p{L}"))
            pe.wait_ge(S("ms_k"), o + 8)
            for b in range(TS):
                for r in range(2):
                    m = tr(bank[0][:, 8 * b + 4 * r:8 * b + 4 * r + 4], pms[:, b, P * r:P * r + P], XH)
            m.then_inc(S(f"ms_pt{L}"), 1)
            pe.wait_ge(S("ld_mvs"), 16 * L + 16)
            pe.wait_ge(*done(f"ms_pte{L}"))
            for b in range(TS):
                for j in range(2):
                    for r in range(2):
                        m = mm(bank[1][:, 4 * b + 2 * j:4 * b + 2 * j + 2], mvs[:, b, r, P * j:P * j + P],
                               pmsT[:, b, r, 2 * j:2 * j + 2], r == 0, r == 1)
            m.then_inc(S(f"ms_o{L}"), 1)

        def mem_attend_dve(dve, link, V, L):
            pm, pmT, mks, mvs, mksT, xqz, pms, pmsT = MEMPLACES[L]
            o = 8 * L
            st = small[:, 0:64]
            link(V.memset(xqz, 0.0))
            for h in range(XH):
                r = slice(64 * (h % 2), 64 * (h % 2) + 64)
                link(V.tensor_copy(xqz[r, :, h // 2, h], xq[r, h // 2, TP:NT]), f"ms_q{L}" if h == XH - 1 else None)

            def maximum(n):
                dve.wait_ge(S("ma_s"), o + n + 1)
                link(V.tensor_reduce(st[:, 4 * (n % 2):4 * (n % 2) + 1], bank[n % 2][:, 0:NMEM], AX.X, ALU.max, negate=True), "ma_mx")

            def out(n):
                h, i = n // 2, n % 2
                r = slice(64 * (h % 2), 64 * (h % 2) + 64)
                dve.wait_ge(S("ma_o"), o + n + 1)
                link(V.tensor_copy(mixm[r, h // 2, P * i:P * i + P], bank[4 + n % 2][r, 0:P]), "ma_oe")

            maximum(0)
            maximum(1)
            for n in range(8):
                dve.wait_ge(S("ma_e"), o + n + 1)
                link(V.reciprocal(st[:, 4 * (n % 2) + 2:4 * (n % 2) + 3], st[:, 4 * (n % 2) + 1:4 * (n % 2) + 2]))
                link(V.tensor_scalar(pm[:, n % 2, :], pm[:, n % 2, :], st[:, 4 * (n % 2) + 2:4 * (n % 2) + 3], None, ALU.mult), "ma_p")
                dve.wait_ge(S("ma_t"), o + n + 1)
                link(V.tensor_copy(pmT[:, n % 2, :, :].rearrange("p t n -> p (t n)"), bank[2 + n % 2][:, 0:256]), "ma_pt")
                if n + 2 < 8:
                    maximum(n + 2)
                if n:
                    out(n - 1)
            out(7)
            for i in range(4):
                dve.wait_ge(S("ms_s"), o + 2 * i + 2)
                link(V.tensor_copy(pms[:, 2 * i:2 * i + 2, :].rearrange("p b n -> p (b n)"), bank[4 + i][0:XH, :]))
            mx, sm = small[0:XH, 64:72], small[0:XH, 72:80]
            link(V.tensor_reduce(mx, pms, AX.X, ALU.max))
            link(V.tensor_tensor(pms, pms, bc(mx, 2, NMEM), ALU.subtract), f"ms_d{L}")
            dve.wait_ge(*done(f"ms_e{L}"))
            link(V.tensor_reduce(sm, pms, AX.X, ALU.add))
            link(V.reciprocal(mx, sm))
            link(V.tensor_tensor(pms, pms, bc(mx, 2, NMEM), ALU.mult), f"ms_p{L}")
            dve.wait_ge(*done(f"ms_pt{L}"))
            link(V.tensor_copy(pmsT.rearrange("p b r h -> p (b r h)"), bank[0][:, 0:64]), f"ms_pte{L}")
            dve.wait_ge(*done(f"ms_o{L}"))
            ov = bank[1][:, 0:32].rearrange("p (b c) -> p b c", b=TS)
            for h in range(XH):
                r = slice(64 * (h % 2), 64 * (h % 2) + 64)
                link(V.tensor_copy(mixm[r, h // 2, TP:NT], ov[r, :, 2 * (h // 2) + h % 2]), f"mixm{L}" if h == XH - 1 else None)

        def mem_attend_act(act, link, f, L):
            pm, pmT, mks, mvs, mksT, xqz, pms, pmsT = MEMPLACES[L]
            o = 8 * L
            st = small[:, 0:64]
            for n in range(8):
                act.wait_ge(S("ma_mx"), o + n + 1)
                if n >= 2:
                    act.wait_ge(S("ma_t"), o + n - 1)
                link(f(pm[:, n % 2, :], bank[n % 2][:, 0:NMEM], ACT.Exp, bias=st[:, 4 * (n % 2):4 * (n % 2) + 1],
                       accum_out=st[:, 4 * (n % 2) + 1:4 * (n % 2) + 2]), "ma_e")
            for b in range(TS):
                act.wait_ge(S("ms_t"), o + b + 1)
                if b >= 2:
                    act.wait_ge(S("ms_s"), o + b - 1)
                link(f(mksT[:, b % 2, :], bank[b % 2][:, :], ACT.Copy), "ms_k")
            act.wait_ge(*done(f"ms_d{L}"))
            link(f(pms, pms, ACT.Exp), f"ms_e{L}")

        def layer_b_pe(pe, mm, tr, got, norm):
            pe.wait_ge(S("mem_u"), 2)
            w = got("mkv1")
            mem_project(mm, w, 1, 0)
            norm(3, NT)
            mem_project(mm, w, 1, 1)
            pe.wait_ge(S("nrm_out"), 4)
            for t in range(6):
                if t % 3 == 0:
                    w = got(f"bq{t // 3}")
                if t >= 2:
                    pe.wait_ge(*done("bq_ev", t - 1))
                c0 = (t % 3) * P
                for k in range(KT):
                    m = mm(bank[t % 2][:, 0:NT], w[:, k, c0:c0 + P], uT[:, k, :], k == 0, k == KT - 1)
                m.then_inc(S("bq_mm"), 1)
            mem_turn(pe, tr, 1)
            for n in range(9):
                c, i = n // 3, n % 3
                if i == 0:
                    w = got(f"bkv{c}")
                if n >= 3:
                    pe.wait_ge(*done("bkv_ev", n - 2))
                a, z = P * i, min(P * i + P, NT)
                for k in range(KT):
                    m = mm(bank[2 + i][0:z - a, :], uT[:, k, a:z], w[:, k, :], k == 0, k == KT - 1)
                m.then_inc(S("bkv_mm"), 1)
            w = got("gxb")
            pe.wait_ge(*done("bkv_ev", 9))
            for i in range(2):
                for k in range(KT):
                    mm(bank[2 + i][:, 0:36], uT[:, k, P * i:P * i + P], w[:, k, 0:36], k == 0, k == KT - 1)
            for c in range(3):
                for k in range(KT):
                    m = mm(bank[4][0:NQ, TS * c:TS * c + TS], w[:, k, NQ * c:NQ * c + NQ], uT[:, k, TP:NT], k == 0, k == KT - 1)
            m.then_inc(S("bg_mm"), 1)
            pe.wait_ge(S("mkv_ev"), 6)
            for j in range(2):
                for k in range(KT):
                    m = mm(bank[5 + j][:, 0:NT], w[:, k, 36 + P * j:36 + P * j + P], uT[:, k, :], k == 0, k == KT - 1)
                m.then_inc(S("bg_mm"), 1)
            pe.wait_ge(*done("bq_ev", 6))
            for n in range(8):
                br, g = n // 4, n % 4
                if n >= 2:
                    pe.wait_ge(*done("kd_ev", n - 1))
                for t in range(2):
                    m = tr(bank[n % 2][0:HD, P * t:P * t + P], kvP[:, t, 2 + 2 * br, HD * g:HD * g + HD], P)
                m.then_inc(S("kd_mm"), 1)
            pe.wait_ge(S("bg_ev"), 1)
            for n in range(8):
                br, g = n // 4, n % 4
                m = tr(bank[2][0:HD, TS * n:TS * n + TS], kvS[:, 2 + 2 * br, HD * g:HD * g + HD], TS)
            m.then_inc(S("kn_mm"), 1)
            pe.wait_ge(S("ld_w1"), 96)
            tr(bank[3][:, 0:32], perow, 32).then_inc(S("kn_mm"), 1)
            pe.wait_ge(*done("kn_ev", 2))
            for c in range(2):
                for i in range(CST):
                    m = mm(bank[4][0:HD, c:c + 1], w1[:, c, i % 8, i // 8, :], pec[:, c, i:i + 1], i == 0, i == CST - 1)
            m.then_inc(S("kn_mm"), 1)
            pe.wait_ge(*done("kn_ev", 3))
            mem_attend(pe, mm, tr, 1)
            pe.wait_ge(*done("mixm1"))
            compress_pe(pe, mm, tr, 0)
            compress_out(pe, mm, 0)

            def scores(n):
                h, i = n // 2, n % 2
                g, nk, r = h // GRP, P * (i + 1), slice(64 * (h % 2), 64 * (h % 2) + 64)
                q = qT[r, h // 2, P * i:P * i + P]
                if n >= 2:
                    pe.wait_ge(S("ps"), n - 1)
                mm(bank[n % 2][:, 0:nk], q, kdup[r, 0, g, 0:nk])
                mm(bank[n % 2][:, TP:TP + nk], q, kdup[r, 1, g, 0:nk])
                mm(bank[(2, 5)[n % 2]][:, 0:15], q, kcp2[r, g, 0:15]).then_inc(S("p_s"), 1)

            def turn_weights(n):
                i = n % 2
                pe.wait_ge(S("p_p"), n + 1)
                if n >= 2:
                    pe.wait_ge(S("p_te"), n - 1)
                    pe.wait_ge(S("p_oe"), n - 1)
                for br in range(2):
                    for t in range(i + 1):
                        tr(bank[3 + n % 2][:, TP * br + P * t:TP * br + P * t + P], sc[:, n % 3, br, P * t:P * t + P], P)
                tr(bank[6 + n % 2][0:15, P:2 * P], scc[:, n % 3, 0:15], P).then_inc(S("p_t"), 1)

            def values(n):
                h, i = n // 2, n % 2
                g = h // GRP
                pe.wait_ge(S("p_te"), n + 1)
                o = bank[6 + n % 2][:, 0:HD]
                for br in range(2):
                    for t in range(i + 1):
                        mm(o, pT[:, n % 2, 2 * br + t, :], kvP[:, t, 3 + 2 * br, HD * g:HD * g + HD], br == 0 and t == 0, False)
                mm(o, pcpT[0:15, n % 2, :], vcp[0:15, g, :], False, True).then_inc(S("p_o"), 1)

            pe.wait_ge(*done("kd_ev", 8))
            pe.wait_ge(S("kve"), 1)
            scores(0)
            scores(1)
            for n in range(2 * NQ):
                if n + 2 < 2 * NQ:
                    scores(n + 2)
                turn_weights(n)
                if n:
                    values(n - 1)
            values(2 * NQ - 1)
            pe.wait_ge(S("p_oe"), 2 * NQ)
            for j in range(6):
                if j >= 2:
                    pe.wait_ge(*done("om_ev", j - 1))
                for i in range(2):
                    m = tr(bank[j % 2][:, P * i:P * i + P], oP[:, i, P * j:P * j + P], P)
                m.then_inc(S("om_mm"), 1)
            pe.wait_ge(*done("om_ev", 6))

            pe.wait_ge(*done("q12"))
            for c in range(1, TS + 1):
                compress_pe(pe, mm, tr, c)
            compress_out(pe, mm, TS)
            compress_scores(pe, mm, TS)
            pe.wait_ge(*done("pc_p"))
            for i in range(2):
                m = mm(bank[i][0:NKV, 0:4 * NCMP], grp[0:NQ, :], pc[:, 4 * i:4 * i + 4, 0:NCMP])
            m.then_inc(S("im"), 1)
            pe.wait_ge(*done("pc_s"))
            for b in range(TS):
                m = tr(bank[2][0:NCMP, NQ * b:NQ * b + NQ], pc[:, b, 0:NCMP], NQ)
            m.then_inc(S("pct"), 1)
            pe.wait_ge(*done("pct_ev"))
            for b in range(TS):
                for j in range(2):
                    m = mm(bank[3][:, NQ * b + 6 * j:NQ * b + 6 * j + 6], vcmp[0:NCMP, b, P * j:P * j + P],
                           pcT[0:NCMP, b, 6 * j:6 * j + 6])
            m.then_inc(S("oc_mm"), 1)

            steps = TS * 10

            def turn(n):
                b, c, j = n // 10, n % 10 // 2, n % 2
                if c == 0 and j == 0:
                    pe.wait_ge(S(f"ld_g{b % 3}"), 256 * (b // 3 + 1))
                if c == 4 and j == 0:
                    pe.wait_ge(S(f"ld_win{b % 2}"), 16 * (b // 2 + 1))
                if n >= 2:
                    pe.wait_ge(S("kt_e"), n - 1)
                if b >= 2 and n % 10 == 0:
                    pe.wait_ge(S("pt_ev"), b - 1)
                if b and n % 10 == 1:
                    pe.wait_ge(S("s_n"), b)
                for r in range(4):
                    src = past_row(b, 4 * c + r)[:, P * j:P * j + P] if c < 4 else winb[b % 2][:, r, P * j:P * j + P]
                    m = tr(bank[j][:, P * r:P * r + P], src, P)
                m.then_inc(S("kt_t"), 1)

            def keys(b):
                for n in range(10 * b, 10 * b + 10):
                    c, j = n % 10 // 2, n % 2
                    if n + 1 < steps and n % 10 < 9:
                        turn(n + 1)
                    pe.wait_ge(S("kt_e"), n + 1)
                    if b and j == 0:
                        pe.wait_ge(S("s_ev"), 5 * b - 4 + c)
                    mm(bank[2 + c][0:NQ, :], qblk[:, b, j, :], kTb[:, j, :], j == 0, j == 1).then_inc(S("k_s"), 1)

            def new_keys(b):
                for br in range(2):
                    for g in range(NKV):
                        m = mm(bank[1][0:NQ, br:br + 1], q12[:, b, g, :], knT[:, br, g, b:b + 1], g == 0, g == NKV - 1)
                m.then_inc(S("k_n"), 1)

            def turn_weights_s(b):
                pe.wait_ge(S("p12"), b + 1)
                for l in range(CST):
                    tr(bank[0][:, NQ * l:NQ * l + NQ], s12[:, P * l:P * l + P], NQ)
                for r in range(4):
                    a = PAST + 1 + P * r
                    tr(bank[0][:, 192 + NQ * r:192 + NQ * r + NQ], s12[:, a:a + P], NQ)
                for br in range(2):
                    m = tr(bank[0][0:TS, 240 + NQ * br:240 + NQ * br + NQ], pz[:, br, b, :], NQ)
                m.then_inc(S("pt_mm"), 1)

            def turn_out(b):
                pe.wait_ge(S("o_s"), b + 1)
                for j in range(2):
                    m = tr(bank[7][:, 256 + 24 * b + NQ * j:256 + 24 * b + NQ * j + NQ], o12[:, P * j:P * j + P], NQ)
                m.then_inc(S("ot_mm"), 1)

            def vals(b):
                pe.wait_ge(S("pt_ev"), b + 1)
                p_, o = pTs[:, b % 2, :], bank[7][0:NQ, 0:256]
                for l in range(CST):
                    mm(o, p_[:, NQ * l:NQ * l + NQ], past_row(b, l)[:, 256:512], l == 0, False)
                for r in range(4):
                    mm(o, p_[:, 192 + NQ * r:192 + NQ * r + NQ], winb[b % 2][:, r, 256:512], False, False)
                for br in range(2):
                    m = mm(o, p_[0:TS, 240 + NQ * br:240 + NQ * br + NQ], kvS[:, 3 + 2 * br, :], False, br == 1)
                m.then_inc(S("pv_mm"), 1)

            pe.wait_ge(*done("oc_ev"))
            pe.wait_ge(*done("pz0"))
            turn(0)
            keys(0)
            new_keys(0)
            for b in range(TS):
                if b + 1 < TS:
                    turn(10 * b + 10)
                    keys(b + 1)
                    new_keys(b + 1)
                turn_weights_s(b)
                if b:
                    turn_out(b - 1)
                vals(b)
            turn_out(TS - 1)

            pe.wait_ge(*done("mixT"))
            for m_ in range(KT):
                if m_ % 2 == 0:
                    w = got(f"wob{m_ // 2}")
                if m_ >= 2:
                    pe.wait_ge(*done("wob_ev", m_ - 1))
                c0 = (m_ % 2) * P
                for j in range(KT):
                    rhs = mixT[:, j, :] if j < 6 else mixm[:, j - 6, :]
                    m = mm(bank[m_ % 2][:, 0:NT], w[:, j, c0:c0 + P], rhs, j == 0, j == KT - 1)
                m.then_inc(S("wob_mm"), 1)
            norm(4, NT)

            pe.wait_ge(S("ld_wr"), 16)
            pe.wait_ge(S("nrm_out"), 5)
            for i in range(3):
                a, z = P * i, min(P * i + P, NT)
                for k in range(KT):
                    m = mm(bank[2][0:z - a, NE * i:NE * i + NE], uT[:, k, a:z], wr[:, k, :], k == 0, k == KT - 1)
            m.then_inc(S("rt"), 1)
            pe.wait_ge(*done("cb"))
            for i in range(3):
                a, z = P * i, min(P * i + P, NT)
                m = tr(bank[3][0:NE, a:z], lg[0:z - a, i, 2, :], z - a)
            m.then_inc(S("cbt"), 1)
            pe.wait_ge(*done("cbt_ev"))
            for e in range(NE):
                if e >= 2:
                    pe.wait_ge(*done("cbb_ev", e - 1))
                mm(bank[e % 2][:, 0:NT], sel8[0:NE, e, :], combT).then_inc(S("cbb"), 1)
            pe.wait_ge(*done("cbb_ev", NE))

            pe.wait_ge(*done("u_split1"))
            with pe.Fori(0, NE) as e:
                for j in range(EFF // P):
                    pe.wait_ge(S("m_sp"), e * ITEMS + (j + 1))
                    if j >= 2:
                        pe.wait_ge(S("m_h"), e * (EFF // P) + j)
                    gate_up(mm, ("m_mm", 1), j, ring_r[:, ring_at.expert[j // 2][0], :].rearrange("p (k c) -> p k c", c=256))
                pe.wait_ge(S("m_h"), e * (EFF // P) + EFF // P + 1)
                for m_ in range(KT):
                    pe.wait_ge(S("m_sp"), e * ITEMS + (EFF // P + m_ + 1))
                    if m_ < 4:
                        pe.wait_ge(S("m_y"), e * KT + 1)
                    else:
                        pe.wait_ge(S("m_y"), e * KT + (m_ - 2))
                    low = ring_r[:, ring_at.expert[GU + m_ // 2][0], 0:EFF // P * 256].rearrange("p (k c) -> p k c", c=256)
                    c0 = (m_ % 2) * P
                    m = split_mm(mm, bank[4 + m_ % 4][:, 0:NT], EFF // P,
                                 lambda k: (whi[:, m_ % 2, k, :], low[:, k, c0:c0 + P]),
                                 lambda k: (hfe[:, 0, k, :], hfe[:, 1, k, :]))
                    m.then_inc(S("m_mm"), 1)

            norm(5, NT)
            pe.wait_ge(S("nrm_out"), 6)
            for n in range(2 * KT + 2):
                i, k = (n // 8, n % 8) if n < 16 else (2, n - 16)
                if n >= 4:
                    pe.wait_ge(*done("y_ev", n - 3))
                if i < 2:
                    m = tr(bank[n % 4][:, 0:P], uT[:, k, P * i:P * i + P], P)
                else:
                    for q in range(4):
                        m = tr(bank[n % 4][0:TS, P * q:P * q + P], uT[:, 4 * k + q, TP:NT], P)
                m.then_inc(S("y_mm"), 1)

        def spread(kd, r, ns):
            row, odd = r // 2, r % 2
            return (xt[HD * row:HD * row + HD, kd, 0:NKV * ns].rearrange("p (j o n) -> p j o n", j=2, o=2)[:, :, odd, :],
                    bank[kd][HD * odd:HD * odd + HD, 2 * ns * row:2 * ns * row + 2 * ns].rearrange("p (j n) -> p j n", j=2))

        def compress_pe(pe, mm, tr, c):
            ns = TP // CST if c == 0 else NSEG
            nv, W = ns - 1, NKV * ns

            def turn(i, kd):
                half = i // 4
                if kd == 0 and i % 4 == 0:
                    pe.wait_ge(S(f"ld_c{half}"), 16 if c == 0 else 16 + 128 * c)
                n = 16 * c + 2 * i + kd
                if n >= 2:
                    for part in range(2):
                        pe.wait_ge(S(f"xe{part}"), n - 1)
                for r in range(2):
                    for j in range(2):
                        a = 256 * kd + P * j
                        m = tr(bank[kd][:, ns * (2 * r + j):ns * (2 * r + j) + ns],
                               gat[0:ns, half, 2 * (i % 4) + r, a:a + P], ns)
                m.then_inc(S("ct"), 1)

            def mul(i, kd):
                if i == 0 and c >= 2:
                    pe.wait_ge(S("hs"), 2 * c - 2)
                for part in range(2):
                    pe.wait_ge(S(f"xe{part}"), 16 * c + 2 * i + kd + 1)
                pair = w1[:, kd, i, :, :].rearrange("p a e -> p (a e)")
                mm(bank[acc(c) + kd][:, 0:W], pair, xt[:, kd, 0:W], i == 0, i == 7).then_inc(S("cm"), 1)

            steps = [(i, kd) for i in range(8) for kd in range(2)]
            turn(*steps[0])
            for n, s in enumerate(steps):
                if n + 1 < len(steps):
                    turn(*steps[n + 1])
                mul(*s)
                if c >= 2 and n == 5:
                    compress_out(pe, mm, c - 1)
                if c >= 2 and n == 9:
                    compress_scores(pe, mm, c - 1)

        def acc(c):
            return 2 + 2 * (c % 2)

        def compress_out(pe, mm, c):
            nv = (TP // CST if c == 0 else NSEG) - 1
            pe.wait_ge(S("ge"), c + 1)
            if c:
                pe.wait_ge(S("kve"), c)
            if c >= 2:
                pe.wait_ge(S("cse"), c - 1)
            mm(bank[6][0:HD, 0:NKV * nv], w2[:, 0, :], hs[:, 0, 0:NKV * nv])
            for g in range(NKV):
                m = mm(bank[7][0:nv, HD * g:HD * g + HD], hs[:, 1, nv * g:nv * g + nv], w2[:, 1, :])
            m.then_inc(S("kv2"), 1)

        def compress_scores(pe, mm, c):
            b = c - 1
            pe.wait_ge(S("kve"), c + 1)
            for g in range(NKV):
                m = mm(bank[7][0:NQ, 256:256 + NCMP], q12[:, b, g, :],
                       kc[:, c % 2, NCMP * g:NCMP * g + NCMP], g == 0, g == NKV - 1)
            m.then_inc(S("cs_mm"), 1)

        def compress_dve(dve, link, V, c):
            ns = TP // CST if c == 0 else NSEG
            nv, W = ns - 1, NKV * ns
            for n in range(16):
                dve.wait_ge(S("ct"), 16 * c + n + 1)
                if c or n >= 2:
                    dve.wait_ge(S("cm"), 16 * c + n - 1)
                for r in (1, 3):
                    link(V.tensor_copy(*spread(n % 2, r, ns)), "xe1", r == 3)
                if c >= 2 and n == 7:
                    compress_out_dve(dve, link, V, c - 1)
                if c >= 2 and n == 11:
                    compress_scores_dve(dve, link, V, c - 1)
            for kd in range(2):
                dve.wait_ge(S("hb"), 2 * c + kd + 1)
                if c:
                    dve.wait_ge(S("kv2"), c)
                o = hs[:, kd, 0:NKV * nv].rearrange("p (g n) -> p g n", g=NKV)
                link(V.tensor_tensor(o, bank[acc(c) + kd][0:HD, 0:W].rearrange("p (g n) -> p g n", g=NKV)[:, :, 0:nv],
                                     hb[:, kd, 0:W].rearrange("p (g n) -> p g n", g=NKV)[:, :, 1:ns], ALU.add), "hs")

        def compress_out_dve(dve, link, V, c):
            nv = (TP // CST if c == 0 else NSEG) - 1
            dve.wait_ge(S("kv2"), c + 1)
            if c == 0:
                k4 = bank[6][0:HD, 0:NKV * nv].rearrange("p (g n) -> p g n", g=NKV)
                link(V.tensor_copy(kcp2[0:HD, :, 0:nv], k4))
                link(V.tensor_copy(kcp2[HD:P, :, 0:nv], k4))
                link(V.tensor_copy(vcp[0:nv, :, :].rearrange("p g d -> p (g d)"), bank[7][0:nv, 0:256]), "kve")
            else:
                if c >= 3:
                    dve.wait_ge(S("cs_mm"), c - 2)
                link(V.tensor_copy(kc[:, c % 2, 0:NKV * nv], bank[6][0:HD, 0:NKV * nv]), signal=False)
                link(V.tensor_copy(vcmp[0:nv, c - 1, :], bank[7][0:nv, 0:256]), "kve")

        def compress_scores_dve(dve, link, V, c):
            dve.wait_ge(S("cs_mm"), c)
            link(V.scalar_tensor_tensor(pc[:, c - 1, 0:NCMP], d12b[:, 0:NCMP], nsl[0:NQ, :],
                                        bank[7][0:NQ, 256:256 + NCMP], ALU.mult, ALU.add), "cse")

        def compress_act(act, link, f, c):
            ns = TP // CST if c == 0 else NSEG
            W = NKV * ns
            for n in range(16):
                act.wait_ge(S("ct"), 16 * c + n + 1)
                if c or n >= 2:
                    act.wait_ge(S("cm"), 16 * c + n - 1)
                for r in (0, 2):
                    link(f(*spread(n % 2, r, ns), ACT.Copy), "xe0", r == 2)
                if c >= 2 and n == 3:
                    compress_gelu(act, link, f, c - 1)
            for kd in range(2):
                act.wait_ge(S("cm"), 16 * c + 15 + kd)
                if c:
                    act.wait_ge(S("hs"), 2 * c)
                link(f(hb[:, kd, 0:W], bank[acc(c) + kd][HD:P, 0:W], ACT.Copy), "hb")

        def compress_gelu(act, link, f, c):
            nv = (TP // CST if c == 0 else NSEG) - 1
            for kd in range(2):
                act.wait_ge(S("hs"), 2 * c + kd + 1)
                o = hs[:, kd, 0:NKV * nv]
                link(f(o, o, ACT.Gelu_apprx_tanh, bias=hconst[:, kd:kd + 1]), "ge" if kd else None)

        def layer_b_dve(dve, link, V, norm):
            dve.wait_ge(S("ma_o"), 8)
            link(V.tensor_tensor(mem_u_b, memT[:, :, :], bc(gain[:, MEM1 * KT:MEM1 * KT + KT], 2, NMEM), ALU.mult), "mem_u")
            norm(3, xT[:, :, :], NT, uT[:, :, :], MIX1)
            mem_rows_dve(dve, link, V, 1)
            for t in range(6):
                dve.wait_ge(*done("bq_mm", t + 1))
                link(V.tensor_scalar(qT[:, t, :], bank[t % 2][:, 0:NT], HD ** -0.5, None, ALU.mult), "bq_ev")
            mem_turn_dve(dve, link, V, 1)
            for n in range(9):
                c, i = n // 3, n % 3
                dve.wait_ge(*done("bkv_mm", n + 1))
                dst = kvP[:, i, 2 * c:2 * c + 2, :] if i < 2 else kvS[:, 2 * c:2 * c + 2, :]
                src = bank[2 + i][0:(P if i < 2 else TS), :].rearrange("p (a d) -> p a d", a=2)
                link(V.tensor_copy(dst, src), "bkv_ev")
            dve.wait_ge(*done("bg_mm", 1))
            dve.wait_ge(S("ld_gbb"), 32)
            for i in range(2):
                link(V.tensor_tensor(gp[:, i, :], bank[2 + i][:, 0:36], gbp, ALU.add))
            link(V.tensor_tensor(g12, bank[4][0:NQ, 0:3 * TS].rearrange("p (c b) -> p c b", c=3), bc(gb12, 2, TS), ALU.add), "bg_ev")
            dve.wait_ge(*done("bg_mm", 3))
            link(V.tensor_scalar(xq[:, 0, :], bank[5][:, 0:NT], HD ** -0.5, None, ALU.mult))
            link(V.tensor_scalar(xq[:, 1, :], bank[6][:, 0:NT], HD ** -0.5, None, ALU.mult))
            for n in range(8):
                dve.wait_ge(*done("kd_mm", n + 1))
                link(V.tensor_copy(kdup[0:HD, n // 4, n % 4, :], bank[n % 2][0:HD, 0:TP]), signal=False)
                link(V.tensor_copy(kdup[HD:P, n // 4, n % 4, :], bank[n % 2][0:HD, 0:TP]), "kd_ev")
            dve.wait_ge(*done("kn_mm", 1))
            link(V.tensor_copy(knT.rearrange("p a g b -> p (a g b)"), bank[2][0:HD, 0:64]), "kn_ev")
            dve.wait_ge(*done("kn_mm", 2))
            link(V.tensor_copy(pec.rearrange("p a b -> p (a b)"), bank[3][:, 0:32]), "kn_ev")
            dve.wait_ge(*done("kn_mm", 3))
            link(V.tensor_copy(hconst, bank[4][0:HD, 0:2]), "kn_ev")
            link(V.memset(q12, 0.0))
            link(V.memset(qblk, 0.0))
            for h in range(NQ):
                g = h // GRP
                src = qT[64 * (h % 2):64 * (h % 2) + 64, h // 2, TP:NT]
                link(V.tensor_copy(q12[:, :, g, h], src))
                link(V.tensor_copy(qblk[64 * (g % 2):64 * (g % 2) + 64, :, g // 2, h], src), "q12" if h == NQ - 1 else None)
            dve.wait_ge(S("ld_pt"), 128)
            link(V.tensor_scalar(idxb, pages, 256.0, C("seg"), ALU.mult, ALU.add), "idx")
            mem_attend_dve(dve, link, V, 1)
            compress_dve(dve, link, V, 0)
            compress_out_dve(dve, link, V, 0)

            def score(n):
                h, i = n // 2, n % 2
                nk, b0 = P * (i + 1), 128 + 8 * (n % 3)
                dve.wait_ge(S("p_s"), n + 1)
                if n >= 3:
                    dve.wait_ge(S("p_t"), n - 2)
                link(V.scalar_tensor_tensor(sc[:, n % 3, :, 0:nk], bc(dist[:, i, 0:nk], 1, 2), -SLOPES[h],
                                            bank[n % 2][:, :].rearrange("p (a k) -> p a k", a=2)[:, :, 0:nk], ALU.mult, ALU.add), signal=False)
                link(V.scalar_tensor_tensor(scc[:, n % 3, 0:15], distc[:, i, 0:15], -SLOPES[h],
                                            bank[(2, 5)[n % 2]][:, 0:15], ALU.mult, ALU.add), "ps")
                link(V.tensor_reduce(small[:, b0 + 1:b0 + 3], sc[:, n % 3, :, 0:nk], AX.X, ALU.max, negate=True), signal=False)
                link(V.tensor_reduce(small[:, b0:b0 + 1], scc[:, n % 3, 0:15], AX.X, ALU.max, negate=True), "p_mx")

            def weigh(n):
                h, i = n // 2, n % 2
                nk, b0 = P * (i + 1), 128 + 8 * (n % 3)
                dve.wait_ge(S("p_e"), n + 1)
                s3 = small[:, b0 + 3:b0 + 6]
                link(V.tensor_tensor(scc[:, n % 3, 0:15], scc[:, n % 3, 0:15], maskc[:, i, 0:15], ALU.mult))
                link(V.tensor_reduce(small[:, b0 + 3:b0 + 4], scc[:, n % 3, 0:15], AX.X, ALU.add))
                link(V.tensor_scalar(s3, s3, 1e-30, None, ALU.max))
                link(V.reciprocal(s3, s3))
                link(V.tensor_tensor(s3, s3, gp[:, i, h:36:NQ], ALU.mult))
                link(V.tensor_scalar(scc[:, n % 3, 0:15], scc[:, n % 3, 0:15], s3[:, 0:1], None, ALU.mult))
                for br in range(2):
                    s_ = sc[:, n % 3, br, 0:nk]
                    link(V.tensor_scalar(s_, s_, s3[:, 1 + br:2 + br], None, ALU.mult), "p_p" if br else None)

            def out(n):
                h, i = n // 2, n % 2
                dve.wait_ge(S("p_o"), n + 1)
                link(V.tensor_copy(oP[:, i, HD * h:HD * h + HD], bank[6 + n % 2][:, 0:HD]), "p_oe")

            dve.wait_ge(*done("gates", 2))
            score(0)
            score(1)
            for n in range(2 * NQ):
                weigh(n)
                if n + 2 < 2 * NQ:
                    score(n + 2)
                if n:
                    out(n - 1)
            out(2 * NQ - 1)
            for j in range(6):
                dve.wait_ge(*done("om_mm", j + 1))
                link(V.tensor_copy(mixT[:, j, 0:TP], bank[j % 2][:, 0:TP]), "om_ev")

            dve.wait_ge(S("ld_d12"), 32)
            for c in range(1, TS + 1):
                compress_dve(dve, link, V, c)
            compress_out_dve(dve, link, V, TS)
            compress_scores_dve(dve, link, V, TS)
            mx, p_ = small[0:NQ, 160:168], pc[:, :, 0:NCMP]
            link(V.tensor_reduce(mx, p_, AX.X, ALU.max))
            link(V.tensor_tensor(p_, p_, bc(mx, 2, NCMP), ALU.subtract), "pc_d")
            dve.wait_ge(*done("pc_e"))
            link(V.tensor_reduce(mx, p_, AX.X, ALU.add))
            link(V.reciprocal(mx, mx))
            link(V.tensor_tensor(p_, p_, bc(mx, 2, NCMP), ALU.mult), "pc_p")
            dve.wait_ge(*done("im"))
            link(V.tensor_tensor(p_, p_, bc(g12[:, 0, :], 2, NCMP), ALU.mult), "pc_s")
            for i in range(2):
                link(V.tensor_copy(psum4[:, 4 * i:4 * i + 4, 0:NCMP],
                                   bank[i][0:NKV, 0:4 * NCMP].rearrange("p (b n) -> p b n", b=4)))
            link(V.memset(imp, 1e9))
            mid = imp[:, :, 1:31]
            link(V.tensor_reduce(mid, psum4[:, :, 3:123].rearrange("p b (j w) -> p b j w", w=4), AX.X, ALU.add))
            link(V.tensor_tensor(mid, mid, psum4[:, :, 7:127].rearrange("p b (j w) -> p b j w", w=4)[:, :, :, 0], ALU.add), "imp")
            dve.wait_ge(*done("pct"))
            link(V.tensor_copy(pcT[0:NCMP, :, :].rearrange("p b h -> p (b h)"), bank[2][0:NCMP, 0:TS * NQ]), "pct_ev")
            dve.wait_ge(S("ld_imp"), 16)
            other, own = bc(imp32, 1, 33), bc(imp32, 2, 33)
            link(V.tensor_tensor(rank, other, own, ALU.is_gt))
            link(V.tensor_tensor(rank2, other, own, ALU.is_equal))
            link(V.tensor_tensor(rank2, rank2, lower[0:32, :].rearrange("p (a b) -> p a b", a=33), ALU.mult))
            link(V.tensor_tensor(rank, rank, rank2, ALU.add))
            link(V.tensor_reduce(sel32, rank, AX.X, ALU.add))
            link(V.tensor_scalar(sel32, sel32, float(NSEL), -FAR, ALU.is_ge, ALU.mult), "sel")
            dve.wait_ge(*done("oc_mm"))
            link(V.tensor_copy(oc.rearrange("p b j c -> p (b j c)"), bank[3][:, 0:TS * NQ]), "oc_ev")
            link(V.memset(pz, 0.0), "pz0")

            dve.wait_ge(S("ld_sel"), 64)
            for b in range(TS):
                if b:
                    dve.wait_ge(S("pt_mm"), b)
                for c in range(5):
                    dve.wait_ge(S("k_s"), 10 * b + 2 * c + 2)
                    a = 512 * c + (c == 4)
                    d_ = d12s[:, 512 * c:512 * c + 512] if c < 4 else d12b[:, NCMP + 1:NCMP + 513]
                    link(V.scalar_tensor_tensor(s12[:, a:a + 512], d_, nsl[0:NQ, :], bank[2 + c][0:NQ, :], ALU.mult, ALU.add), "s_ev")
                dve.wait_ge(S("k_n"), b + 1)
                link(V.tensor_copy(s12[:, PAST:PAST + 1], bank[1][0:NQ, 0:1]), signal=False)
                link(V.tensor_copy(s12[:, PAST + 513:PAST + 514], bank[1][0:NQ, 1:2]), "s_n")
                v = s12[:, 0:PAST].rearrange("p (l j w) -> p l j w", l=CST, w=4)
                link(V.tensor_tensor(v, v, bc(bc(sel12[:, b, 0:NBLK], 1, CST), 3, 4), ALU.add))
                st = small[0:NQ, 176:184]
                br_ = (s12[:, 0:PAST + 1], s12[:, PAST + 1:PAST + 514])
                for r in range(2):
                    link(V.tensor_reduce(st[:, r:r + 1], br_[r], AX.X, ALU.max, negate=True), "s_mx" if r else None)
                dve.wait_ge(S("s_e"), b + 1)
                link(V.reciprocal(st[:, 2:4], st[:, 2:4]))
                link(V.tensor_tensor(st[:, 2:4], st[:, 2:4], g12[:, 1:3, b], ALU.mult))
                for r in range(2):
                    link(V.tensor_scalar(br_[r], br_[r], st[:, 2 + r:3 + r], None, ALU.mult))
                link(V.tensor_copy(pz[:, 0, b, b:b + 1], s12[:, PAST:PAST + 1]), signal=False)
                link(V.tensor_copy(pz[:, 1, b, b:b + 1], s12[:, PAST + 513:PAST + 514]), "p12")
                dve.wait_ge(S("pt_mm"), b + 1)
                if b >= 2:
                    dve.wait_ge(S("pv_mm"), b - 1)
                link(V.tensor_copy(pTs[:, b % 2, 0:240], bank[0][:, 0:240]), signal=False)
                link(V.tensor_copy(pTs[0:TS, b % 2, 240:264], bank[0][0:TS, 240:264]), "pt_ev")
            dve.wait_ge(S("ot_mm"), TS)
            for j in range(2):
                own = bank[7][:, 256:448].rearrange("p (b j c) -> p b j c", b=TS, j=2)[:, :, j, 6 * j:6 * j + 6]
                link(V.tensor_tensor(oTsb[:, :, j, :], own, oc[:, :, j, :], ALU.add))
            for h in range(NQ):
                g = h // GRP
                link(V.tensor_copy(mixT[64 * (h % 2):64 * (h % 2) + 64, h // 2, TP:NT],
                                   oTsb[64 * (g % 2):64 * (g % 2) + 64, :, g // 2, h - 6 * (g // 2)]), "mixT" if h == NQ - 1 else None)
            for m_ in range(KT):
                dve.wait_ge(*done("wob_mm", m_ + 1))
                link(V.tensor_tensor(xT[:, m_, :], xT[:, m_, :], bank[m_ % 2][:, 0:NT], ALU.add), "wob_ev")
            def piece_e(i, e):
                s_, first = ring_at.expert[i // 2]
                dve.wait_ge(S(f"w_in{s_}"), e * ring_at.per[s_] + first)
                c0, kt = (i % 2) * P, 2 * KT if i < EFF // P else EFF // P
                value, low = (x[:, s_, 0:kt * 256].rearrange("p (k c) -> p k c", c=256)[:, :, c0:c0 + P]
                              for x in (ring, ring_r))
                return value, whi[:, i % 2, 0:kt, :], low

            def first_piece(i):
                split(V, link, "m_sp", *piece_e(i, 0))

            norm(4, xT[:, :, :], NT, uT[:, :, :], FFN1, lambda: first_piece(0))
            link(V.tensor_copy(uh, uT[:, :, :]))
            first_piece(1)

            L_, E_, Cb = lg[:, :, 0, :], lg[:, :, 1, :], lg[:, :, 2, :]
            link(V.memset(lg, 0.0))
            dve.wait_ge(*done("rt"))
            link(V.tensor_copy(L_[:, 0:2, :], bank[2][:, 0:2 * NE].rearrange("p (i e) -> p i e", i=2)))
            link(V.tensor_copy(L_[0:TS, 2, :], bank[2][0:TS, 2 * NE:3 * NE]))
            st = small[:, 192:195]
            link(V.tensor_reduce(st, L_, AX.X, ALU.max))
            link(V.tensor_tensor(E_, L_, bc(st, 2, NE), ALU.subtract), "rt_d")
            other, own = bc(L_, 2, NE), bc(L_, 3, NE)
            low8 = lower[:, :].rearrange("p (a b) -> p a b", a=33)[:, 0:NE, 0:NE]
            link(V.tensor_tensor(rk, other, own, ALU.is_gt))
            link(V.tensor_tensor(rk2, other, own, ALU.is_equal))
            link(V.tensor_tensor(rk2, rk2, bc(low8, 1, 3), ALU.mult))
            link(V.tensor_tensor(rk, rk, rk2, ALU.add))
            link(V.tensor_reduce(l8, rk, AX.X, ALU.add))
            link(V.tensor_scalar(l8, l8, 2.0, None, ALU.is_lt))
            dve.wait_ge(*done("rt_e"))
            link(V.tensor_tensor(E_, E_, l8, ALU.mult))
            link(V.tensor_reduce(st, E_, AX.X, ALU.add))
            link(V.reciprocal(st, st))
            link(V.tensor_tensor(Cb, E_, bc(st, 2, NE), ALU.mult), "cb")
            link(V.tensor_tensor(uT_r[:, :, :], uT[:, :, :], uh, ALU.subtract), "u_split1")
            dve.wait_ge(*done("cbt"))
            link(V.tensor_copy(combT, bank[3][0:NE, 0:NT]), "cbt_ev")
            for e in range(NE):
                dve.wait_ge(*done("cbb", e + 1))
                link(V.tensor_copy(comb[:, e, :], bank[e % 2][:, 0:NT]), "cbb_ev")

            link(V.memset(ytmp[:, 0, 0:1], 0.0), "m_y")
            link(V.memset(ytmp[:, 1, 0:1], 0.0), "m_h")
            per = {"m_dv": ITEMS + 2 * (EFF // P) + KT, "m_sp": ITEMS, "m_h": EFF // P, "m_y": KT}
            before = {"m_dv": 0, "m_sp": 2, "m_h": 1, "m_y": 1}

            def expert(e, more):
                n = dict(before)

                def step(ins, name=None):
                    name = name or "m_dv"
                    n[name] += 1
                    ins.then_inc(S(name), 1)
                    dve.wait_ge(S(name), e * per[name] + n[name])

                def ahead(i):
                    if i + 2 < ITEMS:
                        split(V, step, "m_sp", *piece_e(i + 2, e))
                    elif more:
                        split(V, step, "m_sp", *piece_e(i + 2 - ITEMS, e + 1))

                for j in range(EFF // P):
                    dve.wait_ge(S("m_mm"), e * ITEMS + (j + 1))
                    if j < EFF // P - 1:
                        ahead(j)
                    dve.wait_ge(S("m_si"), e * (EFF // P) + (j + 1))
                    step(V.tensor_tensor(hsum[:, 0, :], silu[:, j % 2, :], bank[2 * (j % 2) + 1][:, 0:NT], ALU.mult))
                    split(V, step, "m_h", hsum[:, 0, :], hfe[:, 0, j, :], hfe[:, 1, j, :])
                ahead(EFF // P - 1)
                for m_ in range(KT):
                    dve.wait_ge(S("m_mm"), e * ITEMS + (EFF // P + m_ + 1))
                    ahead(EFF // P + m_)
                    step(V.tensor_tensor(ytmp[:, 0, :], bank[4 + m_ % 4][:, 0:NT], comb[:, e, :], ALU.mult))
                    step(V.tensor_tensor(xT[:, m_, :], xT[:, m_, :], ytmp[:, 0, :], ALU.add), "m_y")

            with dve.Fori(0, NE - 1) as e:
                expert(e, True)
            expert(NE - 1, False)
            dve.wait_ge(S("m_y"), NE * KT + 1)
            norm(5, xT[:, :, :], NT, uT[:, :, :], FINAL)
            for n in range(2 * KT + 2):
                i, k = (n // 8, n % 8) if n < 16 else (2, n - 16)
                dve.wait_ge(*done("y_mm", n + 1))
                if i < 2:
                    link(V.tensor_copy(ysb[:, i, P * k:P * k + P], bank[n % 4][:, 0:P]), "y_ev")
                else:
                    link(V.tensor_copy(ysb[0:TS, 2, 512 * k:512 * k + 512], bank[n % 4][0:TS, :]), "y_ev")

        def layer_b_act(act, link, f, root):
            root(3, NT)
            act.wait_ge(S("bg_ev"), 1)
            link(f(gp, gp, ACT.Sigmoid), "gates")
            link(f(g12, g12, ACT.Sigmoid), "gates")
            mem_attend_act(act, link, f, 1)
            compress_act(act, link, f, 0)
            compress_gelu(act, link, f, 0)

            def expo(n):
                i = n % 2
                nk, b0 = P * (i + 1), 128 + 8 * (n % 3)
                act.wait_ge(S("p_mx"), n + 1)
                link(f(scc[:, n % 3, 0:15], scc[:, n % 3, 0:15], ACT.Exp, bias=small[:, b0:b0 + 1],
                       accum_out=small[:, b0 + 3:b0 + 4]))
                for br in range(2):
                    s_ = sc[:, n % 3, br, 0:nk]
                    link(f(s_, s_, ACT.Exp, bias=small[:, b0 + 1 + br:b0 + 2 + br], accum_out=small[:, b0 + 4 + br:b0 + 5 + br]),
                         "p_e" if br else None)

            def turned(n):
                nk = P * (n % 2 + 1)
                act.wait_ge(S("p_t"), n + 1)
                if n >= 2:
                    act.wait_ge(S("p_o"), n - 1)
                link(f(pT[:, n % 2, :, :].rearrange("p (a t) n -> p a (t n)", a=2)[:, :, 0:nk],
                       bank[3 + n % 2][:, :].rearrange("p (a k) -> p a k", a=2)[:, :, 0:nk], ACT.Copy), signal=False)
                link(f(pcpT[0:15, n % 2, :], bank[6 + n % 2][0:15, P:2 * P], ACT.Copy), "p_te")

            expo(0)
            expo(1)
            for n in range(2 * NQ):
                if n + 2 < 2 * NQ:
                    expo(n + 2)
                turned(n)
            for c in range(1, TS + 1):
                compress_act(act, link, f, c)
            compress_gelu(act, link, f, TS)
            act.wait_ge(*done("pc_d"))
            link(f(pc[:, :, 0:NCMP], pc[:, :, 0:NCMP], ACT.Exp), "pc_e")

            def keys(b):
                for n in range(10 * b, 10 * b + 10):
                    act.wait_ge(S("kt_t"), n + 1)
                    if n >= 2:
                        act.wait_ge(S("k_s"), n - 1)
                    link(f(kTb[:, n % 2, :], bank[n % 2][:, :], ACT.Copy), "kt_e")
                    if b and n % 10 == 5:
                        weights(b - 1)

            def weights(b):
                act.wait_ge(S("s_mx"), b + 1)
                st = small[0:NQ, 176:184]
                for r, (a, z) in enumerate(((0, PAST + 1), (PAST + 1, PAST + 514))):
                    link(f(s12[:, a:z], s12[:, a:z], ACT.Exp, bias=st[:, r:r + 1], accum_out=st[:, 2 + r:3 + r]),
                         "s_e" if r else None)

            def out(b):
                act.wait_ge(S("pv_mm"), b + 1)
                if b:
                    act.wait_ge(S("ot_mm"), b)
                link(f(o12, bank[7][0:NQ, 0:256], ACT.Copy), "o_s")

            for b in range(TS):
                if b >= 2:
                    out(b - 2)
                keys(b)
            out(TS - 2)
            weights(TS - 1)
            out(TS - 1)
            root(4, NT)
            act.wait_ge(*done("rt_d"))
            link(f(lg[:, :, 1, :], lg[:, :, 1, :], ACT.Exp), "rt_e")
            with act.Fori(0, NE) as e:
                for j in range(EFF // P):
                    act.wait_ge(S("m_mm"), e * ITEMS + (j + 1))
                    act.wait_ge(S("m_h"), e * (EFF // P) + max(j, 1))
                    f(silu[:, j % 2, :], bank[2 * (j % 2)][:, 0:NT], ACT.Silu).then_inc(S("m_si"), 1)
            root(5, NT)

        def layer_b_pool(pool, load, store):
            pool.wait_ge(S("ff_y"), KT)
            load("ld_gbb", gbp, I["b_gate_b"].broadcast_to((P, 36)))
            load("ld_gbb", gb12, I["b_gate_b"][0].rearrange("(c h) -> h c", c=3), allow_slow_non_contiguous=True)
            for c in range(2):
                for a in range(2):
                    load("ld_w1", w1[:, c, :, a, :], I["w_cmp1"][0, c].rearrange("(a i p) e -> a p i e", a=2, p=P)[a])
            load("ld_w1", perow, I["pe_cmp"][0].rearrange("c (i a) d -> (c i) (a d)", a=2))
            load("ld_w1", w2, I["w_cmp2"][0].rearrange("c e d -> e c d"))
            for s in range(8):
                load("ld_pt", pages[s:P:8, :], I["page_table"].rearrange("b n -> n b"), allow_slow_non_contiguous=True)
            pool.wait_ge(S("mem_u"), 2)
            load("ld_d12", d12s, I["dist12"][:, 0:PAST])
            mem_store(pool, store, 1)
            pool.wait_ge(S("mkv_mm"), 4)
            mem_load(pool, load, 1)
            pool.wait_ge(*done("bkv_ev", 9))
            for i in range(2):
                store(O["rows_p"][0, 0, P * i:P * i + P].rearrange("t k g d -> t (k g d)"),
                      kvP[:, i, 0:4, :].rearrange("p k d -> p (k d)"), "st_rows")
            for i in range(2):
                store(O["win_p"][0, 0, P * i:P * i + P].rearrange("t k g d -> t (k g d)"),
                      kvP[:, i, 4:6, :].rearrange("p k d -> p (k d)"), "st_win")
            store(O["rows_s"][0, :, 0].rearrange("b k g d -> b (k g d)"), kvS[:, 0:4, :].rearrange("p k d -> p (k d)"), "st_win")
            store(O["win_s"][0, :, WBUF - 1].rearrange("b k g d -> b (k g d)"), kvS[:, 4:6, :].rearrange("p k d -> p (k d)"), "st_win")
            pool.wait_ge(S("st_rows"), 32)
            pool.wait_ge(*done("mixm1"))
            segs = O["rows_p"][0, 0].rearrange("(s l) k g d -> s l (k g d)", l=CST)
            for half in range(2):
                load(f"ld_c{half}", gat[0:TP // CST, half, :, :], segs[:, 8 * half:8 * half + 8, 0:512])
            pool.wait_ge(S("st_mem"), 128)
            load("ld_d12", d12b, I["dist12"][:, PAST:PAST + NSEG + WBUF])

            rows = I["cache_nsa"][0].rearrange("a r (u k) g d -> (a r u) (k g d)", u=2)

            def gather(dst, b, l, kinds, name):
                pool.indirect_dma_start(dst, None, rows, bass.IndirectOffsetOnAxis(ap=idxb[:, b:b + 1], axis=0),
                                        element_offset=(2 * l + kinds) * 512).then_inc(S(name), 16)

            def past(b):
                for l in range(CST):
                    gather(past_row(b, l), b, l, 1, f"ld_g{b % 3}")

            pool.wait_ge(*done("idx"))
            pool.wait_ge(*done("bg_mm", 3))
            past(0)
            pool.wait_ge(S("p_oe"), 2 * NQ)
            for c in range(1, TS + 1):
                for half in range(2):
                    pool.wait_ge(S("ct"), 16 * (c - 1) + 8 * half + 8)
                    for l in range(8):
                        gather(gat[:, half, l, :], c - 1, 8 * half + l, 0, f"ld_c{half}")
            def window(b):
                load(f"ld_win{b % 2}", winb[b % 2], I["cache_nsa_win"][0, b].rearrange("(p r) k g d -> p r (k g d)", r=4))

            pool.wait_ge(S("kv2"), TS + 1)
            past(1)
            pool.wait_ge(*done("oc_ev"))
            pool.wait_ge(S("st_win"), 64)
            window(0)
            window(1)
            past(2)
            for b in range(2, TS):
                pool.wait_ge(S("pv_mm"), b - 1)
                window(b)
                if b + 1 < TS:
                    past(b + 1)
            pool.wait_ge(*done("wob_ev", KT))
            load("ld_wr", wr, I["w_router"][0].rearrange("(k p) e -> p k e", p=P))
            for i in range(2):
                pool.wait_ge(*done("y_ev", KT * (i + 1)))
                store(O["y_prompt"][0, P * i:P * i + P], ysb[:, i, :], "st_y")
            pool.wait_ge(*done("y_ev", 2 * KT + 2))
            store(O["y_sample"][:, 0], ysb[0:TS, 2, :], "st_y")

        def moe_load(sp):
            def read(i, e):
                sp.wait_ge(S("m_mm"), e * ITEMS + 2 * (i + 1))

            def load(i, e):
                s, _ = ring_at.expert[i]
                if i < GU:
                    w = I["w_moe_gu"][0, e].rearrange("(k p) c -> p k c", p=P)
                    for u in range(2):
                        a = EFF * u + 256 * i
                        sp.dma_start(ring[:, s, 2048 * u:2048 * u + 2048].rearrange("p (k c) -> p k c", c=256),
                                     w[:, :, a:a + 256]).then_inc(S(f"w_in{s}"), 16)
                else:
                    w = I["w_moe_d"][0, e].rearrange("(k p) c -> p k c", p=P)
                    a = 256 * (i - GU)
                    sp.dma_start(ring[:, s, 0:EFF // P * 256].rearrange("p (k c) -> p k c", c=256),
                                 w[:, :, a:a + 256]).then_inc(S(f"w_in{s}"), 16)

            n = GU + DN
            last = {i: max(j for j in range(n) if j % RING == i) for i in range(RING)}
            assert all((ring_at.expert[i][0] == ring_at.expert[last[i]][0]) for i in range(RING))
            for i in range(RING):
                sem, value = chunks[len(chunks) - RING + i][1]
                sp.wait_ge(*done(sem, value))
                load(i, 0)
            with sp.Fori(0, NE - 1) as e:
                for i in range(RING, n):
                    read(i - RING, e)
                    load(i, e)
                for i in range(RING):
                    read(last[i], e)
                    load(i, e + 1)
            for i in range(RING, n):
                read(i - RING, NE - 1)
                load(i, NE - 1)

        @block.sync
        def _(sp):
            sp.dma_start(consts[:, :], I["consts"]).then_inc(S("ld_const"), 16)
            sp.dma_start(xin, I["x_prompt"][0].rearrange("(i p) d -> p i d", p=P)).then_inc(S("ld_x"), 16)
            sp.dma_start(xsin, I["x_sample"].rearrange("b t d -> (b t) d")).then_inc(S("ld_x"), 16)
            sp.dma_start(min_, I["mem_prompt"][0].rearrange("(i p) d -> p i d", p=P)).then_inc(S("ld_mem"), 16)
            for row, name in ((0, "norm_mix"), (16, "norm_mem"), (32, "norm_ffn")):
                sp.dma_start(grow[row:row + 16, :], I[name].rearrange("a (k p) -> (a k) p", p=P)).then_inc(S("ld_rows"), 16)
            sp.dma_start(grow[48:56, :], I["norm_final"].rearrange("(k p) -> k p", p=P)).then_inc(S("ld_rows"), 16)
            sp.dma_start(cwrow, I["conv_a"][0].rearrange("j (t d) -> (j t) d", d=MD)).then_inc(S("ld_rows"), 16)
            sp.dma_start(hgrow, I["head_norm_a"][0].rearrange("(t d) -> t d", d=MD)).then_inc(S("ld_rows"), 16)

            def load(n):
                name, _, dmas = chunks[n]
                s, _ = ring_at.at[name]
                if n >= RING:
                    sem, value = chunks[n - RING][1]
                    sp.wait_ge(*done(sem, value))
                for off, parts, dims, src in dmas:
                    k = int(np.prod(dims))
                    sp.dma_start(ring[0:parts, s, off:off + k].rearrange("p (k c) -> p k c", k=dims[0]), src)\
                      .then_inc(S(f"w_in{s}"), 16)

            first_late = len(chunks) - 3
            assert first_late % RING == 2
            for n in range(first_late):
                load(n)
            sp.wait_ge(*done("imp"))
            sp.dma_start(scr_imp, imp.rearrange("p b j -> p (b j)")).then_inc(S("st_imp"), 16)
            sp.wait_ge(S("st_imp"), 16)
            sp.dma_start(imp32, scr_imp.rearrange("g (b j) -> (g b) j", b=TS)).then_inc(S("ld_imp"), 16)
            sp.wait_ge(*done("sel"))
            sp.dma_start(scr_sel.rearrange("g (b j) -> (g b) j", b=TS), sel32).then_inc(S("st_sel"), 16)
            sp.wait_ge(S("st_sel"), 16)
            for g in range(NKV):
                sp.dma_start(sel12[GRP * g:GRP * g + GRP, :, :].rearrange("p b j -> p (b j)"),
                             scr_sel[g:g + 1, :].broadcast_to((GRP, TS * 33))).then_inc(S("ld_sel"), 16)
            sp.wait_ge(S("pv_mm"), TS - 1)
            for n in range(first_late, len(chunks)):
                load(n)
            moe_load(sp)

        @block.tensor
        def _(pe):
            def got(name):
                s, loaded = ring_at.at[name]
                pe.wait_ge(S(f"w_in{s}"), loaded)
                return slot_view(name)

            def mm(out, lhsT, rhs, first=True, last=True, **kw_):
                return nc.tensor.matmul(out, lhsT, rhs, start=first, stop=last, **kw_)

            def tr(out, in_, n):
                return nc.tensor.transpose(out, in_, ident[0:n, 0:n])

            def norm(n, width):
                pe.wait_ge(S("nrm_sq"), n + 1)
                for k in range(KT):
                    m = mm(bank[7][:, 0:width], ones, sq[:, k, 0:width], k == 0, k == KT - 1)
                m.then_inc(S("nrm_mm"), 1)

            pe.wait_ge(S("ld_const"), 16)
            pe.wait_ge(S("ld_x"), 32)
            for k in range(KT):
                if k >= 4:
                    pe.wait_ge(*done("set_ev", k - 3))
                cols = slice(k * P, k * P + P)
                b = bank[k % 4]
                tr(b[:, 0:P], xin[:, 0, cols], P)
                tr(b[:, P:2 * P], xin[:, 1, cols], P)
                tr(b[:, TP:NT], xsin[:, cols], TS).then_inc(S("set_mm"), 1)
            pe.wait_ge(S("ld_mem"), 16)
            for k in range(KT):
                pe.wait_ge(*done("set_ev", k + 5))
                b = bank[k % 4]
                cols = slice(k * P, k * P + P)
                tr(b[:, 0:P], min_[:, 0, cols], P)
                tr(b[:, P:2 * P], min_[:, 1, cols], P).then_inc(S("set_mm"), 1)
            pe.wait_ge(S("ld_rows"), 96)
            tr(bank[4][:, 0:56], grow, 56)
            tr(bank[4][0:MD, 64:128], cwrow, 64)
            tr(bank[4][0:MD, 128:136], hgrow, MH).then_inc(S("set_mm"), 1)

            norm(0, NMEM)
            norm(1, NT)
            pe.wait_ge(S("mem_u"), 1)
            w = got("mkv0")
            mem_project(mm, w, 0, 0)
            mem_project(mm, w, 0, 1)
            mem_turn(pe, tr, 0)

            pe.wait_ge(S("nrm_out"), 2)
            w = got("gxa")
            pe.wait_ge(S("mkv_ev"), 3)
            for k in range(KT):
                mm(bank[2][0:MH, 0:TP], w[:, k, 0:MH], uT[:, k, 0:TP], k == 0, k == KT - 1)
            for k in range(KT):
                mm(bank[3][0:MH, 0:TP], w[:, k, MH:2 * MH], uT[:, k, 0:TP], k == 0, k == KT - 1)
            for k in range(KT):
                m = mm(bank[4][0:TS, 0:2 * MH], uT[:, k, TP:NT], w[:, k, 0:2 * MH], k == 0, k == KT - 1)
            m.then_inc(S("g_mm"), 1)
            for j in range(2):
                for k in range(KT):
                    m = mm(bank[5 + j][:, 0:NT], w[:, k, 16 + P * j:16 + P * j + P], uT[:, k, :], k == 0, k == KT - 1)
                m.then_inc(S("g_mm"), 1)

            for t in range(16):
                if t % 4 == 0:
                    w = got(("q0", "q1", "k0", "k1")[t // 4])
                if t >= 2:
                    pe.wait_ge(*done("qk_ev", t - 1))
                c0 = (t % 4) * MD
                for k in range(KT):
                    m = mm(bank[t % 2][0:MD, 0:NT], w[:, k, c0:c0 + MD], uT[:, k, :], k == 0, k == KT - 1)
                m.then_inc(S("qk_mm"), 1)
            pe.wait_ge(S("g_ev"), 1)
            for c in range(2):
                w = got(f"v{c}")
                for i in range(3):
                    n = 3 * c + i
                    if n >= 3:
                        pe.wait_ge(*done("v_ev", n - 2))
                    toks = slice(P * i, min(P * i + P, NT))
                    for k in range(KT):
                        m = mm(bank[2 + i][0:toks.stop - toks.start, 0:384], uT[:, k, toks], w[:, k, :], k == 0, k == KT - 1)
                    m.then_inc(S("v_mm"), 1)
            for t in range(MH):
                if t % 4 == 0:
                    w = got(f"o{t // 4}")
                if t < 2:
                    pe.wait_ge(*done("qk_ev", 15 + t))
                else:
                    pe.wait_ge(*done("o_ev", t - 1))
                c0 = (t % 4) * MD
                for k in range(KT):
                    m = mm(bank[t % 2][0:MD, 0:NT], w[:, k, c0:c0 + MD], uT[:, k, :], k == 0, k == KT - 1)
                m.then_inc(S("o_mm"), 1)
            pe.wait_ge(S("ld_conv"), 16)
            pe.wait_ge(*done("o_ev", 8))
            for t in range(16):
                m = tr(bank[0][0:MD, 24 * t:24 * t + 24], cvh[:, MD * t:MD * t + MD], 24)
            m.then_inc(S("cvh_mm"), 1)
            pe.wait_ge(*done("v_ev", 6))
            for c in range(4):
                if c:
                    pe.wait_ge(*done("cvo_ev", c))
                for t in range(4 * c, 4 * c + 4):
                    tr(bank[2][0:3, MD * (t % 4):MD * (t % 4) + MD], preP[:, t, TP:TP + 3], MD)
                    m = tr(bank[3][0:TS, MD * (t % 4):MD * (t % 4) + MD], preS[:, t, :, CW - 1], MD)
                m.then_inc(S("cvo_mm"), 1)

            pe.wait_ge(S("gate_x"), 2)
            pe.wait_ge(*done("cvo_ev", 4))
            pe.wait_ge(*done("bd0"))
            mm(bank[4][0:MD, 64:128], ones[0:TS, 0:MD], bdg[:, 0, :, :].rearrange("p b c -> p (b c)"))
            for i in range(2):
                tr(bank[4][:, 16 * i:16 * i + MH], ab[:, 4, P * i:P * i + P], MH)
                m = tr(bank[4][:, 16 * i + MH:16 * i + 16], ab[:, 7, P * i:P * i + P], MH)
            m.then_inc(S("bT_mm"), 1)
            pe.wait_ge(*done("qk_done"))
            pe.wait_ge(S("g_ev"), 2)
            s_bank, m_bank = (bank[0], bank[7]), (bank[1], bank[2])

            def scores(h):
                q, k_ = qk[:, h, :], qk[:, MH + h, :]
                if h >= 2:
                    pe.wait_ge(S("hp"), h - 1)
                mm(s_bank[h % 2][:, 0:TP], k_[:, 0:P], q[:, 0:TP])
                mm(s_bank[h % 2][:, TP:384], k_[:, P:TP], q[:, P:TP])
                mm(m_bank[h % 2][:, 0:TP], sel8[0:MH, h, :], ab[:, 5, :])
                mm(m_bank[h % 2][0:MD, TP:2 * TP], sel8[0:MH, h, 0:MD], ab[:, 6, :]).then_inc(S("sc_mm"), 1)
                if h:
                    pe.wait_ge(S("kw_ev"), h)
                tr(bank[5][:, 0:MD], k_[:, 0:P], MD)
                tr(bank[5][:, MD:2 * MD], k_[:, P:TP], MD).then_inc(S("kt_mm"), 1)

            scores(0)
            scores(1)
            for h in range(MH):
                pe.wait_ge(S("sw"), h + 1)
                if h:
                    pe.wait_ge(S("hp"), h)
                s_, v0, v1 = sw[:, h % 2, :], vp[:, 0, h * MD:h * MD + MD], vp[:, 1, h * MD:h * MD + MD]
                mm(bank[3][0:MD, 0:TP], v0, s_[:, 0:TP], True, False)
                mm(bank[3][0:MD, P:TP], v1, s_[:, TP:384], False, True)
                mm(bank[4][0:MD, 0:TP], ones[:, 0:MD], s_[:, 0:TP], True, False)
                mm(bank[4][0:MD, P:TP], ones[:, 0:MD], s_[:, TP:384], False, True).then_inc(S("nd_mm"), 1)
                pe.wait_ge(S("kw_ev"), h + 1)
                if h:
                    pe.wait_ge(S("c_ev"), h)
                mm(bank[6][0:MD, 0:MD], v0, kw[:, h % 2, 0, :], True, False)
                mm(bank[6][0:MD, 0:MD], v1, kw[:, h % 2, 1, :], False, True)
                mm(bank[6][0:1, P:P + MD], ones[:, 0:1], kw[:, h % 2, 0, :], True, False)
                mm(bank[6][0:1, P:P + MD], ones[:, 0:1], kw[:, h % 2, 1, :], False, True).then_inc(S("c_mm"), 1)
                if h + 2 < MH:
                    scores(h + 2)

            pe.wait_ge(S("c_ev"), 8)
            pe.wait_ge(S("hp"), 8)
            for t in range(16):
                m = tr(bank[t // 4][0:TS, (t % 4) * MD:(t % 4) * MD + MD], qk[:, t, TP:NT], MD)
            m.then_inc(S("qks_mm"), 1)
            for n in range(2 * MH):
                h, half = n // 2, n % 2
                pe.wait_ge(S("kd"), h + 1)
                if n >= 2:
                    pe.wait_ge(S("cup"), n - 1)
                    pe.wait_ge(S("cq"), n - 1)
                mm(bank[n % 2][0:MD, 0:384], vs[:, h * MD:h * MD + MD],
                   kdiag[:, h % 2, 4 * half:4 * half + 4, :]).then_inc(S("op_mm"), 1)
                mm(bank[2 + n % 2][0:MD, 0:384], ones[0:TS, 0:MD],
                   qdiag[:, h % 2, 4 * half:4 * half + 4, :]).then_inc(S("qb_mm"), 1)

            pe.wait_ge(*done("bd"))
            mm(bank[4][0:MD, 0:64], ones[0:TS, 0:MD], bdg[:, 1, :, :].rearrange("p b c -> p (b c)")).then_inc(S("gb_mm"), 1)

            pe.wait_ge(*done("hsq"))
            for h in range(MH):
                m = mm(bank[0][0:MH, 0:NT], csel[0:MD, h, :], sq[0:MD, h, :], h == 0, h == MH - 1)
            m.then_inc(S("hn_mm"), 1)
            pe.wait_ge(S("hn_rs"), 1)
            for h in range(MH):
                if h >= 6:
                    pe.wait_ge(S("hn"), h - 5)
                mm(bank[1 + h % 6][0:MD, 0:NT], sel8[0:MH, h, 0:MD], rs8).then_inc(S("hn_bc"), 1)

            pe.wait_ge(S("hn"), 8)
            def out_heads(m_):
                w = got(f"woa{m_ // 2}")[0]
                if m_ >= 2:
                    pe.wait_ge(*done("woa_ev", m_ - 1))
                for h in range(MH):
                    mm(bank[2 + m_ % 2][:, 0:NT], w[:, h, m_ % 2 * P:m_ % 2 * P + P], hT[:, h, :], h == 0, False)

            def out_first():
                pe.wait_ge(S("ma_pt"), 8)
                out_heads(0)
                out_heads(1)

            mem_attend(pe, mm, tr, 0, out_first)
            pe.wait_ge(*done("mixm0"))
            for m_ in range(KT):
                if m_ >= 2:
                    out_heads(m_)
                w = got(f"woa{m_ // 2}")[1]
                for j in range(2):
                    m = mm(bank[2 + m_ % 2][:, 0:NT], w[:, j, m_ % 2 * P:m_ % 2 * P + P], mixm[:, j, :], False, j == 1)
                m.then_inc(S("woa_mm"), 1)

            norm(2, NT)
            pe.wait_ge(*done("u_split0"))
            for j in range(DFF // P):
                pe.wait_ge(S("ff_sp"), j + 1)
                if j >= 2:
                    pe.wait_ge(S("ff_h"), j - 1)
                gate_up(mm, ("ff_mm", 1), j, by_gu(f"gu{j // 2}", ring_r))
            pe.wait_ge(S("ff_h"), DFF // P)
            for m_ in range(KT):
                pe.wait_ge(S("ff_sp"), DFF // P + m_ + 1)
                if m_ >= 2:
                    pe.wait_ge(S("ff_y"), m_ - 1)
                low = by_dn(f"dn{m_}", ring_r)
                m = split_mm(mm, bank[4 + m_ % 2][:, 0:NT], DFF // P,
                             lambda k: (whi[:, m_ % 2, k, :], low[:, k, :]), lambda k: (hff[:, 0, k, :], hff[:, 1, k, :]))
                m.then_inc(S("ff_mm"), 1)

            layer_b_pe(pe, mm, tr, got, norm)

        @block.vector
        def _(dve):
            link = chain(dve, "dve")
            V = nc.vector

            def norm(n, src, width, dst, g, between=None):
                link(V.tensor_tensor(sq[:, :, 0:width], src, src, ALU.mult), "nrm_sq")
                if between:
                    between()
                dve.wait_ge(S("nrm_mm"), n + 1)
                link(V.tensor_scalar(rtmp[:, 0:width], bank[7][:, 0:width], 1.0 / D, EPS, ALU.mult, ALU.add))
                link(V.reciprocal(rtmp[:, 0:width], rtmp[:, 0:width]), "nrm_rc")
                dve.wait_ge(S("nrm_rs"), n + 1)
                r = rstd[:, 0:width]
                if g is None:
                    link(V.tensor_tensor(dst, src, bc(r, 1, KT), ALU.mult), "nrm_out")
                    return
                for k in range(KT):
                    ins = V.scalar_tensor_tensor(dst[:, k, :], src[:, k, :], gain[:, g * KT + k:g * KT + k + 1], r,
                                                 ALU.mult, ALU.mult)
                    if k == KT - 1:
                        link(ins, "nrm_out")

            for k in range(KT):
                dve.wait_ge(*done("set_mm", k + 1))
                link(V.tensor_copy(xT[:, k, :], bank[k % 4][:, 0:NT]), "set_ev")
            for k in range(KT):
                dve.wait_ge(*done("set_mm", KT + k + 1))
                link(V.tensor_copy(memT[:, k, :], bank[k % 4][:, 0:NMEM]), "set_ev")
            dve.wait_ge(*done("set_mm", 17))
            link(V.tensor_copy(gain[:, :], bank[4][:, 0:56]))
            link(V.tensor_copy(cw, bank[4][0:MD, 64:128]))
            link(V.tensor_copy(hg, bank[4][0:MD, 128:136]), "set_ev")
            norm(0, memT[:, :, :], NMEM, memT[:, :, :], None)
            link(V.tensor_tensor(mem_u_a, memT[:, :, :], bc(gain[:, MEM0 * KT:MEM0 * KT + KT], 2, NMEM), ALU.mult), "mem_u")
            norm(1, xT[:, :, :], NT, uT[:, :, :], MIX0)
            mem_rows_dve(dve, link, V, 0)
            mem_turn_dve(dve, link, V, 0)

            link(V.memset(preP[:, :, 0:3], 0.0), "pre0")
            cflat = csel.rearrange("p a b -> p (a b)")
            link(V.memset(cflat, 0.0))
            link(V.memset(cflat[:, 0:MH * MH:MH + 1], 1.0))
            dve.wait_ge(*done("g_mm", 1))
            dve.wait_ge(S("ld_gb"), 48)
            link(V.tensor_scalar(ab[:, 0, :], bank[2][0:MH, 0:TP], gbias_p[:, 0:1], None, ALU.add))
            link(V.tensor_scalar(ab[:, 1, :], bank[3][0:MH, 0:TP], gbias_p[:, 1:2], None, ALU.add))
            link(V.tensor_tensor(gs.rearrange("p a b -> p (a b)")[:, 0:16], bank[4][0:TS, 0:16], gbias_s, ALU.add), "g_ev")
            dve.wait_ge(*done("g_mm", 3))
            link(V.tensor_scalar(xq[:, 0, :], bank[5][:, 0:NT], HD ** -0.5, None, ALU.mult))
            link(V.tensor_scalar(xq[:, 1, :], bank[6][:, 0:NT], HD ** -0.5, None, ALU.mult), "g_ev")
            ig, fg, tm, lf = (ab[:, i, :] for i in range(4))
            link(V.scalar_tensor_tensor(tm, fg, -1.0, fg, ALU.mult, ALU.max), "lf_abs")
            tms, lfs, a_, mts, ws, gg, emts = (gs[:, i, :] for i in range(2, 9))
            igs, fgs = gs[:, 0, :], gs[:, 1, :]
            link(V.scalar_tensor_tensor(tms, fgs, -1.0, fgs, ALU.mult, ALU.max), "lf_abs")
            dve.wait_ge(S("lf_ln"), 2)
            link(V.scalar_tensor_tensor(lf, fg, 0.0, tm, ALU.min, ALU.subtract))
            F, M, b_, emt, wl, one = (ab[:, i, :] for i in (8, 5, 4, 6, 7, 9))
            link(V.memset(one, 1.0))
            link(V.tensor_tensor_scan(F, one, lf, 0.0, ALU.mult, ALU.add))
            link(V.tensor_tensor(b_, ig, F, ALU.subtract))
            link(V.tensor_tensor_scan(M, one, b_, 0.0, ALU.mult, ALU.max))
            link(V.tensor_tensor(ab[:, 10, :], F, M, ALU.add), "mt_p")
            link(V.tensor_scalar(ab[:, 11, :], b_, M[:, TP - 1:TP], None, ALU.subtract), "mt_p")
            dve.wait_ge(S("ld_st"), 32)
            link(V.scalar_tensor_tensor(lfs, fgs, 0.0, tms, ALU.min, ALU.subtract))
            link(V.tensor_tensor(a_, lfs, m0, ALU.add))
            link(V.tensor_tensor(mts, a_, igs, ALU.max))
            link(V.tensor_tensor(gs[:, 9, :], igs, mts, ALU.subtract))
            link(V.tensor_tensor(gs[:, 10, :], a_, mts, ALU.subtract), "mt_s")
            for t in range(16):
                dve.wait_ge(*done("qk_ev", t + 1))
                o = qk[:, t, 0:TP]
                link(V.tensor_scalar(o, preP[:, t, 0:TP], cw[:, t:t + 1], None, ALU.mult))
                for j in range(1, CW):
                    link(V.scalar_tensor_tensor(o, preP[:, t, j:j + TP], cw[:, 16 * j + t:16 * j + t + 1], o,
                                                ALU.mult, ALU.add), "cv" if j == CW - 1 else None)
            dve.wait_ge(*done("cvh_mm"))
            link(V.tensor_copy(preS[:, :, :, 0:CW - 1],
                               bank[0][0:MD, 0:384].rearrange("p (t b j) -> p t b j", t=16, b=TS)))
            cwv = cw.rearrange("p (j t) -> p j t", j=CW)
            qs = qk[:, :, TP:NT]
            link(V.tensor_tensor(qs, preS[:, :, :, 0], bc(cwv[:, 0, :], 2, TS), ALU.mult))
            for j in range(1, CW):
                link(V.tensor_tensor(ctmp, preS[:, :, :, j], bc(cwv[:, j, :], 2, TS), ALU.mult))
                link(V.tensor_tensor(qs, qs, ctmp, ALU.add), "cv" if j == CW - 1 else None)
            dve.wait_ge(S("gate_x"), 5)
            d8 = ident[0:TS, 0:TS]
            link(V.tensor_tensor(bdg[:, 0, :, :], bc(gg, 1, TS), bc(d8, 2, MH), ALU.mult), "bd0")
            for c in range(4):
                dve.wait_ge(*done("cvo_mm", c + 1))
                link(V.tensor_copy(cv3[:, 384 * c:384 * c + 384], bank[2][0:3, 0:384]), signal=False)
                link(V.tensor_copy(cv8[:, 384 * c:384 * c + 384], bank[3][0:TS, 0:384]), "cvo_ev")
            dve.wait_ge(S("qk_si"), 17)
            link(V.tensor_scalar(qk[:, MH:16, :], qk[:, MH:16, :], MD ** -0.5, None, ALU.mult), "qk_done")

            dve.wait_ge(*done("bT_mm"))
            link(V.tensor_copy(bT.rearrange("p a b -> p (a b)"), bank[4][:, 0:32]))
            link(V.tensor_copy(gb[:, 0, :, :].rearrange("p b c -> p (b c)"), bank[4][0:MD, 64:128]))

            s_bank, m_bank = (bank[0], bank[7]), (bank[1], bank[2])

            def decay(h):
                dve.wait_ge(S("sc_mm"), h + 1)
                w, m_ = wdec[:, h % 2, :], m_bank[h % 2]
                link(V.tensor_scalar(w[:, 0:TP], m_[:, 0:TP], bT[:, 0, h:h + 1], 0.0, ALU.subtract, ALU.max), signal=False)
                link(V.tensor_scalar(w[:, TP:384], m_[:, P:TP], bT[:, 1, h:h + 1], 0.0, ALU.subtract, ALU.max), "wd")

            def weigh(h):
                dve.wait_ge(S("wd_x"), h + 1)
                if h >= 2:
                    dve.wait_ge(S("nd_mm"), h - 1)
                s_ = sw[:, h % 2, :]
                link(V.tensor_tensor(s_, wdec[:, h % 2, :], s_bank[h % 2][:, 0:384], ALU.mult))
                link(V.tensor_tensor(s_[:, 0:P], s_[:, 0:P], tri, ALU.mult), signal=False)
                link(V.tensor_tensor(s_[:, TP:384], s_[:, TP:384], tri, ALU.mult), "sw")
                dve.wait_ge(S("kt_mm"), h + 1)
                if h >= 2:
                    dve.wait_ge(S("c_mm"), h - 1)
                link(V.tensor_scalar(kw[:, h % 2, 0, :], bank[5][:, 0:MD], bT[:, 0, MH + h:MH + h + 1], None, ALU.mult), signal=False)
                link(V.tensor_scalar(kw[:, h % 2, 1, :], bank[5][:, MD:2 * MD], bT[:, 1, MH + h:MH + h + 1], None, ALU.mult), "kw_ev")

            def finish(h):
                dve.wait_ge(S("nd_mm"), h + 1)
                den = bank[4][0:MD, 0:TP]
                link(V.tensor_copy(hden, den))
                link(V.scalar_tensor_tensor(hden, hden, -1.0, hden, ALU.mult, ALU.max))
                link(V.tensor_tensor(hden, hden, m_bank[h % 2][0:MD, TP:2 * TP], ALU.max))
                link(V.reciprocal(hden, hden))
                link(V.tensor_tensor(hT[:, h, 0:TP], bank[3][0:MD, 0:TP], hden, ALU.mult), "hp")
                dve.wait_ge(S("c_mm"), h + 1)
                link(V.tensor_copy(cout[:, h, :], bank[6][0:MD, 0:MD]), signal=False)
                link(V.tensor_copy(nout[:, h, :], bank[6][0:1, P:P + MD]), "c_ev")

            dve.wait_ge(*done("cvo_mm", 4))
            decay(0)
            decay(1)
            weigh(0)
            for h in range(MH):
                if h + 1 < MH:
                    weigh(h + 1)
                if h == 6:
                    dve.wait_ge(S("ld_c"), 16)
                    link(V.tensor_tensor(cs.rearrange("p b h k -> p (b h) k"), cs.rearrange("p b h k -> p (b h) k"),
                                         bc(gb[:, 0, :, :].rearrange("p b h -> p (b h)"), 2, MD), ALU.mult))
                finish(h)
                if h + 2 < MH:
                    decay(h + 2)

            def diag(h):
                if h >= 2:
                    dve.wait_ge(S("op_mm"), 2 * h - 2)
                    dve.wait_ge(S("qb_mm"), 2 * h - 2)
                link(V.tensor_tensor(kdiag[:, h % 2, :, :], bc(kws[:, h, :], 1, TS), bc(d8, 2, MD), ALU.mult))
                link(V.tensor_tensor(qdiag[:, h % 2, :, :], bc(qks[:, h, :], 1, TS), bc(d8, 2, MD), ALU.mult), "kd")
            dve.wait_ge(*done("qks_mm"))
            for i in range(4):
                link(V.tensor_copy(qks[:, 4 * i:4 * i + 4, :], bank[i][0:TS, 0:384].rearrange("p (t d) -> p t d", t=4)),
                     "qks_ev" if i == 3 else None)
            link(V.tensor_tensor(kws, qks[:, MH:16, :], bc(ws, 2, MD), ALU.mult))
            diag(0)
            link(V.tensor_tensor(ns, n0, bc(gg, 2, MD), ALU.mult))
            link(V.tensor_tensor(ns, ns, kws, ALU.add), "n_s")
            link(V.tensor_tensor(n0, ns, qks[:, 0:MH, :], ALU.mult))
            den, rr = gs[:, 11, :], gs[:, 12, :]
            link(V.tensor_reduce(den, n0, AX.X, ALU.add))
            link(V.scalar_tensor_tensor(den, den, -1.0, den, ALU.mult, ALU.max))
            link(V.tensor_tensor(den, den, emts, ALU.max))
            link(V.reciprocal(rr, den))
            link(V.tensor_tensor(bdg[:, 1, :, :], bc(rr, 1, TS), bc(d8, 2, MH), ALU.mult), "bd")

            for h in range(MH):
                if h + 1 < MH:
                    diag(h + 1)
                for half in range(2):
                    n = 2 * h + half
                    c_ = cs[:, 4 * half:4 * half + 4, h, :]
                    dve.wait_ge(S("op_mm"), n + 1)
                    link(V.tensor_tensor(c_, c_, bank[n % 2][0:MD, 0:384].rearrange("p (b k) -> p b k", b=4), ALU.add), "cup")
                    dve.wait_ge(S("qb_mm"), n + 1)
                    link(V.tensor_tensor(ctm, c_, bank[2 + n % 2][0:MD, 0:384].rearrange("p (b k) -> p b k", b=4),
                                         ALU.mult), "cq")
                    link(V.tensor_reduce(num[:, h, 4 * half:4 * half + 4], ctm, AX.X, ALU.add))
            dve.wait_ge(*done("gb_mm"))
            link(V.tensor_copy(gb[:, 1, :, :].rearrange("p b c -> p (b c)"), bank[4][0:MD, 0:64]))
            link(V.tensor_tensor(hT[:, :, TP:NT], num, gb[:, 1, :, :].rearrange("p b h -> p h b"), ALU.mult))

            dve.wait_ge(*done("o_ev", 8))
            link(V.tensor_tensor(hT, hT, og, ALU.mult))
            link(V.tensor_tensor(sq[0:MD, :, :], hT, hT, ALU.mult), "hsq")
            dve.wait_ge(*done("hn_mm"))
            link(V.tensor_scalar(rs8, bank[0][0:MH, 0:NT], 1.0 / MD, EPS, ALU.mult, ALU.add))
            link(V.reciprocal(rs8, rs8), "hn_rc")
            for h in range(MH):
                dve.wait_ge(*done("hn_bc", h + 1))
                link(V.scalar_tensor_tensor(hT[:, h, :], hT[:, h, :], hg[:, h:h + 1], bank[1 + h % 6][0:MD, 0:NT],
                                            ALU.mult, ALU.mult), "hn")

            mem_attend_dve(dve, link, V, 0)

            for m_ in range(KT):
                dve.wait_ge(*done("woa_mm", m_ + 1))
                link(V.tensor_tensor(xT[:, m_, :], xT[:, m_, :], bank[2 + m_ % 2][:, 0:NT], ALU.add), "woa_ev")
            def piece(n):
                name = f"gu{n // 2}" if n < DFF // P else f"dn{n - DFF // P}"
                s_, loaded = ring_at.at[name]
                dve.wait_ge(S(f"w_in{s_}"), loaded)
                if n < DFF // P:
                    c0 = (n % 2) * P
                    split(V, link, "ff_sp", by_gu(name)[:, :, c0:c0 + P], whi[:, n % 2, 0:2 * KT, :],
                          by_gu(name, ring_r)[:, :, c0:c0 + P])
                else:
                    split(V, link, "ff_sp", by_dn(name), whi[:, n % 2, :, :], by_dn(name, ring_r))

            norm(2, xT[:, :, :], NT, uT[:, :, :], FFN0, lambda: piece(0))
            split(V, link, "u_split0", uT[:, :, :], uh, uT_r[:, :, :])
            piece(1)
            for j in range(DFF // P):
                dve.wait_ge(S("ff_mm"), j + 1)
                if j < DFF // P - 1:
                    piece(j + 2)
                dve.wait_ge(S("ff_si"), j + 1)
                link(V.tensor_tensor(hsum[:, 0, :], silu[:, j % 2, :], bank[2 * (j % 2) + 1][:, 0:NT], ALU.mult))
                split(V, link, "ff_h", hsum[:, 0, :], hff[:, 0, j, :], hff[:, 1, j, :])
            piece(DFF // P + 1)
            for m_ in range(KT):
                dve.wait_ge(S("ff_mm"), DFF // P + m_ + 1)
                link(V.tensor_tensor(xT[:, m_, :], xT[:, m_, :], bank[4 + m_ % 2][:, 0:NT], ALU.add), "ff_y")
                if m_ + 2 < KT:
                    piece(DFF // P + m_ + 2)

            layer_b_dve(dve, link, V, norm)

        @block.scalar
        def _(act):
            link = chain(act, "act")

            def f(out, in_, fn, **kw_):
                return nc.scalar.activation(out, in_, fn, **kw_)

            def root(n, width):
                act.wait_ge(S("nrm_rc"), n + 1)
                link(f(rstd[:, 0:width], rtmp[:, 0:width], ACT.Sqrt), "nrm_rs")

            root(0, NMEM)
            root(1, NT)
            act.wait_ge(*done("pre0"))
            def log_forget():
                act.wait_ge(S("lf_abs"), 2)
                tm, tms = ab[:, 2, :], gs[:, 2, :]
                link(f(tm, tm, ACT.Exp, scale=-1.0))
                link(f(tms, tms, ACT.Exp, scale=-1.0))
                link(f(tm, tm, ACT.Ln, bias=1.0), "lf_ln")
                link(f(tms, tms, ACT.Ln, bias=1.0), "lf_ln")

            def gate_weights():
                act.wait_ge(S("mt_p"), 2)
                act.wait_ge(*done("mt_s"))
                link(f(ab[:, 6, :], ab[:, 10, :], ACT.Exp, scale=-1.0), "gate_x")
                link(f(ab[:, 7, :], ab[:, 11, :], ACT.Exp), "gate_x")
                link(f(gs[:, 6, :], gs[:, 9, :], ACT.Exp), "gate_x")
                link(f(gs[:, 7, :], gs[:, 10, :], ACT.Exp), "gate_x")
                link(f(gs[:, 8, :], gs[:, 5, :], ACT.Exp, scale=-1.0), "gate_x")

            for t in range(16):
                if t == 2:
                    log_forget()
                if t == 5:
                    gate_weights()
                act.wait_ge(*done("qk_mm", t + 1))
                link(f(preP[:, t, 3:TP + 3], bank[t % 2][0:MD, 0:TP], ACT.Copy), signal=False)
                link(f(preS[:, t, :, CW - 1], bank[t % 2][0:MD, TP:NT], ACT.Copy), "qk_ev")
            for n in range(6):
                act.wait_ge(*done("v_mm", n + 1))
                c, i = n // 3, n % 3
                dst = vp[:, i, 384 * c:384 * c + 384] if i < 2 else vs[:, 384 * c:384 * c + 384]
                link(f(dst, bank[2 + i][0:(P if i < 2 else TS), 0:384], ACT.Copy), "v_ev")
            for h in range(MH):
                act.wait_ge(*done("o_mm", h + 1))
                link(f(og[:, h, :], bank[h % 2][0:MD, 0:NT], ACT.Sigmoid), "o_ev")
            for t in range(16):
                act.wait_ge(S("cv"), t + 1)
                link(f(qk[:, t, 0:TP], qk[:, t, 0:TP], ACT.Silu), "qk_si")
            act.wait_ge(S("cv"), 17)
            link(f(qk[:, :, TP:NT], qk[:, :, TP:NT], ACT.Silu), "qk_si")
            for h in range(MH):
                act.wait_ge(S("wd"), h + 1)
                w = wdec[:, h % 2, :]
                link(f(w, w, ACT.Exp, scale=-1.0), "wd_x")
            act.wait_ge(S("hn_rc"), 1)
            link(f(rs8, rs8, ACT.Sqrt), "hn_rs")
            mem_attend_act(act, link, f, 0)
            root(2, NT)
            for j in range(DFF // P):
                act.wait_ge(S("ff_mm"), j + 1)
                if j >= 2:
                    act.wait_ge(S("ff_h"), j - 1)
                link(f(silu[:, j % 2, :], bank[2 * (j % 2)][:, 0:NT], ACT.Silu), "ff_si")
            layer_b_act(act, link, f, root)

        @block.gpsimd
        def _(pool):
            def load(name, dst, src, **kw_):
                pool.dma_start(dst, src, **kw_).then_inc(S(name), 16)

            stores, named = [0], {}

            def store(dst, src, name="stored"):
                pool.dma_start(dst, src).then_inc(S(name), 16)
                stores[0] += name == "stored"
                named[name] = named.get(name, 0) + 1

            pool.wait_ge(*done("set_mm", 17))
            load("ld_st", n0, I["state_mlstm_n"][0])
            load("ld_st", m0, I["state_mlstm_m"][0])
            load("ld_conv", cvh, I["state_mlstm_conv"][0].rearrange("b j c -> (b j) c"))
            load("ld_gb", gbias_p[:, 0:1], I["b_gate_a"][0].rearrange("(g h o) -> g h o", g=2, o=1)[0])
            load("ld_gb", gbias_p[:, 1:2], I["b_gate_a"][0].rearrange("(g h o) -> g h o", g=2, o=1)[1])
            load("ld_gb", gbias_s, I["b_gate_a"].broadcast_to((TS, 16)))
            store(O["conv_s"][0, :, 0:CW - 2, :], I["state_mlstm_conv"][0, :, 1:CW - 1, :])
            store(O["win_s"][0, :, 0:WBUF - 1], I["cache_nsa_win"][0, :, 1:WBUF])
            mem_store(pool, store, 0)
            pool.wait_ge(S("mt_p"), 1)
            store(O["m_p"][0, 0].rearrange("(h o) -> h o", o=1), ab[:, 10, TP - 1:TP], "st_a")
            pool.wait_ge(*done("cvo_ev", 4))
            store(O["conv_p"][0, 0], cv3, "st_cv")
            store(O["conv_s"][0, :, CW - 2, :], cv8, "st_cv")
            pool.wait_ge(S("cv"), 17)
            pool.wait_ge(*done("cvh_mm"))
            pool.wait_ge(S("st_cv"), 32)
            load("ld_c", cs.rearrange("p b h k -> p (b h) k"), I["state_mlstm_C"][0].rearrange("b h v k -> v (b h) k"))
            pool.wait_ge(S("c_ev"), 8)
            store(O["C_p"][0, 0].rearrange("h v k -> v h k"), cout, "st_cv")
            store(O["n_p"][0], nout, "st_cv")
            pool.wait_ge(S("c_mm"), 8)
            pool.wait_ge(S("nd_mm"), 8)
            pool.wait_ge(*done("qks_mm"))
            pool.wait_ge(S("st_a"), 16)
            pool.wait_ge(*done("mt_s"))
            store(O["m_s"][0], gs[:, 5, :])
            pool.wait_ge(*done("n_s"))
            store(O["n_s"][0], ns, "st_n")
            pool.wait_ge(S("cup"), 16)
            store(O["C_s"][0].rearrange("b h v k -> v (b h) k"), cs.rearrange("p b h k -> p (b h) k"), "st_c")
            pool.wait_ge(S("st_n"), 16)
            pool.wait_ge(*done("hsq"))
            pool.wait_ge(S("gate_x"), 5)
            mem_load(pool, load, 0)
            layer_b_pool(pool, load, store)
            pool.wait_ge(S("stored"), 16 * stores[0])
            for name in ("st_mem", "st_a", "st_cv", "st_n", "st_c", "st_rows", "st_win", "st_y"):
                pool.wait_ge(S(name), 16 * named[name])


_OUTS = [("y_prompt", (1, TP, D)), ("y_sample", (TS, 1, D)),
         ("mem_k_p", (2, 1, NMEM, XH, HD)), ("mem_v_p", (2, 1, NMEM, XH, HD)),
         ("C_p", (1, 1, MH, MD, MD)), ("n_p", (1, 1, MH, MD)), ("m_p", (1, 1, MH)), ("conv_p", (1, 1, CW - 1, 2 * TOK)),
         ("rows_p", (1, 1, TP, 4, NKV, HD)), ("win_p", (1, 1, TP, 2, NKV, HD)),
         ("C_s", (1, TS, MH, MD, MD)), ("n_s", (1, TS, MH, MD)), ("m_s", (1, TS, MH)), ("conv_s", (1, TS, CW - 1, 2 * TOK)),
         ("rows_s", (1, TS, 1, 4, NKV, HD)), ("win_s", (1, TS, WBUF, 2, NKV, HD))]


def kernel(**inputs):
    import concourse.bacc as _bacc
    from concourse.bass_utils import run_bass_kernel_spmd as _run

    nc = _bacc.Bacc("TRN2", target_bir_lowering=False, num_devices=1)
    arrays, I, O = {}, {}, {}
    laid = dict(inputs)
    laid["consts"], laid["dist12"] = _const_arrays(), _dist12_arrays()
    for name, a in laid.items():
        a = np.ascontiguousarray(a)
        arrays[f"in_{name}"] = a
        I[name] = nc.dram_tensor(f"in_{name}", a.shape, mybir.dt.from_np(a.dtype), kind="ExternalInput").ap()
    for name, shape in _OUTS:
        O[name] = nc.dram_tensor(f"out_{name}", shape, F32, kind="ExternalOutput").ap()
    build(nc, I, O)
    r = _run(nc, [arrays], core_ids=[0])
    return tuple(r.results[0][f"out_{name}"] for name, _ in _OUTS)
```
